# Optimizing a Trainium2 kernel written in Bass

```python
import math
import jax
import jax.numpy as jnp
from jax import lax
import numpy as np

D_MODEL = 1024
BATCH = 1
SEQ = 128
DEPTH = 1
DEC_BATCH = 1
DEC_SEQ = 256
PAST_LEN = 128

GRID_W = 64
D_SSM = 512
SSM_GROUP = 16
N_SSM_GROUPS = D_SSM // SSM_GROUP
SSM_STATE = 64
N_DIR = 2
D_GMLP = D_MODEL - D_SSM
GMLP_HEADS = 4
GMLP_HEAD_DIM = D_GMLP // GMLP_HEADS
CHUNK = 128
D_MIX = D_SSM + D_GMLP
D_IN = D_SSM + 2 * D_GMLP
N_EXPERTS = 16
N_EXPERT_GROUPS = 4
EXPERTS_PER_GROUP = N_EXPERTS // N_EXPERT_GROUPS
TOP_K = 2
D_EXPERT = 512
N_MOD = 6
EPS = 1e-6
DT_MIN = 1e-3
DT_MAX = 1e-1

kernel_name = "hybrid_s5_gmlp_grouped_moe_diffusion_step"

def _rmsnorm(x, w):
    xf = x.astype(jnp.float32)
    y = xf * lax.rsqrt(jnp.mean(xf * xf, axis=-1, keepdims=True) + EPS)
    return (y * w.astype(jnp.float32)).astype(x.dtype)

def _lin_combine(left, right):
    a_l, b_l = left
    a_r, b_r = right
    return a_r * a_l, a_r * b_l + b_r

def _scan_direction(ug, abar, bbar, cm, s0, reverse):
    L = ug.shape[1]
    bu = jnp.einsum('gnh,blgh->blgn', bbar, ug)
    first = L - 1 if reverse else 0
    last = 0 if reverse else L - 1
    bu = bu.at[:, first].add(abar[None] * s0)
    a = jnp.broadcast_to(abar, bu.shape)
    _, s = lax.associative_scan(_lin_combine, (a, bu), axis=1, reverse=reverse)
    y = jnp.real(jnp.einsum('ghn,blgn->blgh', cm, s))
    return y, s[:, last]

def _ssm_mixer(u, s0, a_re, a_im, log_dt, b_re, b_im, c_re, c_im, d, w_glu):
    bsz, L = u.shape[0], u.shape[1]
    f32 = jnp.float32
    A = lax.complex(a_re.astype(f32), a_im.astype(f32))
    dt = jnp.exp(log_dt.astype(f32))[..., None]
    abar = jnp.exp(A * dt)
    bbar = ((abar - 1.0) / A)[..., None] * lax.complex(b_re.astype(f32), b_im.astype(f32))
    cm = lax.complex(c_re.astype(f32), c_im.astype(f32))
    uf = u.astype(f32)
    ug = uf.reshape(bsz, L, N_SSM_GROUPS, SSM_GROUP).astype(jnp.complex64)
    y_f, s_f = _scan_direction(ug, abar[0], bbar[0], cm[0], s0[:, 0], False)
    y_b, s_b = _scan_direction(ug, abar[1], bbar[1], cm[1], s0[:, 1], True)
    y = (y_f + y_b).reshape(bsz, L, D_SSM) + d.astype(f32) * uf
    y = jax.nn.gelu(y)
    y = y * jax.nn.sigmoid(y @ w_glu.astype(f32))
    st = jnp.stack([s_f, s_b], axis=1)
    return y.astype(u.dtype), jnp.real(st), jnp.imag(st)

def _gmlp_mixer(u, v, ln_w, ln_b, w_s, b_s):
    bsz, L = u.shape[0], u.shape[1]
    vf = v.astype(jnp.float32)
    mu = jnp.mean(vf, axis=-1, keepdims=True)
    var = jnp.mean(jnp.square(vf - mu), axis=-1, keepdims=True)
    vn = ((vf - mu) * lax.rsqrt(var + EPS) * ln_w.astype(jnp.float32) + ln_b.astype(jnp.float32)).astype(u.dtype)
    vc = vn.reshape(bsz, L // CHUNK, CHUNK, GMLP_HEADS, GMLP_HEAD_DIM)
    s = jnp.einsum('hpq,bcqhd->bcphd', w_s, vc) + jnp.transpose(b_s)[None, None, :, :, None]
    return u * s.reshape(bsz, L, D_GMLP)

def _moe(h, router_w, router_b, w_gate, w_up, w_down):
    T = h.shape[0]
    scores = jax.nn.sigmoid((h @ router_w).astype(jnp.float32))
    sel = scores + router_b.astype(jnp.float32)
    grouped = sel.reshape(T, N_EXPERT_GROUPS, EXPERTS_PER_GROUP)
    gscore = lax.top_k(grouped, TOP_K)[0].sum(-1)
    g = jnp.argmax(gscore, axis=-1)
    in_group = jnp.take_along_axis(grouped, g[:, None, None], axis=1)[:, 0]
    _, loc = lax.top_k(in_group, TOP_K)
    expert = g[:, None] * EXPERTS_PER_GROUP + loc
    w = jnp.take_along_axis(scores, expert, axis=1)
    w = w / jnp.sum(w, axis=-1, keepdims=True)
    gates = jnp.sum(jax.nn.one_hot(expert, N_EXPERTS, dtype=jnp.float32) * w[..., None], axis=1)
    hg = jnp.einsum('td,edf->tef', h, w_gate)
    hu = jnp.einsum('td,edf->tef', h, w_up)
    act = jax.nn.silu(hg) * hu * gates[..., None].astype(h.dtype)
    return jnp.einsum('tef,efd->td', act, w_down)

def _layer(x, mod, s0, lp, router_w, router_b):
    shift1, scale1, gate1, shift2, scale2, gate2 = [m[:, None, :] for m in jnp.split(mod, N_MOD, axis=-1)]
    h = _rmsnorm(x, lp['norm1_w']) * (1.0 + scale1) + shift1
    z = h @ lp['w_in']
    u_ssm = z[..., :D_SSM]
    zg = jax.nn.gelu(z[..., D_SSM:])
    u_g, v_g = zg[..., :D_GMLP], zg[..., D_GMLP:]
    y_ssm, st_re, st_im = _ssm_mixer(u_ssm, s0, lp['a_re'], lp['a_im'], lp['log_dt'], lp['b_re'], lp['b_im'],
                                     lp['c_re'], lp['c_im'], lp['d'], lp['w_glu'])
    y_g = _gmlp_mixer(u_g, v_g, lp['ln_w'], lp['ln_b'], lp['w_s'], lp['b_s'])
    x = x + gate1 * (jnp.concatenate([y_ssm, y_g], axis=-1) @ lp['w_out'])
    h2 = _rmsnorm(x, lp['norm2_w']) * (1.0 + scale2) + shift2
    moe_out = _moe(h2.reshape(-1, D_MODEL), router_w, router_b, lp['w_gate'], lp['w_up'], lp['w_down'])
    x = x + gate2 * moe_out.reshape(x.shape)
    return x, st_re, st_im

def setup_inputs(seed: int = 0) -> dict:
    key = jax.random.key(seed)
    ks = jax.random.split(key, 32)
    f32 = jnp.float32
    nrm = lambda k, shape, s: jax.random.normal(k, shape, f32) * s
    n_idx = jnp.arange(SSM_STATE, dtype=f32)
    a_im_base = math.pi * n_idx
    return {
        "x_prompt": nrm(ks[0], (BATCH, SEQ, D_MODEL), 1.0),
        "x_sample": nrm(ks[1], (DEC_BATCH, DEC_SEQ, D_MODEL), 1.0),
        "c": nrm(ks[2], (DEC_BATCH, D_MODEL), 1.0),
        "state_ssm_re": nrm(ks[3], (DEC_BATCH, DEPTH, N_DIR, N_SSM_GROUPS, SSM_STATE), 0.1),
        "state_ssm_im": nrm(ks[4], (DEC_BATCH, DEPTH, N_DIR, N_SSM_GROUPS, SSM_STATE), 0.1),
        "c_ctx": nrm(ks[5], (D_MODEL,), 1.0),
        "norm1_w": 1.0 + nrm(ks[6], (DEPTH, D_MODEL), 0.02),
        "norm2_w": 1.0 + nrm(ks[7], (DEPTH, D_MODEL), 0.02),
        "w_mod": nrm(ks[8], (DEPTH, D_MODEL, N_MOD * D_MODEL), 0.5 * D_MODEL ** -0.5),
        "b_mod": nrm(ks[9], (DEPTH, N_MOD * D_MODEL), 0.02),
        "w_in": nrm(ks[10], (DEPTH, D_MODEL, D_IN), D_MODEL ** -0.5),
        "ssm_a_re": -0.5 + nrm(ks[11], (DEPTH, N_DIR, N_SSM_GROUPS, SSM_STATE), 0.01),
        "ssm_a_im": a_im_base + nrm(ks[12], (DEPTH, N_DIR, N_SSM_GROUPS, SSM_STATE), 0.01),
        "ssm_log_dt": jax.random.uniform(ks[13], (DEPTH, N_DIR, N_SSM_GROUPS), f32, math.log(DT_MIN), math.log(DT_MAX)),
        "ssm_b_re": nrm(ks[14], (DEPTH, N_DIR, N_SSM_GROUPS, SSM_STATE, SSM_GROUP), (0.5 / SSM_GROUP) ** 0.5),
        "ssm_b_im": nrm(ks[15], (DEPTH, N_DIR, N_SSM_GROUPS, SSM_STATE, SSM_GROUP), (0.5 / SSM_GROUP) ** 0.5),
        "ssm_c_re": nrm(ks[16], (DEPTH, N_DIR, N_SSM_GROUPS, SSM_GROUP, SSM_STATE), (0.5 / SSM_STATE) ** 0.5),
        "ssm_c_im": nrm(ks[17], (DEPTH, N_DIR, N_SSM_GROUPS, SSM_GROUP, SSM_STATE), (0.5 / SSM_STATE) ** 0.5),
        "ssm_d": nrm(ks[18], (DEPTH, D_SSM), 1.0),
        "w_glu": nrm(ks[19], (DEPTH, D_SSM, D_SSM), D_SSM ** -0.5),
        "gmlp_ln_w": 1.0 + nrm(ks[20], (DEPTH, D_GMLP), 0.02),
        "gmlp_ln_b": nrm(ks[21], (DEPTH, D_GMLP), 0.02),
        "gmlp_w_s": nrm(ks[22], (DEPTH, GMLP_HEADS, CHUNK, CHUNK), CHUNK ** -0.5),
        "gmlp_b_s": 1.0 + nrm(ks[23], (DEPTH, GMLP_HEADS, CHUNK), 0.02),
        "w_out": nrm(ks[24], (DEPTH, D_MIX, D_MODEL), D_MIX ** -0.5),
        "router_w": nrm(ks[25], (D_MODEL, N_EXPERTS), D_MODEL ** -0.5),
        "router_b": nrm(ks[26], (N_EXPERTS,), 0.01),
        "w_gate": nrm(ks[27], (DEPTH, N_EXPERTS, D_MODEL, D_EXPERT), D_MODEL ** -0.5),
        "w_up": nrm(ks[28], (DEPTH, N_EXPERTS, D_MODEL, D_EXPERT), D_MODEL ** -0.5),
        "w_down": nrm(ks[29], (DEPTH, N_EXPERTS, D_EXPERT, D_MODEL), D_EXPERT ** -0.5),
        "final_norm_w": 1.0 + nrm(ks[30], (D_MODEL,), 0.02),
    }

def reference(x_prompt, x_sample, c, state_ssm_re, state_ssm_im, c_ctx, norm1_w, norm2_w, w_mod, b_mod, w_in,
              ssm_a_re, ssm_a_im, ssm_log_dt, ssm_b_re, ssm_b_im, ssm_c_re, ssm_c_im, ssm_d, w_glu,
              gmlp_ln_w, gmlp_ln_b, gmlp_w_s, gmlp_b_s, w_out, router_w, router_b, w_gate, w_up, w_down,
              final_norm_w):
    f32 = jnp.float32
    bsz_p = x_prompt.shape[0]
    zero_state = lax.complex(jnp.zeros((bsz_p, N_DIR, N_SSM_GROUPS, SSM_STATE), f32),
                             jnp.zeros((bsz_p, N_DIR, N_SSM_GROUPS, SSM_STATE), f32))
    xp = x_prompt
    xs = x_sample
    new_re = []
    new_im = []
    for l in range(DEPTH):
        lp = {
            'norm1_w': norm1_w[l], 'norm2_w': norm2_w[l], 'w_in': w_in[l],
            'a_re': ssm_a_re[l], 'a_im': ssm_a_im[l], 'log_dt': ssm_log_dt[l],
            'b_re': ssm_b_re[l], 'b_im': ssm_b_im[l], 'c_re': ssm_c_re[l], 'c_im': ssm_c_im[l],
            'd': ssm_d[l], 'w_glu': w_glu[l], 'ln_w': gmlp_ln_w[l], 'ln_b': gmlp_ln_b[l],
            'w_s': gmlp_w_s[l], 'b_s': gmlp_b_s[l], 'w_out': w_out[l],
            'w_gate': w_gate[l], 'w_up': w_up[l], 'w_down': w_down[l],
        }
        mod_ctx = jax.nn.silu(c_ctx)[None, :] @ w_mod[l] + b_mod[l]
        xp, st_re, st_im = _layer(xp, mod_ctx, zero_state, lp, router_w, router_b)
        new_re.append(st_re)
        new_im.append(st_im)
        mod_lat = jax.nn.silu(c) @ w_mod[l] + b_mod[l]
        s0 = lax.complex(state_ssm_re[:, l].astype(f32), state_ssm_im[:, l].astype(f32))
        xs, _, _ = _layer(xs, mod_lat, s0, lp, router_w, router_b)
    y_prompt = _rmsnorm(xp, final_norm_w)
    y_sample = _rmsnorm(xs, final_norm_w)
    new_state_ssm_re = jnp.stack(new_re, axis=1)
    new_state_ssm_im = jnp.stack(new_im, axis=1)
    return (y_prompt, y_sample, new_state_ssm_re, new_state_ssm_im)


_drawn_inputs = setup_inputs


def setup_inputs(seed=0):
    import zlib

    import numpy as np

    out = dict(_drawn_inputs(seed))
    spreads = {}
    factors = {'state_ssm_re': 8.0,
     'state_ssm_im': 56.832,
     'norm1_w': 2.888,
     'ssm_a_re': 70.496,
     'ssm_c_re': 3.423,
     'ssm_c_im': 2.979,
     'gmlp_ln_w': 25.217,
     'gmlp_ln_b': 24.249,
     'gmlp_b_s': 21.552,
     'final_norm_w': 7.41,
     'norm2_w': 8.0,
     'router_b': 5.271}
    for name, (base, spread) in spreads.items():
        noise = np.random.default_rng([zlib.crc32(name.encode()), seed]).standard_normal(out[name].shape)
        drawn = base * np.exp(spread * noise) if base else spread * noise
        out[name] = jnp.asarray(drawn.astype(out[name].dtype))
    for name, factor in factors.items():
        out[name] = (out[name] * factor).astype(out[name].dtype)
    return out
```

```python
from contextlib import ExitStack

import concourse.bass as bass
from concourse import mybir

F32 = mybir.dt.float32
I32 = mybir.dt.int32
U32 = mybir.dt.uint32
ALU = mybir.AluOpType
ACT = mybir.ActivationFunctionType
AX = mybir.AxisListType

P = 128
D = 1024
KD = D // P
DS = 512
NT = 3
CH = 4
NC = 97
TOK = NC * CH
T0 = [0, 132, 260]
GP = 16
Q = 2 * GP
ROWS = 98
LAT = 33
HEADS = 4
NE = 16
DE = 512
PAIRS = 2 * NT * P
SORTED = PAIRS + P
UNIT = 4096
EPS = 1e-6
PI = 3.141592653589793
BIG = 1.0e30


class Steps:

    def __init__(self, eng, sem):
        self.eng, self.sem, self.n = eng, sem, 0

    def __call__(self, ins):
        ins.then_inc(self.sem, 1)
        self.n += 1
        return self.n

    def settle(self, n=None):
        self.eng.wait_ge(self.sem, self.n if n is None else n)


def build(nc, io):
    ctx = ExitStack()
    with ctx:
        sems = {}

        def S(name):
            if name not in sems:
                sems[name] = ctx.enter_context(nc.semaphore(name))
            return sems[name]

        arena = ctx.enter_context(nc.sbuf_tensor("arena", [P, 9 * UNIT + 16128], F32))
        n_i = ctx.enter_context(nc.sbuf_tensor("n_i", [P, NE], I32))
        off_i = ctx.enter_context(nc.sbuf_tensor("off_i", [P, NE], I32))
        pos_u = ctx.enter_context(nc.sbuf_tensor("pos_u", [P, 8], U32))
        wts = ctx.enter_context(nc.sbuf_tensor("wts", [P, 8], F32))
        psum = ctx.enter_context(nc.psum_tensor("psum", [P, 8, 512], F32))
        bank = [psum[:, i, :] for i in range(8)]

        def view(off, *dims):
            n = 1
            for x in dims:
                n *= x
            v = arena[:, off:off + n]
            if len(dims) == 2:
                v = v.rearrange("p (a b) -> p a b", a=dims[0])
            if len(dims) == 3:
                v = v.rearrange("p (a b c) -> p a b c", a=dims[0], b=dims[1])
            if len(dims) == 4:
                v = v.rearrange("p (a b c d) -> p a b c d", a=dims[0], b=dims[1], c=dims[2])
            return v

        def slot(s):
            return s * UNIT

        F = 9 * UNIT
        X = view(F, NT, D)
        h1T = view(F + 3072, KD, TOK)
        yT = h1T
        U = view(F + 6176, GP, NC)
        L = view(F + 7728, GP, P)
        wglu = view(F + 9776, 4, DS)
        ugT = view(F + 11824, HEADS, TOK)
        vn = view(F + 13376, NT, DS)
        gT = view(F + 13376, 4, TOK)
        xn = view(F + 11824, NT, D)
        BT = view(slot(3), 2, Q, 16)
        Bb = view(slot(3) + 1024, 2, Q, 16)
        Cbd = view(slot(4), 2, Q, 32)
        CA = view(slot(3), 2, Q, P)
        BB = [view(slot(5), Q, P), view(F + 3072, Q, P)]
        rawB = arena[0:64, slot(6):slot(6) + 2048]
        rawC = arena[0:64, F + 7728:F + 7728 + 2048]
        CT = view(F + 9776, 2, Q, 16)
        prod1 = view(F + 10800, Q, 16)
        prod2 = view(F + 11312, Q, 16)
        Bt = view(slot(7), 2, Q, P)
        V = view(slot(5), 2 * ROWS, 32)
        prm = slot(6) + 2176
        lnw = view(prm, DS)
        lnb = view(prm + 512, DS)
        bsr = view(prm + 1024, HEADS, P)
        wsraw = view(slot(0), HEADS, P)
        wsT = view(slot(0) + 512, HEADS, P)
        wout = [view(slot(7), KD, 512), view(slot(8), KD, 512)]
        rows = view(slot(3), 3, 2, D)
        g2rows = view(F + 10240, 2, D)
        h2 = view(slot(5), NT, D)
        h2T = view(slot(6), KD, NT * P)
        hsr = view(slot(7), 6, D)
        hTs = view(F + 3072, KD, SORTED)
        ystage = view(F + 12288, D)
        actT = view(F + 13312, 4, P)
        sg = view(F + 13824, 2, P)
        picked = view(slot(3), NT, 2, D)
        fnw = view(slot(5), D)

        cur = [F + 14928]

        def small(*dims):
            n = 1
            for x in dims:
                n *= x
            v = view(cur[0], *dims)
            cur[0] += n
            assert cur[0] <= F + 16128
            return v

        ident = small(P)
        vecT = small(P)
        sil = small(KD, 2)
        modT = small(48, 2)
        aff1 = small(KD, 2)
        aff2 = small(KD, 2)
        Tre = small(2, 2, GP)
        Tim = small(2, 2, GP)
        dt1, dt2 = small(2, 2, GP), small(2, 2, GP)
        pt1, pt2 = small(2, 2, GP), small(2, 2, GP)
        st = small(32)
        fin = small(2, Q)

        epsc = small(1)
        bnst, bnag = small(6), small(6)

        pc = [prm]

        def temp(*dims):
            n = 1
            for x in dims:
                n *= x
            v = view(pc[0], *dims)
            pc[0] += n
            assert pc[0] <= slot(7)
            return v

        arow = temp(P)
        adrow = temp(P)
        dtr = temp(4)
        acol = temp(4, Q)
        adcol = temp(2, Q)
        tp = [temp(Q) for _ in range(8)]
        sincos_in = view(pc[0] - 7 * Q, 2 * Q)
        sincos_out = view(pc[0] - 5 * Q, 2 * Q)
        pw = temp(5, 2, Q)
        pwB = temp(2, 4, Q)
        pwC = temp(2, 4, Q)
        s0c = small(2, Q)
        statesT = small(P)
        vrows = view(slot(6) + 2048, P)

        hsd = nc.dram_tensor("sorted_tokens", (SORTED, D), F32, kind="Internal").ap()
        ysd = nc.dram_tensor("sorted_outputs", (SORTED, D), F32, kind="Internal").ap()
        w_mod = io["w_mod"][0].rearrange("(k p) n -> p k n", p=P)
        w_in = io["w_in"][0].rearrange("(k p) n -> p k n", p=P)
        w_out = io["w_out"][0].rearrange("(k p) n -> p k n", p=P)
        wg = io["w_gate"][0].rearrange("e (k p) n -> p e k n", p=P)
        wu = io["w_up"][0].rearrange("e (k p) n -> p e k n", p=P)
        wd = io["w_down"][0].rearrange("e (k p) n -> p e k n", p=P)

        def mod_half(m, h):
            return ("mod", 2 * m + h, w_mod[:, :, m * D + h * 512:m * D + h * 512 + 512])

        def in_part(n):
            return ("in", n, w_in[:, :, n * 512:n * 512 + 512])

        units = [mod_half(0, 0), mod_half(0, 1), mod_half(1, 0), mod_half(1, 1), in_part(0),
                 mod_half(2, 0), mod_half(2, 1), in_part(1), mod_half(3, 0), mod_half(3, 1),
                 in_part(2), mod_half(4, 0), mod_half(4, 1), mod_half(5, 0), mod_half(5, 1)]
        RING = 3
        GROUPS = 3
        EROUNDS = NE // GROUPS

        def chunk_dst(t, b):
            return U[32 * t:32 * t + 32, b:GP:4, :]

        def chunk_src(t, b):
            return psum[32 * b:32 * b + 32, 0:4, 0:TOK].rearrange("p c (j t) -> p t c j", t=CH)[:, t, :, :]

        def eunits(g):
            return view(slot(3 * g), KD, 512), view(slot(3 * g + 1), KD, 512), view(slot(3 * g + 2), 4, D)

        router_w = view(slot(6) + 3840, KD, NE)
        rbrow = view(slot(6) + 3968, NE)
        rc = [slot(6) + 3072]

        def rtemp(*dims):
            n = 1
            for x in dims:
                n *= x
            v = view(rc[0], *dims)
            rc[0] += n
            assert rc[0] <= slot(6) + 3840
            return v

        tri = rtemp(P)
        ones = rtemp(P)
        desc = rtemp(NE)
        sig, sel, r1, r2, mk, oh1, oh2 = (rtemp(NT, NE) for _ in range(7))
        g1, g2, g3, g4 = (rtemp(NT, 4) for _ in range(4))
        q1, q2, q3 = rtemp(4), rtemp(4), rtemp(4)
        desc_i = rtemp(NE).bitcast(I32)
        sgm = view(slot(5), 4, TOK)
        xtmp = view(slot(5) + 3072, 512)
        FAM = "abc"

        block = ctx.enter_context(nc.Block())


        @block.sync
        def _(sp):
            for i, (_, _, src) in enumerate(units):
                if i >= RING:
                    sp.wait_ge(S("unit_used"), i - RING + 1)
                sp.dma_start(view(slot(i % RING), KD, 512), src).then_inc(S(f"unit_in{i % RING}"), 16)
                if i == 9:
                    sp.wait_ge(S("params_done"), 1)
                    sp.dma_start(wglu, io["w_glu"][0].rearrange("(k p) n -> p k n", p=P)
                                 ).then_inc(S("wglu_in"), 16)
                    sp.dma_start(lnw, io["gmlp_ln_w"][0].partition_broadcast(P)).then_inc(S("ln_in"), 16)
                    sp.dma_start(lnb, io["gmlp_ln_b"][0].partition_broadcast(P)).then_inc(S("ln_in"), 16)
                    sp.dma_start(bsr, io["gmlp_b_s"][0].partition_broadcast(P)).then_inc(S("ln_in"), 16)
            sp.wait_ge(S("unit_used"), 13)
            sp.dma_start(wsraw, io["gmlp_w_s"][0].rearrange("h p q -> p h q")).then_inc(S("ws_in"), 16)
            sp.wait_ge(S("v_ready"), 16)
            for h in range(2):
                sp.dma_start(wout[h], w_out[:, :, h * 512:h * 512 + 512]).then_inc(S("wout_in"), 16)

            def load(g, e):
                for name, dst, w in zip(("gate", "up", "down"), eunits(g), (wg, wu, wd)):
                    if not isinstance(e, int) or e >= GROUPS:
                        for f in FAM:
                            if name == "gate":
                                sp.wait_ge(S(f"act_done_{f}"), (e - (GROUPS - 1)) * 4)
                            if name == "down":
                                sp.wait_ge(S(f"evac_v_{f}"), (e - (GROUPS - 1)) + 1)
                    src = w[:, e, :, :] if isinstance(e, int) else \
                        w[:, bass.ds(e, 1), :, :].rearrange("p o k n -> p (o k) n")
                    sp.dma_start(dst, src).then_inc(S(f"{name}_in{g}"), 16)

            sp.wait_ge(S("unit_used"), 15)
            sp.wait_ge(S("spatial_ready"), 3)
            load(0, 0)
            for t in range(6):
                if t == 0:
                    sp.wait_ge(S("tok_sent"), 16 * 7)
                sp.dma_start(hsr[:, t, :], hsd[t * P:(t + 1) * P, :]).then_inc(S(f"hs_in{t}"), 16)
            load(1, 1)
            sp.wait_ge(S("hs_ready"), 12)
            sp.wait_ge(S("routed"), 1)
            load(2, 2)
            with sp.Fori(1, EROUNDS) as r:
                for g in range(GROUPS):
                    load(g, r * GROUPS + g)
            load(0, NE - 1)
            for f in FAM:
                sp.wait_ge(S(f"evac_v_{f}"), NE - 2 + 1)
            sp.dma_start(fnw, io["final_norm_w"].partition_broadcast(P)).then_inc(S("fnw_in"), 16)
            sp.wait_ge(S("states_copied"), 1)
            for ri, name in enumerate(("out_re", "out_im")):
                dst = io[name].rearrange("a b d (g t) n -> (a b d g) (t n)", t=2)
                sp.dma_start(dst, statesT[32 * ri:32 * ri + 32, :]).then_inc(S("out_done"), 16)
            for t in range(NT):
                sp.wait_ge(S("final_done"), t + 1)
                dst = io["out_p"][0] if t == 0 else io["out_s"][0, (t - 1) * P:t * P, :]
                sp.dma_start(dst, X[:, t, :]).then_inc(S("out_done"), 16)
            sp.wait_ge(S("out_done"), 16 * 5)

        @block.tensor
        def _(pe):
            mm, tr = nc.tensor.matmul, nc.tensor.transpose
            pe.wait_ge(S("ident_ready"), 1)
            pe.wait_ge(S("vec_in"), 9 * 16)
            tr(bank[7][:, 0:96], vrows[0:96, :], ident[0:96, 0:96]).then_inc(S("vec_ready"), 1)
            pe.wait_ge(S("a_in"), 4 * 16)
            tr(bank[6][:, 0:P], arow[:, :], ident[:, :])
            pe.wait_ge(S("adt_done"), 1)
            tr(bank[6][:, P:P + 64], adrow[0:64, :], ident[0:64, 0:64]).then_inc(S("acol_ready"), 1)
            pe.wait_ge(S("b_in"), 32)
            for h in range(16):
                last = tr(bank[h // 8][:, (h % 8) * 64:(h % 8) * 64 + 64],
                          rawB.rearrange("q (n h) -> q h n", h=16)[:, h, :], ident[0:64, 0:64])
            last.then_inc(S("bt_raw_ready"), 1)
            pe.wait_ge(S("c_in"), 64)
            for h in range(16):
                last = tr(bank[2 + h // 8][:, (h % 8) * 64:(h % 8) * 64 + 64],
                          rawC[:, h * P:(h + 1) * P], ident[0:64, 0:64])
            last.then_inc(S("ct_raw_ready"), 1)

            def unit_wait(i):
                pe.wait_ge(S(f"unit_in{i % RING}"), 16 * (i // RING + 1))
                return view(slot(i % RING), KD, 512)

            def modulation(i, b, base):
                w = unit_wait(i)
                col = 8 * units[i][1] - base
                for kk in range(4):
                    for k in range(KD):
                        last = mm(bank[b][:, col + 2 * kk:col + 2 * kk + 2], w[:, k, kk * P:(kk + 1) * P],
                                  sil[:, k, :], start=(k == 0), stop=(k == KD - 1))
                return last

            pe.wait_ge(S("sil_ready"), 1)
            for i in range(4):
                modulation(i, 5, 0).then_inc(S("unit_used"), 1)

            pe.wait_ge(S("bb_done"), 1)
            pe.wait_ge(S("small_copied"), 2)
            for q in range(Q):
                out = bank[6 + q // 16][:, (q % 16) * 32:(q % 16) * 32 + 32]
                mm(out, BB[0][:, q, :], Cbd[:, 0, q, :], start=True, stop=False)
                last = mm(out, BB[1][:, q, :], Cbd[:, 1, q, :], start=False, stop=True)
            last.then_inc(S("lk_ready"), 1)
            for n in range(16):
                if n >= 4:
                    pe.wait_ge(S("bt_copied"), n - 3)
                for j in range(4):
                    ri, q = divmod(4 * n + j, Q)
                    last = tr(bank[n % 4][:, j * P:(j + 1) * P], BB[ri][:, q, :], ident[:, :])
                last.then_inc(S("bt_ready"), 1)

            pe.wait_ge(S("xn_done"), 3)
            for k in range(KD):
                if k == 1:
                    pe.wait_ge(S("mod_a_copied"), 1)
                if k >= 2:
                    pe.wait_ge(S("h1_done"), k - 1)
                for t in range(NT):
                    last = tr(bank[4 + k % 2][:, T0[t]:T0[t] + P], xn[:, t, k * P:(k + 1) * P], ident[:, :])
                last.then_inc(S("xt_ready"), 1)

            def z_columns(w, c, out):
                for k in range(KD):
                    last = mm(out, w[:, k, c * P:(c + 1) * P], h1T[:, k, :], start=(k == 0), stop=(k == KD - 1))
                return last

            pe.wait_ge(S("h1_done"), KD)
            pe.wait_ge(S("gap_done"), 1)
            w = unit_wait(4)
            for c in range(4):
                pe.wait_ge(S("bt_copied"), 13 + c)
                last = z_columns(w, c, bank[c][:, 0:TOK])
            last.then_inc(S("unit_used"), 1)
            pe.wait_ge(S("lk_copied"), 1)
            modulation(5, 6, 32).then_inc(S("unit_used"), 1)
            modulation(6, 6, 32).then_inc(S("unit_used"), 1)

            pe.wait_ge(S("u_done_a"), 1)
            pe.wait_ge(S("u_done_v"), 1)
            for n in range(16):
                if n >= 4:
                    pe.wait_ge(S("v_copied"), n - 3)
                for ri in range(2):
                    for j in range(2):
                        q = 2 * n + j
                        c = (2 * ri + j) * NC
                        last = mm(bank[n % 4][:, c:c + NC], Bt[:, ri, q, :], U[:, q % GP, :], start=True, stop=True)
                last.then_inc(S("v_ready"), 1)

            w = unit_wait(7)
            for c in range(4):
                if c >= 2:
                    pe.wait_ge(S("ug_done"), c - 1)
                last = z_columns(w, c, bank[4 + c % 2][:, 0:TOK])
                last.then_inc(S("zu_ready") if c < 3 else S("unit_used"), 1)
            modulation(8, 6, 32).then_inc(S("unit_used"), 1)
            modulation(9, 6, 32).then_inc(S("unit_used"), 1)
            w = unit_wait(10)
            for t in range(NT):
                b = (7, 4, 5)[t]
                if t > 0:
                    pe.wait_ge(S("ug_done"), t + 2)
                for k in range(KD):
                    last = mm(bank[b][:, :], h1T[:, k, T0[t]:T0[t] + P], w[:, k, :],
                              start=(k == 0), stop=(k == KD - 1))
                last.then_inc(S("zv_ready") if t < 2 else S("unit_used"), 1)
            for i in range(11, 15):
                modulation(i, 6, 32).then_inc(S("unit_used"), 1)

            pe.wait_ge(S("ws_in"), 16)
            pe.wait_ge(S("vg_done"), 2)
            for h in range(HEADS):
                last = tr(bank[4][:, h * P:(h + 1) * P], wsraw[:, h, :], ident[:, :])
            last.then_inc(S("ws_ready"), 1)
            pe.wait_ge(S("ws_copied"), 1)
            pe.wait_ge(S("mod_b_copied"), 1)
            pe.wait_ge(S("vg_done"), 3)
            for t in range(NT):
                pe.wait_ge(S("vn_done"), t + 1)
                b = (7, 5, 6)[t]
                for h in range(HEADS):
                    last = mm(bank[b][:, h * P:(h + 1) * P], vn[:, t, h * P:(h + 1) * P], wsT[:, h, :],
                              start=True, stop=True)
                last.then_inc(S("spatial_ready"), 1)

            pe.wait_ge(S("lat_states"), 1)
            pe.wait_ge(S("ctx_states"), 1)
            pe.wait_ge(S("v_copied"), 16)
            for b in range(4):
                for c in range(4):
                    gp = 4 * c + b
                    out = bank[b][:, c * NC:(c + 1) * NC]
                    mm(out, L[:, gp, :], U[:, gp, :], start=True, stop=False)
                    for d in range(2):
                        for ri in range(2):
                            last = mm(out, CA[:, ri, d * GP + gp, :],
                                      V[:, d * ROWS + d:d * ROWS + d + NC, ri * GP + gp],
                                      start=False, stop=(d == 1 and ri == 1))
                last.then_inc(S("y_ready"), 1)
            pe.wait_ge(S("fin_done"), 1)
            tr(bank[4][0:64, 0:P], fin.rearrange("p a b -> p (a b)"), ident[:, :]).then_inc(S("states_ready"), 1)

            def spread(n, col):
                for half in range(2):
                    i = 2 * n + half
                    for kk in range(4):
                        last = mm(bank[4 + i % 4][:, kk * P:(kk + 1) * P],
                                  col[:, 4 * half + kk:4 * half + kk + 1].broadcast_to([P, P]), ident[:, :],
                                  start=True, stop=True)
                    last.then_inc(S("spread_ready"), 1)

            pe.wait_ge(S("aff2_done"), 1)
            pe.wait_ge(S("yg_done"), 3)
            pe.wait_ge(S("states_copied"), 1)
            cols = [aff2[:, :, s] for s in range(2)] + [modT[:, 24:32, s] for s in range(2)] \
                + [modT[:, 16:24, s] for s in range(2)]
            for n, col in enumerate(cols):
                if n >= 2:
                    pe.wait_ge(S("spread_copied"), 2 * n - 2)
                spread(n, col)

            pe.wait_ge(S("wglu_in"), 16)
            pe.wait_ge(S("g_done"), 16)
            for c in range(4):
                for k in range(4):
                    last = mm(bank[c][:, 0:TOK], wglu[:, k, c * P:(c + 1) * P], gT[:, k, :],
                              start=(k == 0), stop=(k == 3))
                last.then_inc(S("glu_ready"), 1)
            pe.wait_ge(S("yt_done"), 4)
            pe.wait_ge(S("wout_in"), 32)
            for n in range(6):
                if n == 0:
                    pe.wait_ge(S("spread_copied"), 12)
                if n >= 4:
                    pe.wait_ge(S("x1_done"), n - 3)
                t, h = divmod(n, 2)
                for k in range(KD):
                    last = mm(bank[4 + n % 4][:, :], yT[:, k, T0[t]:T0[t] + P], wout[h][:, k, :],
                              start=(k == 0), stop=(k == KD - 1))
                last.then_inc(S("wo_ready"), 1)
            for n in range(6):
                t, h = divmod(n, 2)
                pe.wait_ge(S("h2_done"), t + 1)
                if n >= 4:
                    pe.wait_ge(S("h2t_copied"), n - 3)
                for kk in range(4):
                    k = 4 * h + kk
                    last = tr(bank[n % 4][:, kk * P:(kk + 1) * P], h2[:, t, k * P:(k + 1) * P], ident[:, :])
                last.then_inc(S("h2t_ready"), 1)
            pe.wait_ge(S("h2t_copied"), 6)
            pe.wait_ge(S("x1_done"), 6)
            pe.wait_ge(S("rw_in"), 32)
            for t in range(NT):
                for k in range(KD):
                    last = mm(bank[4][:, t * NE:(t + 1) * NE], h2T[:, k, t * P:(t + 1) * P], router_w[:, k, :],
                              start=(k == 0), stop=(k == KD - 1))
            last.then_inc(S("logits_ready"), 1)
            for n in range(4):
                col = modT[:, 40:48, n // 2]
                for kk in range(4):
                    last = mm(bank[(6, 7, 2, 3)[n]][:, kk * P:(kk + 1) * P],
                              col[:, 4 * (n % 2) + kk:4 * (n % 2) + kk + 1].broadcast_to([P, P]), ident[:, :],
                              start=True, stop=True)
                last.then_inc(S("g2_ready"), 1)
            pe.wait_ge(S("mk_done"), 1)
            pe.wait_ge(S("tri_done"), 1)
            for t in range(NT):
                mm(bank[5][:, t * NE:(t + 1) * NE], tri[:, :], mk[:, t, :], start=True, stop=(t == 0))
                for s in range(t):
                    mm(bank[5][:, t * NE:(t + 1) * NE], ones[:, :], mk[:, s, :], start=False, stop=(s == t - 1))
            for s in range(NT):
                last = mm(bank[5][:, 48:64], ones[:, :], mk[:, s, :], start=(s == 0), stop=(s == NT - 1))
            last.then_inc(S("ranks_ready"), 1)

            for n in range(12):
                t, h = divmod(n, 2)
                pe.wait_ge(S(f"hs_in{t}"), 16)
                if n == 2:
                    pe.wait_ge(S("g2_copied"), 4)
                if n >= 4:
                    pe.wait_ge(S("hs_copied_a") if n % 2 == 0 else S("hs_copied_v"), (n - 4) // 2 + 1)
                for kk in range(4):
                    k = 4 * h + kk
                    last = tr(bank[n % 4][:, kk * P:(kk + 1) * P], hsr[:, t, k * P:(k + 1) * P], ident[:, :])
                last.then_inc(S("hs_ready"), 1)
            pe.wait_ge(S("hs_copied_a"), 6)
            pe.wait_ge(S("hs_copied_v"), 6)
            pe.wait_ge(S("pad_done"), 1)
            pe.wait_ge(S("int_done"), 1)

            def one_pass(f, e, g, width, start):
                wgt, wup, wdn = eunits(g)
                for j in range(4):
                    for c, w in ((0, wgt), (P, wup)):
                        for k in range(KD):
                            last = mm(bank[j][:, c:c + width], w[:, k, j * P:(j + 1) * P],
                                      hTs[:, k, bass.ds(start, width)], start=(k == 0), stop=(k == KD - 1))
                    last.then_inc(S(f"gu_ready_{f}"), 1)

            def down(f, e, g, width):
                wdn = eunits(g)[2]
                for h in range(2):
                    for j in range(4):
                        last = mm(bank[4 + h][0:width, :], actT[:, j, 0:width], wdn[:, j, h * 512:h * 512 + 512],
                                  start=(j == 0), stop=(j == 3))
                    last.then_inc(S(f"down_ready_{f}"), 1)

            def expert(e, g, round_):
                n = pe.value_load(n_i[0:1, bass.ds(e, 1)], min_val=0, max_val=NT * P)
                start = pe.value_load(off_i[0:1, bass.ds(e, 1)], min_val=0, max_val=PAIRS)
                pe.wait_ge(S(f"gate_in{g}"), 16 * (round_ + 1))
                pe.wait_ge(S(f"up_in{g}"), 16 * (round_ + 1))
                with pe.If(n > 64):
                    one_pass("a", e, g, P, start)
                with pe.Else():
                    one_pass("a", e, g, 64, start)
                pe.wait_ge(S(f"down_in{g}"), 16 * (round_ + 1))
                pe.wait_ge(S("act_done_a"), (e + 1) * 4)
                for x in FAM:
                    pe.wait_ge(S(f"evac_a_{x}"), e + 1)
                    pe.wait_ge(S(f"evac_v_{x}"), e + 1)
                with pe.If(n > 64):
                    down("a", e, g, P)
                with pe.Else():
                    down("a", e, g, 64)
                for i, (f, before) in enumerate((("b", "a"), ("c", "b"))):
                    with pe.If(n > P * (i + 1)):
                        first = pe.value_load(off_i[0:1, bass.ds(e, 1)], min_val=0, max_val=PAIRS - P * (i + 1))
                        one_pass(f, e, g, P, first + P * (i + 1))
                        pe.wait_ge(S(f"act_done_{f}"), (e + 1) * 4)
                        pe.wait_ge(S(f"evac_a_{before}"), e + 2)
                        pe.wait_ge(S(f"evac_v_{before}"), e + 2)
                        down(f, e, g, P)
                    with pe.Else():
                        pe.sem_inc(S(f"gu_ready_{f}"), 4)
                        pe.sem_inc(S(f"down_ready_{f}"), 2)

            with pe.Fori(0, EROUNDS) as r:
                for g in range(GROUPS):
                    expert(r * GROUPS + g, g, r)
            expert(NE - 1, 0, EROUNDS)

        @block.scalar
        def _(act):
            A = nc.scalar.activation
            a = Steps(act, S("act_own"))
            for r0, src in ((0, io["c_ctx"].rearrange("(k p) -> k p", p=P)),
                            (8, io["c"][0].rearrange("(k p) -> k p", p=P)),
                            (16, io["norm1_w"][0].rearrange("(k p) -> k p", p=P)),
                            (24, io["norm2_w"][0].rearrange("(k p) -> k p", p=P)),
                            (32, io["b_mod"][0].rearrange("(k p) -> k p", p=P))):
                act.dma_start(vrows[r0:r0 + src.shape[0], :], src).then_inc(S("vec_in"), 16)
            for t in range(CH):
                act.dma_start(vrows[80:96, 32 * t:32 * t + 32],
                              io["ssm_d"][0].rearrange("(g h) -> g h", h=32)).then_inc(S("vec_in"), 16)
            for i in range(2):
                act.dma_start(dtr[32 * i:32 * i + 32, 0:2],
                              io["ssm_log_dt"][0].rearrange("d (g t) -> (d g) t", t=2)).then_inc(S("dt_in"), 16)
            for i, name in enumerate(("ssm_a_re", "ssm_a_im", "state_ssm_re", "state_ssm_im")):
                src = io[name][0] if i < 2 else io[name][0, 0]
                act.dma_start(arow[32 * i:32 * i + 32, :],
                              src.rearrange("d (g t) n -> (d g) (t n)", t=2)).then_inc(S("a_in"), 16)
            for i, name in enumerate(("ssm_b_re", "ssm_b_im")):
                act.dma_start(rawB[32 * i:32 * i + 32, :],
                              io[name][0].rearrange("d (g t) n h -> (d g) (t n h)", t=2)).then_inc(S("b_in"), 16)
            for i, name in enumerate(("ssm_c_re", "ssm_c_im")):
                for g in range(2):
                    act.dma_start(rawC[32 * i:32 * i + 32, :].rearrange("q (h t n) -> q t h n", h=16, t=2)[:, g],
                                  io[name][0].rearrange("d (g t) h n -> (d g) t h n", t=2)[:, g]
                                  ).then_inc(S("c_in"), 16)
            for t in range(NT):
                src = io["x_prompt"][0] if t == 0 else io["x_sample"][0, (t - 1) * P:t * P, :]
                act.dma_start(X[:, t, :], src).then_inc(S("x_in"), 16)
            act.wait_ge(S("dt_in"), 32)
            A(dtr[0:64, 0:2], dtr[0:64, 0:2], ACT.Exp).then_inc(S("dt_ready"), 1)
            act.wait_ge(S("phase_done"), 1)
            A(tp[5][:, :], adcol[:, 0, :], ACT.Exp).then_inc(S("trig_done"), 1)
            A(sincos_out, sincos_in, ACT.Sin).then_inc(S("trig_done"), 1)
            act.wait_ge(S("small_copied"), 1)
            A(sil.rearrange("p k s -> p s k"), vecT[:, 0:16].rearrange("p (s k) -> p s k", s=2),
              ACT.Silu).then_inc(S("sil_ready"), 1)
            act.wait_ge(S("x_in"), 48)
            for t in range(NT):
                n = a(A(xn[:, t, :], X[:, t, :], ACT.Square, accum_out=st[:, t:t + 1]))
            a.settle()
            A(st[:, 3:6], st[:, 0:3], ACT.Sqrt, bias=epsc[:, 0:1], scale=1.0 / D).then_inc(S("root_done"), 1)
            act.wait_ge(S("rstd_done"), 1)
            for t in range(NT):
                A(xn[:, t, :], X[:, t, :], ACT.Copy, scale=st[:, 6 + t:7 + t]).then_inc(S("xn_done"), 1)
            for n in range(16):
                act.wait_ge(S("bt_ready"), n + 1)
                ri, q = divmod(4 * n, Q)
                A(Bt[:, ri, q:q + 4, :], bank[n % 4][:, :].rearrange("p (a b) -> p a b", a=4),
                  ACT.Copy).then_inc(S("bt_copied"), 1)
            act.wait_ge(S("aff1_done"), 1)
            for k in range(KD):
                act.wait_ge(S("xt_ready"), k + 1)
                b = bank[4 + k % 2]
                A(h1T[:, k, 0:P], b[:, 0:P], ACT.Identity, bias=modT[:, k, 0:1], scale=aff1[:, k, 0:1])
                A(h1T[:, k, T0[1]:TOK], b[:, T0[1]:TOK], ACT.Identity, bias=modT[:, k, 1:2],
                  scale=aff1[:, k, 1:2]).then_inc(S("h1_done"), 1)
            act.wait_ge(S("unit_used"), 5)
            for b in range(2):
                for t in range(CH):
                    last = A(chunk_dst(t, b), chunk_src(t, b), ACT.Copy)
            last.then_inc(S("u_done_a"), 1)
            for c in range(4):
                act.wait_ge(S("zu_ready") if c < 3 else S("unit_used"), c + 1 if c < 3 else 8)
                A(ugT[:, c, :], bank[4 + c % 2][:, 0:TOK], ACT.Gelu_apprx_tanh).then_inc(S("ug_done"), 1)
            for t in range(NT):
                act.wait_ge(S("zv_ready") if t < 2 else S("unit_used"), t + 1 if t < 2 else 11)
                A(vn[:, t, :], bank[(7, 4, 5)[t]][:, :], ACT.Gelu_apprx_tanh).then_inc(S("vg_done"), 1)
            act.wait_ge(S("ln_var"), 1)
            A(st[:, 16:19], st[:, 12:15], ACT.Sqrt, bias=epsc[:, 0:1]).then_inc(S("ln_root"), 1)
            act.wait_ge(S("spatial_ready"), 3)
            for b in range(4):
                act.wait_ge(S("y_ready"), b + 1)
                for t in range(CH):
                    A(gT[32 * b:32 * b + 32, :, :].rearrange("p c (j t) -> p t c j", t=CH)[:, t, :, :],
                      bank[b][32 * t:32 * t + 32, 0:4 * NC].rearrange("p (c j) -> p c j", c=4),
                      ACT.Gelu_apprx_tanh).then_inc(S("g_done"), 1)
            for c in range(4):
                act.wait_ge(S("glu_ready"), c + 1)
                A(sgm[:, c, :], bank[c][:, 0:TOK], ACT.Sigmoid).then_inc(S("sgm_done"), 1)
            for t in range(NT):
                act.wait_ge(S("x1_done"), 2 * t + 2)
                a(A(h2[:, t, :], X[:, t, :], ACT.Square, accum_out=st[:, t:t + 1]))
                a.settle()
                A(st[:, 3 + t:4 + t], st[:, t:t + 1], ACT.Sqrt, bias=epsc[:, 0:1],
                  scale=1.0 / D).then_inc(S("root2_done"), 1)
            for n in range(6):
                act.wait_ge(S("h2t_ready"), n + 1)
                t, h = divmod(n, 2)
                A(h2T[:, 4 * h:4 * h + 4, t * P:(t + 1) * P], bank[n % 4][:, :].rearrange("p (a b) -> p a b", a=4),
                  ACT.Copy).then_inc(S("h2t_copied"), 1)
            act.wait_ge(S("logits_ready"), 1)
            A(r1.rearrange("p a b -> p (a b)"), bank[4][:, 0:NT * NE], ACT.Exp, scale=-1.0).then_inc(S("exp_done"), 1)
            for n in range(0, 12, 2):
                act.wait_ge(S("hs_ready"), n + 1)
                t, h = divmod(n, 2)
                A(hTs[:, 4 * h:4 * h + 4, t * P:(t + 1) * P], bank[n % 4][:, :].rearrange("p (a b) -> p a b", a=4),
                  ACT.Copy).then_inc(S("hs_copied_a"), 1)

            act.wait_ge(S("int_done"), 1)
            act.wait_ge(S("tok_sent"), 16 * 7)
            for f in FAM:
                act.sem_inc(S(f"evac_a_{f}"), 1)
                act.sem_inc(S(f"written_{f}"), 16)

            def one_pass(f, e, i, start):
                for j in range(4):
                    act.wait_ge(S(f"gu_ready_{f}"), e * 4 + j + 1)
                    if j >= 2:
                        act.wait_ge(S(f"act_done_{f}"), e * 4 + j - 1)
                    A(sg[:, j % 2, :], bank[j][:, 0:P], ACT.Silu).then_inc(S(f"silu_done_{f}"), 1)
                act.wait_ge(S(f"down_ready_{f}"), e * 2 + 1)
                if f == "a":
                    for x in FAM:
                        act.wait_ge(S(f"written_{x}"), (e + 1) * 16)
                else:
                    act.wait_ge(S("written_a" if f == "b" else "written_b"), (e + 2) * 16)
                A(ystage[:, 0:512], bank[4][:, :], ACT.Copy).then_inc(S(f"evac_a_{f}"), 1)
                act.wait_ge(S(f"evac_a_{f}"), e + 2)
                act.wait_ge(S(f"evac_v_{f}"), e + 2)
                act.dma_start(ysd[bass.ds(start + P * i, P), :], ystage[:, :]).then_inc(S(f"written_{f}"), 16)

            def expert(e):
                start = act.value_load(off_i[0:1, bass.ds(e, 1)], min_val=0, max_val=PAIRS)
                one_pass("a", e, 0, start)
                for i, f in enumerate("bc", 1):
                    n = act.value_load(n_i[0:1, bass.ds(e, 1)], min_val=0, max_val=NT * P)
                    with act.If(n > P * i):
                        start = act.value_load(off_i[0:1, bass.ds(e, 1)], min_val=0, max_val=PAIRS - P * i)
                        one_pass(f, e, i, start)
                    with act.Else():
                        act.sem_inc(S(f"silu_done_{f}"), 4)
                        act.sem_inc(S(f"evac_a_{f}"), 1)
                        act.sem_inc(S(f"written_{f}"), 16)

            with act.Fori(0, NE) as e:
                expert(e)
            for t in range(NT):
                act.wait_ge(S("x2_done"), t + 1)
                a(A(picked[:, t, 0, :], X[:, t, :], ACT.Square, accum_out=st[:, t:t + 1]))
                a.settle()
                A(st[:, 3 + t:4 + t], st[:, t:t + 1], ACT.Sqrt, bias=epsc[:, 0:1],
                  scale=1.0 / D).then_inc(S("root3_done"), 1)

        @block.vector
        def _(dve):
            V_ = nc.vector
            d = Steps(dve, S("dve_own"))

            def v(ins):
                d(ins)
                d.settle()

            tt, ts, stt, cp = V_.tensor_tensor, V_.tensor_scalar, V_.scalar_tensor_tensor, V_.tensor_copy
            v(V_.memset(epsc[:, :], EPS))
            dve.wait_ge(S("dt_ready"), 1)
            dve.wait_ge(S("a_in"), 64)
            tt(adrow[0:64, :].rearrange("q (t n) -> q t n", t=2), arow[0:64, :].rearrange("q (t n) -> q t n", t=2),
               dtr[0:64, 0:2].unsqueeze(2).broadcast_to([64, 2, 64]), ALU.mult).then_inc(S("adt_done"), 1)
            dve.wait_ge(S("vec_ready"), 1)
            cp(vecT[:, 0:96], bank[7][:, 0:96]).then_inc(S("small_copied"), 1)
            dve.wait_ge(S("acol_ready"), 1)
            d(cp(acol.rearrange("p a b -> p (a b)"), bank[6][:, 0:P]))
            d(cp(s0c.rearrange("p a b -> p (a b)"), bank[6][:, 64:P]))
            v(cp(adcol.rearrange("p a b -> p (a b)"), bank[6][:, P:P + 64]))
            dve.sem_inc(S("small_copied"), 1)
            ar, ai, adi = acol[:, 0, :], acol[:, 1, :], adcol[:, 1, :]
            k, r, rq = tp[0][:, :], tp[1][:, :], tp[2][:, :]
            lim = 3.1415925
            v(ts(k, adi, 1.0 / (2 * PI), 12582912.0, ALU.mult, ALU.add))
            v(ts(k, k, -12582912.0, None, ALU.add))
            v(stt(r, k, -6.28125, adi, ALU.mult, ALU.add))
            v(stt(r, k, -(2 * PI - 6.28125), r, ALU.mult, ALU.add))
            v(ts(rq, r, PI / 2, None, ALU.add))
            v(ts(k, rq, PI, -2 * PI, ALU.is_gt, ALU.mult))
            v(tt(rq, rq, k, ALU.add))
            ts(sincos_in, sincos_in, lim, -lim, ALU.min, ALU.max).then_inc(S("phase_done"), 1)

            dve.wait_ge(S("bt_raw_ready"), 1)
            for i in range(2):
                d(cp(BT.rearrange("p r q h -> p h (r q)")[:, 8 * i:8 * i + 8, :],
                     bank[i][:, :].rearrange("p (h q) -> p h q", h=8)))
            dve.wait_ge(S("ct_raw_ready"), 1)
            for i in range(2):
                d(cp(CT.rearrange("p r q h -> p h (r q)")[:, 8 * i:8 * i + 8, :],
                     bank[2 + i][:, :].rearrange("p (h q) -> p h q", h=8)))
            dve.wait_ge(S("root_done"), 1)
            V_.reciprocal(st[:, 6:9], st[:, 3:6]).then_inc(S("rstd_done"), 1)

            dve.wait_ge(S("trig_done"), 2)
            d(V_.memset(pw[:, 0, 0, :], 1.0))
            d(V_.memset(pw[:, 0, 1, :], 0.0))
            d(tt(pw[:, 1, 0, :], tp[5][:, :], tp[4][:, :], ALU.mult))
            v(tt(pw[:, 1, 1, :], tp[5][:, :], tp[3][:, :], ALU.mult))

            def cmul(o, x, y):
                d(tt(tp[0][:, :], x[:, 0, :], y[:, 0, :], ALU.mult))
                d(tt(tp[1][:, :], x[:, 1, :], y[:, 1, :], ALU.mult))
                d(tt(tp[2][:, :], x[:, 0, :], y[:, 1, :], ALU.mult))
                v(tt(tp[3][:, :], x[:, 1, :], y[:, 0, :], ALU.mult))
                d(tt(o[:, 0, :], tp[0][:, :], tp[1][:, :], ALU.subtract))
                v(tt(o[:, 1, :], tp[2][:, :], tp[3][:, :], ALU.add))

            cmul(pw[:, 2], pw[:, 1], pw[:, 1])
            cmul(pw[:, 3], pw[:, 2], pw[:, 1])
            cmul(pw[:, 4], pw[:, 2], pw[:, 2])
            er1, den, fr, fi, m0, m1 = (x[:, :] for x in tp[:6])
            ei = pw[:, 1, 1, :]
            d(ts(er1, pw[:, 1, 0, :], -1.0, None, ALU.add))
            d(tt(m0, ar, ar, ALU.mult))
            v(tt(m1, ai, ai, ALU.mult))
            v(tt(m0, m0, m1, ALU.add))
            v(V_.reciprocal(den, m0))
            d(tt(m0, er1, ar, ALU.mult))
            v(tt(m1, ei, ai, ALU.mult))
            v(tt(m0, m0, m1, ALU.add))
            v(tt(fr, m0, den, ALU.mult))
            d(tt(m0, ei, ar, ALU.mult))
            v(tt(m1, er1, ai, ALU.mult))
            v(tt(m0, m0, m1, ALU.subtract))
            v(tt(fi, m0, den, ALU.mult))
            for t in range(CH):
                for x, kf, kb in ((pwB, 3 - t, t), (pwC, t + 1, 4 - t)):
                    d(cp(x[:, :, t, 0:GP], pw[:, kf, :, 0:GP]))
                    d(cp(x[:, :, t, GP:Q], pw[:, kb, :, GP:Q]))
            for ri in range(2):
                d(cp(Tre[:, :, ri, :], pw[:, 4, 0, :].rearrange("p (d g) -> p d g", d=2)))
            d(cp(Tim[:, :, 0, :], pw[:, 4, 1, :].rearrange("p (d g) -> p d g", d=2)))
            v(ts(Tim[:, :, 1, :], pw[:, 4, 1, :].rearrange("p (d g) -> p d g", d=2), -1.0, None, ALU.mult))

            def over_h(x, n=16):
                return x.unsqueeze(2).broadcast_to([P, Q, n])

            def halves(o, in0, in1, op):
                for g in range(2):
                    part = slice(64 * g, 64 * g + 64)
                    d(tt(o[part, :, 16 * g:16 * g + 16], in0[part], in1[part], op))

            for o, x, y, op in ((0, 0, 1, ALU.subtract), (1, 1, 0, ALU.add)):
                d(tt(prod1, BT[:, x], over_h(fr), ALU.mult))
                v(tt(prod2, BT[:, y], over_h(fi), ALU.mult))
                v(tt(Bb[:, o], prod1, prod2, op))
            dve.wait_ge(S("zeros_done"), 1)
            for t in range(CH):
                for o, x, y, op in ((0, 0, 1, ALU.subtract), (1, 1, 0, ALU.add)):
                    d(tt(prod1, Bb[:, x], over_h(pwB[:, 0, t, :]), ALU.mult))
                    v(tt(prod2, Bb[:, y], over_h(pwB[:, 1, t, :]), ALU.mult))
                    halves(BB[o][:, :, 32 * t:32 * t + 32], prod1, prod2, op)
                    d.settle()
            for g in range(2):
                part = slice(64 * g, 64 * g + 64)
                d(cp(Cbd[part, 0, :, 16 * g:16 * g + 16], CT[part, 0]))
                v(ts(Cbd[part, 1, :, 16 * g:16 * g + 16], CT[part, 1], -1.0, None, ALU.mult))
            dve.sem_inc(S("bb_done"), 1)

            dve.wait_ge(S("unit_used"), 4)
            v(tt(modT[:, 0:16, :], bank[5][:, 0:32].rearrange("p (a b) -> p a b", b=2),
                 vecT[:, 32:48].unsqueeze(2).broadcast_to([P, 16, 2]), ALU.add))
            dve.sem_inc(S("mod_a_copied"), 1)
            stt(aff1, modT[:, 8:16, :], 1.0, vecT[:, 16:24].unsqueeze(2).broadcast_to([P, KD, 2]),
                ALU.add, ALU.mult).then_inc(S("aff1_done"), 1)

            dve.wait_ge(S("lk_ready"), 1)
            for to in range(CH):
                for ti in range(CH):
                    o = L[32 * ti:32 * ti + 32, :, 32 * to:32 * to + 32]
                    if ti <= to:
                        s = ti + 3 - to
                        d(cp(o, bank[6][32 * s:32 * s + 32, :].rearrange("p (a b) -> p a b", a=GP)))
                    else:
                        s = ti - to
                        d(cp(o, bank[7][32 * s:32 * s + 32, :].rearrange("p (a b) -> p a b", a=GP)))
            d.settle()
            for t in range(CH):
                o = L[32 * t:32 * t + 32, :, 32 * t:32 * t + 32]
                d(tt(o, o, bank[7][0:32, :].rearrange("p (a b) -> p a b", a=GP), ALU.add))
            d.settle()
            dve.sem_inc(S("lk_copied"), 1)
            for gp in range(GP):
                d(stt(L[:, gp, :], ident[:, :], vecT[:, 80 + gp:81 + gp], L[:, gp, :], ALU.mult, ALU.add))
            dve.wait_ge(S("ca_zero"), 1)
            for t in range(CH):
                d(tt(prod1, CT[:, 0], over_h(pwC[:, 0, t, :]), ALU.mult))
                v(tt(prod2, CT[:, 1], over_h(pwC[:, 1, t, :]), ALU.mult))
                halves(CA[:, 0, :, 32 * t:32 * t + 32], prod1, prod2, ALU.subtract)
                d.settle()
                d(tt(prod1, CT[:, 0], over_h(pwC[:, 1, t, :]), ALU.mult))
                v(tt(prod2, CT[:, 1], over_h(pwC[:, 0, t, :]), ALU.mult))
                for g in range(2):
                    part = slice(64 * g, 64 * g + 64)
                    d(stt(CA[part, 1, :, 32 * t + 16 * g:32 * t + 16 * g + 16], prod1[part], -1.0, prod2[part],
                          ALU.mult, ALU.subtract))
                d.settle()
            dve.sem_inc(S("params_done"), 1)

            dve.wait_ge(S("unit_used"), 5)
            for b in range(2, 4):
                for t in range(CH):
                    last = cp(chunk_dst(t, b), chunk_src(t, b))
            last.then_inc(S("u_done_v"), 1)
            Vr = V.rearrange("p (d r) (i g) -> p d i g r", d=2, i=2)
            for n in range(16):
                dve.wait_ge(S("v_ready"), n + 1)
                dr, g0 = (2 * n) // GP, (2 * n) % GP
                for ri in range(2):
                    last = cp(Vr[:, dr, ri, g0:g0 + 2, 1 - dr:1 - dr + NC],
                              bank[n % 4][:, 2 * ri * NC:2 * ri * NC + 2 * NC].rearrange("p (g j) -> p g j", g=2))
                    if ri == 0:
                        d(last)
                last.then_inc(S("v_copied"), 1)
            dve.wait_ge(S("v_copied"), 16)
            d.settle()
            d(V_.memset(V[:, 0, :], 0.0))
            d(cp(V[:, LAT, :].rearrange("p (i g) -> p i g", i=2), s0c[:, :, 0:GP]))
            v(cp(V[:, 2 * ROWS - 1, :].rearrange("p (i g) -> p i g", i=2), s0c[:, :, GP:Q]))
            dve.sem_inc(S("v_init"), 1)

            def row_pair(f, b):
                return V[:, f:b + 1:b - f, :].rearrange("p d (i g) -> p d i g", i=2)

            for s in range(64):
                prev = row_pair(LAT + s, 2 * ROWS - 1 - s)
                nxt = row_pair(LAT + 1 + s, 2 * ROWS - 2 - s)
                d(tt(dt1, prev, Tre, ALU.mult))
                d(tt(dt2[:, :, ::-1, :], prev, Tim, ALU.mult))
                d.settle(d.n - 1)
                d(tt(nxt, nxt, dt1, ALU.add))
                d.settle()
                last = tt(nxt, nxt, dt2, ALU.add)
                if s < 63:
                    v(last)
            last.then_inc(S("lat_states"), 1)

            dve.wait_ge(S("ln_in"), 48)
            for t in range(NT):
                dve.wait_ge(S("vg_done"), t + 1)
                v(V_.bn_stats(bnst[:, :], vn[:, t, :]))
                v(V_.bn_aggr(bnag[:, 2 * t:2 * t + 2], bnst[:, :]))
            bv = bnag[:, 0:6].rearrange("p (t m) -> p m t", m=2)
            cp(st[:, 12:15], bv[:, 1, :]).then_inc(S("ln_var"), 1)
            dve.wait_ge(S("ln_root"), 1)
            v(V_.reciprocal(st[:, 20:23], st[:, 16:19]))
            for t in range(NT):
                v(ts(vn[:, t, :], vn[:, t, :], bnag[:, 2 * t:2 * t + 1], st[:, 20 + t:21 + t],
                     ALU.subtract, ALU.mult))
                v(tt(vn[:, t, :], vn[:, t, :], lnw[:, :], ALU.mult))
                tt(vn[:, t, :], vn[:, t, :], lnb[:, :], ALU.add).then_inc(S("vn_done"), 1)
            dve.wait_ge(S("ws_ready"), 1)
            cp(wsT.rearrange("p a b -> p (a b)"), bank[4][:, :]).then_inc(S("ws_copied"), 1)
            dve.wait_ge(S("unit_used"), 15)
            v(tt(modT[:, 16:48, :], bank[6][:, 0:64].rearrange("p (a b) -> p a b", b=2),
                 vecT[:, 48:80].unsqueeze(2).broadcast_to([P, 32, 2]), ALU.add))
            dve.sem_inc(S("mod_b_copied"), 1)
            stt(aff2, modT[:, 32:40, :], 1.0, vecT[:, 24:32].unsqueeze(2).broadcast_to([P, KD, 2]),
                ALU.add, ALU.mult).then_inc(S("aff2_done"), 1)
            for t in range(NT):
                dve.wait_ge(S("spatial_ready"), t + 1)
                o = yT[:, 4:8, T0[t]:T0[t] + P]
                v(tt(o, bank[(7, 5, 6)[t]][:, :].rearrange("p (a b) -> p a b", a=4), bsr, ALU.add))
                tt(o, o, ugT[:, :, T0[t]:T0[t] + P], ALU.mult).then_inc(S("yg_done"), 1)
            dve.wait_ge(S("ctx_states"), 1)
            d(cp(fin[:, :, 0:GP], V[:, LAT - 1, :].rearrange("p (i g) -> p i g", i=2)))
            cp(fin[:, :, GP:Q], V[:, ROWS, :].rearrange("p (i g) -> p i g", i=2)).then_inc(S("fin_done"), 1)
            dve.wait_ge(S("states_ready"), 1)
            cp(statesT[0:64, :], bank[4][0:64, 0:P]).then_inc(S("states_copied"), 1)
            dve.wait_ge(S("y_ready"), 4)
            for n in range(12):
                dve.wait_ge(S("spread_ready"), n + 1)
                cp(rows[:, n // 4, (n // 2) % 2, (n % 2) * 512:(n % 2) * 512 + 512],
                   bank[4 + n % 4][:, :]).then_inc(S("spread_copied"), 1)
            for c in range(4):
                dve.wait_ge(S("sgm_done"), c + 1)
                tt(yT[:, c, :], gT[:, c, :], sgm[:, c, :], ALU.mult).then_inc(S("yt_done"), 1)
            for n in range(6):
                t, h = divmod(n, 2)
                c = slice(h * 512, h * 512 + 512)
                dve.wait_ge(S("wo_ready"), n + 1)
                v(tt(xtmp[:, :], bank[4 + n % 4][:, :], rows[:, 2, min(t, 1), c], ALU.mult))
                tt(X[:, t, c], X[:, t, c], xtmp[:, :], ALU.add).then_inc(S("x1_done"), 1)
                if n < 5:
                    dve.wait_ge(S("x1_done"), n + 1)
            for t in range(NT):
                dve.wait_ge(S("root2_done"), t + 1)
                v(V_.reciprocal(st[:, 6 + t:7 + t], st[:, 3 + t:4 + t]))
                v(stt(h2[:, t, :], X[:, t, :], st[:, 6 + t:7 + t], rows[:, 0, min(t, 1), :], ALU.mult, ALU.mult))
                tt(h2[:, t, :], h2[:, t, :], rows[:, 1, min(t, 1), :], ALU.add).then_inc(S("h2_done"), 1)

            flat = "p a b -> p (a b)"
            row16 = desc[:, :].unsqueeze(1).broadcast_to([P, NT, NE])
            row4 = desc[:, 12:16].unsqueeze(1).broadcast_to([P, NT, 4])
            dve.wait_ge(S("exp_done"), 1)
            dve.wait_ge(S("tri_done"), 1)
            v(ts(r1.rearrange(flat), r1.rearrange(flat), 1.0, None, ALU.add))
            v(V_.reciprocal(sig.rearrange(flat), r1.rearrange(flat)))
            v(tt(sel, sig, rbrow[:, :].unsqueeze(1).broadcast_to([P, NT, NE]), ALU.add))
            quad = sel.rearrange("p t (g e) -> p e t g", e=4)
            d(tt(g1, quad[:, 0], quad[:, 1], ALU.max))
            d(tt(g2, quad[:, 0], quad[:, 1], ALU.min))
            d(tt(g3, quad[:, 2], quad[:, 3], ALU.max))
            v(tt(g4, quad[:, 2], quad[:, 3], ALU.min))
            v(tt(g4, g2, g4, ALU.max))
            d(tt(g2, g1, g3, ALU.min))
            v(tt(g1, g1, g3, ALU.max))
            v(tt(g2, g2, g4, ALU.max))
            v(tt(g1, g1, g2, ALU.add))

            def first_max(o, x, n, prio, scratch):
                v(V_.tensor_reduce(q1[:, 0:NT], x, AX.X, ALU.max))
                v(tt(scratch, x, q1[:, 0:NT].unsqueeze(2).broadcast_to([P, NT, n]), ALU.is_equal))
                v(tt(scratch, scratch, prio, ALU.mult))
                v(V_.tensor_reduce(q1[:, 0:NT], scratch, AX.X, ALU.max))
                v(tt(o, scratch, q1[:, 0:NT].unsqueeze(2).broadcast_to([P, NT, n]), ALU.is_equal))

            first_max(g3, g1, 4, row4, g2)
            v(ts(g3, g3, BIG, -BIG, ALU.mult, ALU.add))
            v(tt(r1.rearrange("p t (g e) -> p (t g) e", e=4), sel.rearrange("p t (g e) -> p (t g) e", e=4),
                 g3.rearrange(flat).unsqueeze(2).broadcast_to([P, 12, 4]), ALU.add))
            first_max(oh1, r1, NE, row16, r2)
            v(stt(r1, oh1, -BIG, r1, ALU.mult, ALU.add))
            first_max(oh2, r1, NE, row16, r2)
            tt(mk, oh1, oh2, ALU.add).then_inc(S("mk_done"), 1)
            v(tt(r1, sig, oh1, ALU.mult))
            v(V_.tensor_reduce(q1[:, 0:NT], r1, AX.X, ALU.add))
            v(tt(r1, sig, oh2, ALU.mult))
            v(V_.tensor_reduce(q2[:, 0:NT], r1, AX.X, ALU.add))
            v(tt(q3[:, 0:NT], q1[:, 0:NT], q2[:, 0:NT], ALU.add))
            v(V_.reciprocal(st[:, 24:27], q3[:, 0:NT]))
            d(tt(wts[:, 0:3], q1[:, 0:NT], st[:, 24:27], ALU.mult))
            d(tt(wts[:, 3:6], q2[:, 0:NT], st[:, 24:27], ALU.mult))
            dve.wait_ge(S("ranks_ready"), 1)
            cnt, inc = r2[:, 0, :], r2[:, 1, :]
            v(cp(cnt, bank[5][:, 48:64]))
            v(V_.tensor_tensor_scan(inc, ones[:, 0:NE], cnt, 0.0, ALU.mult, ALU.add))
            v(tt(inc, inc, cnt, ALU.subtract))
            d(cp(n_i[:, :], cnt))
            v(cp(off_i[:, :], inc))
            dve.sem_inc(S("int_done"), 1)
            v(tt(r1, bank[5][:, 0:NT * NE].rearrange("p (t e) -> p t e", t=NT),
                 inc.unsqueeze(1).broadcast_to([P, NT, NE]), ALU.add))
            for o, c in ((oh1, 0), (oh2, 3)):
                v(tt(o, o, r1, ALU.mult))
                v(V_.tensor_reduce(q1[:, 0:NT], o, AX.X, ALU.add))
                v(cp(pos_u[:, c:c + 3], q1[:, 0:NT]))
            dve.sem_inc(S("routed"), 1)
            dve.wait_ge(S("glu_ready"), 4)
            for n in range(4):
                dve.wait_ge(S("g2_ready"), n + 1)
                cp(g2rows[:, n // 2, (n % 2) * 512:(n % 2) * 512 + 512],
                   bank[(6, 7, 2, 3)[n]][:, :]).then_inc(S("g2_copied"), 1)
            for n in range(1, 12, 2):
                dve.wait_ge(S("hs_ready"), n + 1)
                t, h = divmod(n, 2)
                cp(hTs[:, 4 * h:4 * h + 4, t * P:(t + 1) * P],
                   bank[n % 4][:, :].rearrange("p (a b) -> p a b", a=4)).then_inc(S("hs_copied_v"), 1)

            for f in FAM:
                dve.sem_inc(S(f"evac_v_{f}"), 1)

            def one_pass(f, e):
                for j in range(4):
                    dve.wait_ge(S(f"silu_done_{f}"), e * 4 + j + 1)
                    tt(actT[:, j, :], sg[:, j % 2, :], bank[j][:, P:2 * P], ALU.mult).then_inc(S(f"act_done_{f}"), 1)
                dve.wait_ge(S(f"down_ready_{f}"), e * 2 + 2)
                if f == "a":
                    for x in FAM:
                        dve.wait_ge(S(f"written_{x}"), (e + 1) * 16)
                else:
                    dve.wait_ge(S("written_a" if f == "b" else "written_b"), (e + 2) * 16)
                cp(ystage[:, 512:D], bank[5][:, :]).then_inc(S(f"evac_v_{f}"), 1)

            def expert(e):
                one_pass("a", e)
                for i, f in enumerate("bc"):
                    n = dve.value_load(n_i[0:1, bass.ds(e, 1)], min_val=0, max_val=NT * P)
                    with dve.If(n > P * (i + 1)):
                        one_pass(f, e)
                    with dve.Else():
                        dve.sem_inc(S(f"act_done_{f}"), 4)
                        dve.sem_inc(S(f"evac_v_{f}"), 1)

            with dve.Fori(0, NE) as e:
                expert(e)

            for t in range(NT):
                dve.wait_ge(S(f"picked_in{t}"), 32)
                y0, y1 = picked[:, t, 0, :], picked[:, t, 1, :]
                v(ts(y0, y0, wts[:, t:t + 1], None, ALU.mult))
                v(stt(y0, y1, wts[:, 3 + t:4 + t], y0, ALU.mult, ALU.add))
                v(tt(y0, y0, g2rows[:, min(t, 1), :], ALU.mult))
                tt(X[:, t, :], X[:, t, :], y0, ALU.add).then_inc(S("x2_done"), 1)
            dve.wait_ge(S("fnw_in"), 16)
            for t in range(NT):
                dve.wait_ge(S("root3_done"), t + 1)
                v(V_.reciprocal(st[:, 6 + t:7 + t], st[:, 3 + t:4 + t]))
                stt(X[:, t, :], X[:, t, :], st[:, 6 + t:7 + t], fnw[:, :], ALU.mult,
                    ALU.mult).then_inc(S("final_done"), 1)

        @block.gpsimd
        def _(pool):
            G = nc.gpsimd
            p = Steps(pool, S("pool_own"))

            def w(ins):
                p(ins)
                p.settle()

            w(G.memset(ident[:, :], 0.0))
            G.affine_select(out=ident[:, :], in_=ident[:, :], compare_op=ALU.not_equal, fill=1.0, base=0,
                            pattern=[[-1, P]], channel_multiplier=1).then_inc(S("ident_ready"), 1)
            p(G.memset(BB[0], 0.0))
            p(G.memset(BB[1], 0.0))
            w(G.memset(Cbd, 0.0))
            pool.sem_inc(S("zeros_done"), 1)
            pool.wait_ge(S("lk_ready"), 1)
            G.memset(CA, 0.0).then_inc(S("ca_zero"), 1)
            pool.wait_ge(S("bt_ready"), 16)
            G.memset(h1T[:, :, P:T0[1]], 0.0).then_inc(S("gap_done"), 1)
            pool.wait_ge(S("x_in"), 48)
            pool.wait_ge(S("v_init"), 1)
            for s in range(32):
                f, b = s, ROWS + LAT - 1 - s
                prev = V[:, f:b + 1:b - f, :].rearrange("p d (i g) -> p d i g", i=2)
                f, b = s + 1, ROWS + LAT - 2 - s
                nxt = V[:, f:b + 1:b - f, :].rearrange("p d (i g) -> p d i g", i=2)
                p(G.tensor_tensor(pt1, prev, Tre, ALU.mult))
                w(G.tensor_tensor(pt2[:, :, ::-1, :], prev, Tim, ALU.mult))
                w(G.tensor_tensor(nxt, nxt, pt1, ALU.add))
                last = G.tensor_tensor(nxt, nxt, pt2, ALU.add)
                if s < 31:
                    w(last)
            last.then_inc(S("ctx_states"), 1)
            pool.wait_ge(S("yg_done"), 3)
            pool.dma_start(router_w, io["router_w"].rearrange("(k p) n -> p k n", p=P)).then_inc(S("rw_in"), 16)
            pool.dma_start(rbrow, io["router_b"].partition_broadcast(P)).then_inc(S("rw_in"), 16)
            p(G.memset(ones[:, :], 1.0))
            w(G.memset(tri[:, :], 1.0))
            p(G.affine_select(out=tri[:, :], in_=tri[:, :], compare_op=ALU.is_gt, fill=0.0, base=0,
                              pattern=[[1, P]], channel_multiplier=-1))
            w(G.iota(desc_i, [[-1, NE]], base=NE, channel_multiplier=0))
            G.tensor_copy(desc[:, :], desc_i).then_inc(S("tri_done"), 1)
            pool.wait_ge(S("rw_in"), 32)
            pool.wait_ge(S("routed"), 1)
            for k in range(2):
                for t in range(NT):
                    pool.indirect_dma_start(
                        out=hsd, out_offset=bass.IndirectOffsetOnAxis(ap=pos_u[:, 3 * k + t:3 * k + t + 1], axis=0),
                        in_=h2[:, t, :], in_offset=None).then_inc(S("tok_sent"), 16)
            pool.dma_start(ysd[PAIRS:SORTED, :], h2[:, 0, :]).then_inc(S("tok_sent"), 16)
            G.memset(hTs[:, :, PAIRS:SORTED], 0.0).then_inc(S("pad_done"), 1)
            for f in FAM:
                pool.wait_ge(S(f"written_{f}"), 16 * (NE + 1))
            for t in range(NT):
                for k in range(2):
                    pool.indirect_dma_start(
                        out=picked[:, t, k, :], out_offset=None, in_=ysd,
                        in_offset=bass.IndirectOffsetOnAxis(ap=pos_u[:, 3 * k + t:3 * k + t + 1], axis=0)
                    ).then_inc(S(f"picked_in{t}"), 16)


IN_NAMES = ["x_prompt", "x_sample", "c", "state_ssm_re", "state_ssm_im", "c_ctx", "norm1_w", "norm2_w", "w_mod",
            "b_mod", "w_in", "ssm_a_re", "ssm_a_im", "ssm_log_dt", "ssm_b_re", "ssm_b_im", "ssm_c_re", "ssm_c_im",
            "ssm_d", "w_glu", "gmlp_ln_w", "gmlp_ln_b", "gmlp_w_s", "gmlp_b_s", "w_out", "router_w", "router_b",
            "w_gate", "w_up", "w_down", "final_norm_w"]
OUTS = [("out_p", (1, 128, 1024)), ("out_s", (1, 256, 1024)), ("out_re", (1, 1, 2, 32, 64)),
        ("out_im", (1, 1, 2, 32, 64))]


def kernel(**inputs):
    import concourse.bacc as bacc
    import numpy as np
    from concourse.bass_utils import run_bass_kernel_spmd

    nc = bacc.Bacc("TRN2", target_bir_lowering=False, num_devices=1)
    arrays, io = {}, {}
    for name in IN_NAMES:
        a = np.ascontiguousarray(inputs[name])
        arrays[f"in_{name}"] = a
        io[name] = nc.dram_tensor(f"in_{name}", a.shape, mybir.dt.from_np(a.dtype), kind="ExternalInput").ap()
    for name, shape in OUTS:
        io[name] = nc.dram_tensor(name, shape, F32, kind="ExternalOutput").ap()
    build(nc, io)
    r = run_bass_kernel_spmd(nc, [arrays], core_ids=[0])
    return tuple(r.results[0][name] for name, _ in OUTS)
```

```python
from contextlib import ExitStack

import concourse.bass as bass
from concourse import mybir

F32 = mybir.dt.float32
I32 = mybir.dt.int32
U32 = mybir.dt.uint32
ALU = mybir.AluOpType
ACT = mybir.ActivationFunctionType
AX = mybir.AxisListType

P = 128
D = 1024
KD = D // P
DS = 512
NT = 3
CH = 4
NC = 97
TOK = NC * CH
T0 = [0, 132, 260]
GP = 16
Q = 2 * GP
ROWS = 98
LAT = 33
HEADS = 4
NE = 16
DE = 512
PAIRS = 2 * NT * P
SORTED = PAIRS + P
UNIT = 4096
EPS = 1e-6
PI = 3.141592653589793
BIG = 1.0e30


class Steps:

    def __init__(self, eng, sem):
        self.eng, self.sem, self.n = eng, sem, 0

    def __call__(self, ins):
        ins.then_inc(self.sem, 1)
        self.n += 1
        return self.n

    def settle(self, n=None):
        self.eng.wait_ge(self.sem, self.n if n is None else n)


def build(nc, io):
    ctx = ExitStack()
    with ctx:
        sems = {}

        def S(name):
            if name not in sems:
                sems[name] = ctx.enter_context(nc.semaphore(name))
            return sems[name]

        arena = ctx.enter_context(nc.sbuf_tensor("arena", [P, 9 * UNIT + 16128], F32))
        n_i = ctx.enter_context(nc.sbuf_tensor("n_i", [P, NE], I32))
        off_i = ctx.enter_context(nc.sbuf_tensor("off_i", [P, NE], I32))
        pos_u = ctx.enter_context(nc.sbuf_tensor("pos_u", [P, 8], U32))
        wts = ctx.enter_context(nc.sbuf_tensor("wts", [P, 8], F32))
        psum = ctx.enter_context(nc.psum_tensor("psum", [P, 8, 512], F32))
        bank = [psum[:, i, :] for i in range(8)]

        def view(off, *dims):
            n = 1
            for x in dims:
                n *= x
            v = arena[:, off:off + n]
            if len(dims) == 2:
                v = v.rearrange("p (a b) -> p a b", a=dims[0])
            if len(dims) == 3:
                v = v.rearrange("p (a b c) -> p a b c", a=dims[0], b=dims[1])
            if len(dims) == 4:
                v = v.rearrange("p (a b c d) -> p a b c d", a=dims[0], b=dims[1], c=dims[2])
            return v

        def slot(s):
            return s * UNIT

        F = 9 * UNIT
        X = view(F, NT, D)
        h1T = view(F + 3072, KD, TOK)
        yT = h1T
        U = view(F + 6176, GP, NC)
        L = view(F + 7728, GP, P)
        wglu = view(F + 9776, 4, DS)
        ugT = view(F + 11824, HEADS, TOK)
        vn = view(F + 13376, NT, DS)
        gT = view(F + 13376, 4, TOK)
        xn = view(F + 11824, NT, D)
        BT = view(slot(7), 2, Q, 16)
        Bb = view(slot(7) + 1024, 2, Q, 16)
        Cbd = view(slot(8) + 2048, 2, Q, 32)
        CA = view(slot(3), 2, Q, P)
        BB = [view(slot(5), Q, P), view(slot(2), Q, P)]
        rawB = arena[0:64, slot(6):slot(6) + 2048]
        rawC = arena[0:64, F + 7728:F + 7728 + 2048]
        CT = view(F + 9776, 2, Q, 16)
        prod1 = view(F + 10800, Q, 16)
        prod2 = view(F + 11312, Q, 16)
        Bt = view(slot(7), 2, Q, P)
        V = view(slot(5), 2 * ROWS, 32)
        prm = slot(6) + 2176
        lnw = view(prm, DS)
        lnb = view(prm + 512, DS)
        bsr = view(prm + 1024, HEADS, P)
        wsraw = view(slot(2), HEADS, P)
        wsT = view(slot(2) + 512, HEADS, P)
        wout = [view(slot(7), KD, 512), view(slot(8), KD, 512)]
        g1rows = view(F + 6176, 2, D)
        abrows = view(F + 9776, 2, 2, D)
        mrow1 = arena[0:2, slot(8):slot(8) + 2048]
        n2rows = view(F + 13872, D)
        mrow = arena[0:2, slot(2) + 1024:slot(2) + 4096]
        g2rows = view(F + 10240, 2, D)
        h2 = view(slot(6), NT, D)
        h2T = view(F + 3072, KD, NT * P)
        hsr = view(slot(7), 6, D)
        hTs = view(F + 3072, KD, SORTED)
        ystage = view(F + 12288, D)
        actT = view(F + 13312, 4, P)
        sg = view(F + 13824, 2, P)
        picked = view(slot(3), NT, 2, D)
        fnw = view(slot(5), D)

        cur = [F + 14928]

        def small(*dims):
            n = 1
            for x in dims:
                n *= x
            v = view(cur[0], *dims)
            cur[0] += n
            assert cur[0] <= F + 16128
            return v

        ident = small(P)
        vecT = small(P)
        sil = small(KD, 2)
        modT = small(2, 2, KD)
        aff1 = small(2, KD)
        Tre = small(2, 2, GP)
        Tim = small(2, 2, GP)
        dt1, dt2 = small(2, 2, GP), small(2, 2, GP)
        pt1, pt2 = small(2, 2, GP), small(2, 2, GP)
        st = small(32)
        fin = small(2, Q)

        epsc = small(1)
        bnst, bnag = small(6), small(6)

        pc = [prm]

        def temp(*dims):
            n = 1
            for x in dims:
                n *= x
            v = view(pc[0], *dims)
            pc[0] += n
            assert pc[0] <= slot(7)
            return v

        arow = temp(P)
        adrow = temp(P)
        dtr = temp(4)
        acol = temp(4, Q)
        adcol = temp(2, Q)
        tp = [temp(Q) for _ in range(8)]
        sincos_in = view(pc[0] - 7 * Q, 2 * Q)
        sincos_out = view(pc[0] - 5 * Q, 2 * Q)
        pw = temp(5, 2, Q)
        pwB = temp(2, 4, Q)
        pwC = temp(2, 4, Q)
        s0c = small(2, Q)
        statesT = small(P)
        vrows = view(slot(6) + 2048, P)

        hsd = nc.dram_tensor("sorted_tokens", (SORTED, D), F32, kind="Internal").ap()
        modd = nc.dram_tensor("modulation_rows", (6, 2, D), F32, kind="Internal").ap()
        ysd = nc.dram_tensor("sorted_outputs", (SORTED, D), F32, kind="Internal").ap()
        w_mod = io["w_mod"][0].rearrange("(k p) n -> p k n", p=P)
        w_in = io["w_in"][0].rearrange("(k p) n -> p k n", p=P)
        w_out = io["w_out"][0].rearrange("(k p) n -> p k n", p=P)
        wg = io["w_gate"][0].rearrange("e (k p) n -> p e k n", p=P)
        wu = io["w_up"][0].rearrange("e (k p) n -> p e k n", p=P)
        wd = io["w_down"][0].rearrange("e (k p) n -> p e k n", p=P)

        def mod_half(m, h):
            return ("mod", 2 * m + h, w_mod[:, :, m * D + h * 512:m * D + h * 512 + 512])

        def in_part(n):
            return ("in", n, w_in[:, :, n * 512:n * 512 + 512])

        units = [mod_half(0, 0), mod_half(0, 1), mod_half(1, 0), mod_half(1, 1), in_part(0), in_part(1), in_part(2)] \
            + [mod_half(m, h) for m in (2, 4, 3, 5) for h in range(2)]
        RING = 2
        NPRE = 13
        GROUPS = 3
        EROUNDS = NE // GROUPS

        def chunk_dst(t, b):
            return U[32 * t:32 * t + 32, b:GP:4, :]

        def chunk_src(t, b):
            return psum[32 * b:32 * b + 32, 0:4, 0:TOK].rearrange("p c (j t) -> p t c j", t=CH)[:, t, :, :]

        def eunits(g):
            return view(slot(3 * g), KD, 512), view(slot(3 * g + 1), KD, 512), view(slot(3 * g + 2), 4, D)

        router_w = view(slot(6) + 3840, KD, NE)
        rbrow = view(slot(6) + 3968, NE)
        rc = [slot(6) + 3072]

        def rtemp(*dims):
            n = 1
            for x in dims:
                n *= x
            v = view(rc[0], *dims)
            rc[0] += n
            assert rc[0] <= slot(6) + 3840
            return v

        tri = rtemp(P)
        ones = rtemp(P)
        desc = rtemp(NE)
        sig, sel, r1, r2, mk, oh1, oh2 = (rtemp(NT, NE) for _ in range(7))
        g1, g2, g3, g4 = (rtemp(NT, 4) for _ in range(4))
        q1, q2, q3 = rtemp(4), rtemp(4), rtemp(4)
        desc_i = rtemp(NE).bitcast(I32)
        sgm = view(slot(6), 4, TOK)
        xtmp = view(F + 6176 + 2048, 512)
        FAM = "abc"

        block = ctx.enter_context(nc.Block())


        @block.sync
        def _(sp):
            def prologue_unit(i):
                if i >= RING:
                    sp.wait_ge(S("unit_used"), i - RING + 1)
                sp.dma_start(view(slot(i % RING), KD, 512), units[i][2]).then_inc(S(f"unit_in{i % RING}"), 16)

            sp.wait_ge(S("vec_in"), 5 * 16)
            prologue_unit(0)
            for i, name in enumerate(("ssm_b_re", "ssm_b_im")):
                sp.dma_start(rawB[32 * i:32 * i + 32, :],
                             io[name][0].rearrange("d (g t) n h -> (d g) (t n h)", t=2)).then_inc(S("b_in"), 16)
            prologue_unit(1)
            for i, name in enumerate(("ssm_c_re", "ssm_c_im")):
                for g in range(2):
                    sp.dma_start(rawC[32 * i:32 * i + 32, :].rearrange("q (h t n) -> q t h n", h=16, t=2)[:, g],
                                 io[name][0].rearrange("d (g t) h n -> (d g) t h n", t=2)[:, g]
                                 ).then_inc(S("c_in"), 16)
            for i in range(2, 7):
                prologue_unit(i)
            sp.wait_ge(S("params_done"), 1)
            sp.dma_start(wglu, io["w_glu"][0].rearrange("(k p) n -> p k n", p=P)).then_inc(S("wglu_in"), 16)
            sp.dma_start(lnw, io["gmlp_ln_w"][0].partition_broadcast(P)).then_inc(S("ln_in"), 16)
            sp.dma_start(lnb, io["gmlp_ln_b"][0].partition_broadcast(P)).then_inc(S("ln_in"), 16)
            sp.dma_start(bsr, io["gmlp_b_s"][0].partition_broadcast(P)).then_inc(S("ln_in"), 16)
            sp.wait_ge(S("bt_ready"), 16)
            sp.dma_start(wsraw, io["gmlp_w_s"][0].rearrange("h p q -> p h q")).then_inc(S("ws_in"), 16)
            prologue_unit(7)
            prologue_unit(8)
            sp.wait_ge(S("v_ready"), 16)
            for h in range(2):
                sp.dma_start(wout[h], w_out[:, :, h * 512:h * 512 + 512]).then_inc(S("wout_in"), 16)
            for i in range(9, 15):
                prologue_unit(i)

            def load(g, e):
                for name, dst, w in zip(("gate", "up", "down"), eunits(g), (wg, wu, wd)):
                    if not isinstance(e, int) or e >= GROUPS:
                        for f in FAM:
                            if name == "gate":
                                sp.wait_ge(S(f"act_done_{f}"), (e - (GROUPS - 1)) * 4)
                            if name == "down":
                                sp.wait_ge(S(f"evac_v_{f}"), (e - (GROUPS - 1)) + 1)
                    src = w[:, e, :, :] if isinstance(e, int) else \
                        w[:, bass.ds(e, 1), :, :].rearrange("p o k n -> p (o k) n")
                    sp.dma_start(dst, src).then_inc(S(f"{name}_in{g}"), 16)

            sp.wait_ge(S("y_ready"), 4)
            sp.wait_ge(S("modd_in2"), 16)
            sp.dma_start(g1rows.rearrange("p a b -> p (a b)"),
                         modd[2].rearrange("s d -> (s d)").partition_broadcast(P)).then_inc(S("g1_in"), 16)
            sp.wait_ge(S("states_copied"), 1)
            load(1, 1)
            sp.wait_ge(S("yt_done"), 4)
            sp.dma_start(n2rows, io["norm2_w"][0].partition_broadcast(P)).then_inc(S("n2_in"), 16)
            for i, m in enumerate((4, 3)):
                sp.wait_ge(S(f"modd_in{m}"), 16)
                sp.dma_start(abrows[:, i].rearrange("p a b -> p (a b)"),
                             modd[m].rearrange("s d -> (s d)").partition_broadcast(P)).then_inc(S("ab_in"), 16)
            sp.wait_ge(S("unit_used"), 15)
            sp.wait_ge(S("modd_in5"), 16)
            load(0, 0)
            for t in range(6):
                if t == 0:
                    sp.wait_ge(S("tok_sent"), 16 * 7)
                sp.dma_start(hsr[:, t, :], hsd[t * P:(t + 1) * P, :]).then_inc(S(f"hs_in{t}"), 16)
            sp.wait_ge(S("hs_ready"), 12)
            sp.dma_start(g2rows.rearrange("p a b -> p (a b)"),
                         modd[5].rearrange("s d -> (s d)").partition_broadcast(P)).then_inc(S("g2_in"), 16)
            sp.wait_ge(S("routed"), 1)
            load(2, 2)
            with sp.Fori(1, EROUNDS) as r:
                for g in range(GROUPS):
                    load(g, r * GROUPS + g)
            load(0, NE - 1)
            for f in FAM:
                sp.wait_ge(S(f"evac_v_{f}"), NE - 2 + 1)
            sp.dma_start(fnw, io["final_norm_w"].partition_broadcast(P)).then_inc(S("fnw_in"), 16)
            sp.wait_ge(S("states_copied"), 1)
            for ri, name in enumerate(("out_re", "out_im")):
                dst = io[name].rearrange("a b d (g t) n -> (a b d g) (t n)", t=2)
                sp.dma_start(dst, statesT[32 * ri:32 * ri + 32, :]).then_inc(S("out_done"), 16)
            for t in range(NT):
                sp.wait_ge(S("final_done"), t + 1)
                dst = io["out_p"][0] if t == 0 else io["out_s"][0, (t - 1) * P:t * P, :]
                sp.dma_start(dst, X[:, t, :]).then_inc(S("out_done"), 16)
            sp.wait_ge(S("out_done"), 16 * 5)

        @block.tensor
        def _(pe):
            mm, tr = nc.tensor.matmul, nc.tensor.transpose
            pe.wait_ge(S("ident_ready"), 1)
            pe.wait_ge(S("vec_in"), 5 * 16)
            pe.wait_ge(S("d_in"), 4 * 16)
            tr(bank[7][:, 0:96], vrows[0:96, :], ident[0:96, 0:96]).then_inc(S("vec_ready"), 1)
            pe.wait_ge(S("a_in"), 4 * 16)
            tr(bank[6][:, 0:P], arow[:, :], ident[:, :])
            pe.wait_ge(S("adt_done"), 1)
            tr(bank[6][:, P:P + 64], adrow[0:64, :], ident[0:64, 0:64]).then_inc(S("acol_ready"), 1)
            def unit_wait(i):
                pe.wait_ge(S(f"unit_in{i % RING}"), 16 * (i // RING + 1))
                return view(slot(i % RING), KD, 512)

            def modulation(i, b, bias):
                w = unit_wait(i)
                out = bank[b][0:2, :]
                for k in range(KD):
                    last = mm(out, sil[:, k, :], w[:, k, :], start=(k == 0), stop=(k == KD - 1 and not bias))
                if bias:
                    last.then_inc(S("unit_used"), 1)
                    for kk in range(4):
                        c = 32 + 4 * units[i][1] + kk
                        last = mm(out[:, kk * P:(kk + 1) * P], vecT[:, c:c + 1].broadcast_to([P, 2]), ident[:, :],
                                  start=False, stop=(kk == 3))
                return last

            pe.wait_ge(S("sil_ready"), 1)
            pe.wait_ge(S("small_copied"), 1)
            modulation(0, 4, False).then_inc(S("unit_used"), 1)
            modulation(1, 7, False).then_inc(S("unit_used"), 1)
            pe.wait_ge(S("b_in"), 32)
            for h in range(16):
                last = tr(bank[h // 8][:, (h % 8) * 64:(h % 8) * 64 + 64],
                          rawB.rearrange("q (n h) -> q h n", h=16)[:, h, :], ident[0:64, 0:64])
            last.then_inc(S("bt_raw_ready"), 1)
            pe.wait_ge(S("mrow_done"), 1)
            modulation(2, 4, False).then_inc(S("unit_used"), 1)
            pe.wait_ge(S("c_in"), 64)
            for h in range(16):
                last = tr(bank[2 + h // 8][:, (h % 8) * 64:(h % 8) * 64 + 64],
                          rawC[:, h * P:(h + 1) * P], ident[0:64, 0:64])
            last.then_inc(S("ct_raw_ready"), 1)
            pe.wait_ge(S("mrow_done"), 2)
            modulation(3, 7, False).then_inc(S("unit_used"), 1)
            pe.wait_ge(S("mrow_done"), 4)
            for i in range(16):
                last = tr(bank[5][:, 2 * i:2 * i + 2], mrow1[0:2, i * P:(i + 1) * P], ident[0:2, 0:2])
            last.then_inc(S("mod_a_ready"), 1)

            pe.wait_ge(S("xn_done"), 3)
            for k in range(KD):
                if k == 1:
                    pe.wait_ge(S("mod_a_copied"), 1)
                if k >= 2:
                    pe.wait_ge(S("h1_done"), k - 1)
                for t in range(NT):
                    last = tr(bank[4 + k % 2][:, T0[t]:T0[t] + P], xn[:, t, k * P:(k + 1) * P], ident[:, :])
                last.then_inc(S("xt_ready"), 1)

            def z_columns(w, c, out):
                for k in range(KD):
                    last = mm(out, w[:, k, c * P:(c + 1) * P], h1T[:, k, :], start=(k == 0), stop=(k == KD - 1))
                return last

            pe.wait_ge(S("h1_done"), KD)
            pe.wait_ge(S("gap_done"), 1)
            w = unit_wait(4)
            for c in range(4):
                pe.wait_ge(S("raw_copied"), 2)
                last = z_columns(w, c, bank[c][:, 0:TOK])
            last.then_inc(S("unit_used"), 1)
            pe.wait_ge(S("bb_done"), 1)
            pe.wait_ge(S("small_copied"), 2)
            for q in range(Q):
                out = bank[6 + q // 16][:, (q % 16) * 32:(q % 16) * 32 + 32]
                mm(out, BB[0][:, q, :], Cbd[:, 0, q, :], start=True, stop=False)
                last = mm(out, BB[1][:, q, :], Cbd[:, 1, q, :], start=False, stop=True)
            last.then_inc(S("lk_ready"), 1)
            pe.wait_ge(S("u_done_a"), 1)
            pe.wait_ge(S("u_done_v"), 1)
            for n in range(16):
                if n >= 4:
                    pe.wait_ge(S("bt_copied"), n - 3)
                for j in range(4):
                    ri, q = divmod(4 * n + j, Q)
                    last = tr(bank[n % 4][:, j * P:(j + 1) * P], BB[ri][:, q, :], ident[:, :])
                last.then_inc(S("bt_ready"), 1)
            pe.wait_ge(S("bt_copied"), 16)
            for n in range(16):
                if n >= 4:
                    pe.wait_ge(S("v_copied"), n - 3)
                for ri in range(2):
                    for j in range(2):
                        q = 2 * n + j
                        c = (2 * ri + j) * NC
                        last = mm(bank[n % 4][:, c:c + NC], Bt[:, ri, q, :], U[:, q % GP, :], start=True, stop=True)
                last.then_inc(S("v_ready"), 1)

            w = unit_wait(5)
            for c in range(4):
                if c >= 2:
                    pe.wait_ge(S("ug_done"), c - 1)
                last = z_columns(w, c, bank[4 + c % 2][:, 0:TOK])
                last.then_inc(S("zu_ready") if c < 3 else S("unit_used"), 1)
            w = unit_wait(6)
            pe.wait_ge(S("lk_copied"), 1)
            for t in range(NT):
                b = (7, 4, 5)[t]
                if t > 0:
                    pe.wait_ge(S("ug_done"), t + 2)
                for k in range(KD):
                    last = mm(bank[b][:, :], h1T[:, k, T0[t]:T0[t] + P], w[:, k, :],
                              start=(k == 0), stop=(k == KD - 1))
                last.then_inc(S("zv_ready") if t < 2 else S("unit_used"), 1)
            pe.wait_ge(S("v_copied"), 16)
            for i in range(7, NPRE):
                if i >= 9:
                    pe.wait_ge(S("mrow_done"), i - 4)
                modulation(i, (i + 1) % 2, True).then_inc(S("mrow_ready"), 1)
            pe.wait_ge(S("ws_in"), 16)
            pe.wait_ge(S("vg_done"), 2)
            for h in range(HEADS):
                last = tr(bank[4][:, h * P:(h + 1) * P], wsraw[:, h, :], ident[:, :])
            last.then_inc(S("ws_ready"), 1)
            pe.wait_ge(S("ws_copied"), 1)
            pe.wait_ge(S("vg_done"), 3)
            for t in range(NT):
                pe.wait_ge(S("vn_done"), t + 1)
                b = (7, 5, 6)[t]
                for h in range(HEADS):
                    last = mm(bank[b][:, h * P:(h + 1) * P], vn[:, t, h * P:(h + 1) * P], wsT[:, h, :],
                              start=True, stop=True)
                last.then_inc(S("spatial_ready"), 1)

            for i in range(NPRE, 15):
                pe.wait_ge(S("mrow_done"), i - 4)
                modulation(i, (i + 1) % 2, True).then_inc(S("mrow_ready"), 1)
            pe.wait_ge(S("mrow_done"), 12)
            pe.wait_ge(S("lat_states"), 1)
            pe.wait_ge(S("ctx_states"), 1)
            for b in range(4):
                for c in range(4):
                    gp = 4 * c + b
                    out = bank[b][:, c * NC:(c + 1) * NC]
                    mm(out, L[:, gp, :], U[:, gp, :], start=True, stop=False)
                    for d in range(2):
                        for ri in range(2):
                            last = mm(out, CA[:, ri, d * GP + gp, :],
                                      V[:, d * ROWS + d:d * ROWS + d + NC, ri * GP + gp],
                                      start=False, stop=(d == 1 and ri == 1))
                last.then_inc(S("y_ready"), 1)
            pe.wait_ge(S("fin_done"), 1)
            tr(bank[4][0:64, 0:P], fin.rearrange("p a b -> p (a b)"), ident[:, :]).then_inc(S("states_ready"), 1)

            pe.wait_ge(S("wglu_in"), 16)
            pe.wait_ge(S("g_done"), 16)
            for c in range(4):
                for k in range(4):
                    last = mm(bank[c][:, 0:TOK], wglu[:, k, c * P:(c + 1) * P], gT[:, k, :],
                              start=(k == 0), stop=(k == 3))
                last.then_inc(S("glu_ready"), 1)
            pe.wait_ge(S("yt_done"), 4)
            pe.wait_ge(S("wout_in"), 32)
            for n in range(6):
                if n == 0:
                    pe.wait_ge(S("yg_done"), 3)
                    pe.wait_ge(S("states_copied"), 1)
                if n >= 4:
                    pe.wait_ge(S("x1_done"), n - 3)
                t, h = divmod(n, 2)
                for k in range(KD):
                    last = mm(bank[4 + n % 4][:, :], yT[:, k, T0[t]:T0[t] + P], wout[h][:, k, :],
                              start=(k == 0), stop=(k == KD - 1))
                last.then_inc(S("wo_ready"), 1)
            for n in range(6):
                t, h = divmod(n, 2)
                pe.wait_ge(S("h2_done"), t + 1)
                if n >= 4:
                    pe.wait_ge(S("h2t_copied"), n - 3)
                for kk in range(4):
                    k = 4 * h + kk
                    last = tr(bank[n % 4][:, kk * P:(kk + 1) * P], h2[:, t, k * P:(k + 1) * P], ident[:, :])
                last.then_inc(S("h2t_ready"), 1)
            pe.wait_ge(S("h2t_copied"), 6)
            pe.wait_ge(S("x1_done"), 6)
            pe.wait_ge(S("rw_in"), 32)
            for t in range(NT):
                for k in range(KD):
                    last = mm(bank[4][:, t * NE:(t + 1) * NE], h2T[:, k, t * P:(t + 1) * P], router_w[:, k, :],
                              start=(k == 0), stop=(k == KD - 1))
            last.then_inc(S("logits_ready"), 1)
            pe.wait_ge(S("mk_done"), 1)
            pe.wait_ge(S("tri_done"), 1)
            for t in range(NT):
                mm(bank[5][:, t * NE:(t + 1) * NE], tri[:, :], mk[:, t, :], start=True, stop=(t == 0))
                for s in range(t):
                    mm(bank[5][:, t * NE:(t + 1) * NE], ones[:, :], mk[:, s, :], start=False, stop=(s == t - 1))
            for s in range(NT):
                last = mm(bank[5][:, 48:64], ones[:, :], mk[:, s, :], start=(s == 0), stop=(s == NT - 1))
            last.then_inc(S("ranks_ready"), 1)

            for n in range(12):
                t, h = divmod(n, 2)
                pe.wait_ge(S(f"hs_in{t}"), 16)
                if n >= 4:
                    pe.wait_ge(S("hs_copied_a") if n % 2 == 0 else S("hs_copied_v"), (n - 4) // 2 + 1)
                for kk in range(4):
                    k = 4 * h + kk
                    last = tr(bank[n % 4][:, kk * P:(kk + 1) * P], hsr[:, t, k * P:(k + 1) * P], ident[:, :])
                last.then_inc(S("hs_ready"), 1)
            pe.wait_ge(S("hs_copied_a"), 6)
            pe.wait_ge(S("hs_copied_v"), 6)
            pe.wait_ge(S("pad_done"), 1)
            pe.wait_ge(S("int_done"), 1)

            def one_pass(f, e, g, width, start):
                wgt, wup, wdn = eunits(g)
                for j in range(4):
                    for c, w in ((0, wgt), (P, wup)):
                        for k in range(KD):
                            last = mm(bank[j][:, c:c + width], w[:, k, j * P:(j + 1) * P],
                                      hTs[:, k, bass.ds(start, width)], start=(k == 0), stop=(k == KD - 1))
                    last.then_inc(S(f"gu_ready_{f}"), 1)

            def down(f, e, g, width):
                wdn = eunits(g)[2]
                for h in range(2):
                    for j in range(4):
                        last = mm(bank[4 + h][0:width, :], actT[:, j, 0:width], wdn[:, j, h * 512:h * 512 + 512],
                                  start=(j == 0), stop=(j == 3))
                    last.then_inc(S(f"down_ready_{f}"), 1)

            def expert(e, g, round_):
                n = pe.value_load(n_i[0:1, bass.ds(e, 1)], min_val=0, max_val=NT * P)
                start = pe.value_load(off_i[0:1, bass.ds(e, 1)], min_val=0, max_val=PAIRS)
                pe.wait_ge(S(f"gate_in{g}"), 16 * (round_ + 1))
                pe.wait_ge(S(f"up_in{g}"), 16 * (round_ + 1))
                with pe.If(n > 64):
                    one_pass("a", e, g, P, start)
                with pe.Else():
                    one_pass("a", e, g, 64, start)
                pe.wait_ge(S(f"down_in{g}"), 16 * (round_ + 1))
                pe.wait_ge(S("act_done_a"), (e + 1) * 4)
                for x in FAM:
                    pe.wait_ge(S(f"evac_a_{x}"), e + 1)
                    pe.wait_ge(S(f"evac_v_{x}"), e + 1)
                with pe.If(n > 64):
                    down("a", e, g, P)
                with pe.Else():
                    down("a", e, g, 64)
                for i, (f, before) in enumerate((("b", "a"), ("c", "b"))):
                    with pe.If(n > P * (i + 1)):
                        first = pe.value_load(off_i[0:1, bass.ds(e, 1)], min_val=0, max_val=PAIRS - P * (i + 1))
                        one_pass(f, e, g, P, first + P * (i + 1))
                        pe.wait_ge(S(f"act_done_{f}"), (e + 1) * 4)
                        pe.wait_ge(S(f"evac_a_{before}"), e + 2)
                        pe.wait_ge(S(f"evac_v_{before}"), e + 2)
                        down(f, e, g, P)
                    with pe.Else():
                        pe.sem_inc(S(f"gu_ready_{f}"), 4)
                        pe.sem_inc(S(f"down_ready_{f}"), 2)

            with pe.Fori(0, EROUNDS) as r:
                for g in range(GROUPS):
                    expert(r * GROUPS + g, g, r)
            expert(NE - 1, 0, EROUNDS)

        @block.scalar
        def _(act):
            A = nc.scalar.activation
            a = Steps(act, S("act_own"))
            for r0, src in ((0, io["c_ctx"].rearrange("(k p) -> k p", p=P)),
                            (8, io["c"][0].rearrange("(k p) -> k p", p=P)),
                            (16, io["norm1_w"][0].rearrange("(k p) -> k p", p=P)),
                            (24, io["norm2_w"][0].rearrange("(k p) -> k p", p=P)),
                            (32, io["b_mod"][0].rearrange("(k p) -> k p", p=P))):
                act.dma_start(vrows[r0:r0 + src.shape[0], :], src).then_inc(S("vec_in"), 16)
            for t in range(NT):
                src = io["x_prompt"][0] if t == 0 else io["x_sample"][0, (t - 1) * P:t * P, :]
                act.dma_start(X[:, t, :], src).then_inc(S("x_in"), 16)
            act.wait_ge(S("dt_in"), 32)
            A(dtr[0:64, 0:2], dtr[0:64, 0:2], ACT.Exp).then_inc(S("dt_ready"), 1)
            act.wait_ge(S("phase_done"), 1)
            A(tp[5][:, :], adcol[:, 0, :], ACT.Exp).then_inc(S("trig_done"), 1)
            A(sincos_out, sincos_in, ACT.Sin).then_inc(S("trig_done"), 1)
            act.wait_ge(S("small_copied"), 1)
            A(sil.rearrange("p k s -> p s k"), vecT[:, 0:16].rearrange("p (s k) -> p s k", s=2),
              ACT.Silu).then_inc(S("sil_ready"), 1)
            def first_rows(i):
                act.wait_ge(S("unit_used"), i + 1)
                A(mrow1[:, i * 512:(i + 1) * 512], bank[(4, 7)[i % 2]][0:2, :], ACT.Copy).then_inc(S("mrow_done"), 1)

            act.wait_ge(S("x_in"), 48)
            for t in range(NT):
                n = a(A(xn[:, t, :], X[:, t, :], ACT.Square, accum_out=st[:, t:t + 1]))
            a.settle()
            A(st[:, 3:6], st[:, 0:3], ACT.Sqrt, bias=epsc[:, 0:1], scale=1.0 / D).then_inc(S("root_done"), 1)
            act.wait_ge(S("rstd_done"), 1)
            for t in range(NT):
                A(xn[:, t, :], X[:, t, :], ACT.Copy, scale=st[:, 6 + t:7 + t]).then_inc(S("xn_done"), 1)
            for i in range(4):
                first_rows(i)
            act.wait_ge(S("aff1_done"), 1)
            for k in range(KD):
                act.wait_ge(S("xt_ready"), k + 1)
                b = bank[4 + k % 2]
                A(h1T[:, k, 0:P], b[:, 0:P], ACT.Identity, bias=modT[:, 0, 0, k:k + 1], scale=aff1[:, 0, k:k + 1])
                A(h1T[:, k, T0[1]:TOK], b[:, T0[1]:TOK], ACT.Identity, bias=modT[:, 0, 1, k:k + 1],
                  scale=aff1[:, 1, k:k + 1]).then_inc(S("h1_done"), 1)
            act.wait_ge(S("unit_used"), 5)
            for b in range(2):
                for t in range(CH):
                    last = A(chunk_dst(t, b), chunk_src(t, b), ACT.Copy)
            last.then_inc(S("u_done_a"), 1)
            act.wait_ge(S("lk_ready"), 1)
            for to in range(CH):
                for ti in range(CH):
                    o = L[32 * ti:32 * ti + 32, :, 32 * to:32 * to + 32]
                    b, s = (6, ti + 3 - to) if ti <= to else (7, ti - to)
                    last = A(o, bank[b][32 * s:32 * s + 32, :].rearrange("p (a b) -> p a b", a=GP), ACT.Copy)
            last.then_inc(S("l_gathered"), 1)
            Vr = V.rearrange("p (d r) (i g) -> p d i g r", d=2, i=2)
            for n in range(16):
                act.wait_ge(S("v_ready"), n + 1)
                dr, g0 = (2 * n) // GP, (2 * n) % GP
                for ri in range(2):
                    last = A(Vr[:, dr, ri, g0:g0 + 2, 1 - dr:1 - dr + NC],
                             bank[n % 4][:, 2 * ri * NC:2 * ri * NC + 2 * NC].rearrange("p (g j) -> p g j", g=2),
                             ACT.Copy)
                last.then_inc(S("v_copied"), 1)
            for c in range(4):
                act.wait_ge(S("zu_ready") if c < 3 else S("unit_used"), c + 1 if c < 3 else 6)
                A(ugT[:, c, :], bank[4 + c % 2][:, 0:TOK], ACT.Gelu_apprx_tanh).then_inc(S("ug_done"), 1)
            for t in range(NT):
                act.wait_ge(S("zv_ready") if t < 2 else S("unit_used"), t + 1 if t < 2 else 7)
                A(vn[:, t, :], bank[(7, 4, 5)[t]][:, :], ACT.Gelu_apprx_tanh).then_inc(S("vg_done"), 1)
            def ln_root():
                act.wait_ge(S("ln_var"), 1)
                A(st[:, 16:19], st[:, 12:15], ACT.Sqrt, bias=epsc[:, 0:1]).then_inc(S("ln_root"), 1)

            for i in range(8):
                m = (2, 4, 3, 5)[i // 2]
                c = (i // 2) % 3 * D + (i % 2) * 512
                if i == 6:
                    act.wait_ge(S("modd_in2"), 16)
                if i == NPRE - 7:
                    ln_root()
                act.wait_ge(S("mrow_ready"), i + 1)
                A(mrow[:, c:c + 512], bank[i % 2][0:2, :], ACT.Copy).then_inc(S("mrow_done"), 1)
                if i % 2 == 1:
                    act.wait_ge(S("mrow_done"), i + 5)
                    act.dma_start(modd[m], mrow[:, c - 512:c + 512]).then_inc(S(f"modd_in{m}"), 16)
            act.wait_ge(S("spatial_ready"), 3)
            for b in range(4):
                act.wait_ge(S("y_ready"), b + 1)
                for t in range(CH):
                    A(gT[32 * b:32 * b + 32, :, :].rearrange("p c (j t) -> p t c j", t=CH)[:, t, :, :],
                      bank[b][32 * t:32 * t + 32, 0:4 * NC].rearrange("p (c j) -> p c j", c=4),
                      ACT.Gelu_apprx_tanh).then_inc(S("g_done"), 1)
            for c in range(4):
                act.wait_ge(S("glu_ready"), c + 1)
                A(sgm[:, c, :], bank[c][:, 0:TOK], ACT.Sigmoid).then_inc(S("sgm_done"), 1)
            for t in range(NT):
                act.wait_ge(S("x1_done"), 2 * t + 2)
                a(A(h2[:, t, :], X[:, t, :], ACT.Square, accum_out=st[:, t:t + 1]))
                a.settle()
                A(st[:, 3 + t:4 + t], st[:, t:t + 1], ACT.Sqrt, bias=epsc[:, 0:1],
                  scale=1.0 / D).then_inc(S("root2_done"), 1)
            for n in range(6):
                act.wait_ge(S("h2t_ready"), n + 1)
                t, h = divmod(n, 2)
                A(h2T[:, 4 * h:4 * h + 4, t * P:(t + 1) * P], bank[n % 4][:, :].rearrange("p (a b) -> p a b", a=4),
                  ACT.Copy).then_inc(S("h2t_copied"), 1)
            act.wait_ge(S("logits_ready"), 1)
            A(r1.rearrange("p a b -> p (a b)"), bank[4][:, 0:NT * NE], ACT.Exp, scale=-1.0).then_inc(S("exp_done"), 1)
            for n in range(0, 12, 2):
                act.wait_ge(S("hs_ready"), n + 1)
                t, h = divmod(n, 2)
                A(hTs[:, 4 * h:4 * h + 4, t * P:(t + 1) * P], bank[n % 4][:, :].rearrange("p (a b) -> p a b", a=4),
                  ACT.Copy).then_inc(S("hs_copied_a"), 1)

            act.wait_ge(S("int_done"), 1)
            act.wait_ge(S("tok_sent"), 16 * 7)
            for f in FAM:
                act.sem_inc(S(f"evac_a_{f}"), 1)
                act.sem_inc(S(f"written_{f}"), 16)

            def one_pass(f, e, i, start):
                for j in range(4):
                    act.wait_ge(S(f"gu_ready_{f}"), e * 4 + j + 1)
                    if j >= 2:
                        act.wait_ge(S(f"act_done_{f}"), e * 4 + j - 1)
                    A(sg[:, j % 2, :], bank[j][:, 0:P], ACT.Silu).then_inc(S(f"silu_done_{f}"), 1)
                act.wait_ge(S(f"down_ready_{f}"), e * 2 + 1)
                if f == "a":
                    for x in FAM:
                        act.wait_ge(S(f"written_{x}"), (e + 1) * 16)
                else:
                    act.wait_ge(S("written_a" if f == "b" else "written_b"), (e + 2) * 16)
                A(ystage[:, 0:512], bank[4][:, :], ACT.Copy).then_inc(S(f"evac_a_{f}"), 1)
                act.wait_ge(S(f"evac_a_{f}"), e + 2)
                act.wait_ge(S(f"evac_v_{f}"), e + 2)
                act.dma_start(ysd[bass.ds(start + P * i, P), :], ystage[:, :]).then_inc(S(f"written_{f}"), 16)

            def expert(e):
                start = act.value_load(off_i[0:1, bass.ds(e, 1)], min_val=0, max_val=PAIRS)
                one_pass("a", e, 0, start)
                for i, f in enumerate("bc", 1):
                    n = act.value_load(n_i[0:1, bass.ds(e, 1)], min_val=0, max_val=NT * P)
                    with act.If(n > P * i):
                        start = act.value_load(off_i[0:1, bass.ds(e, 1)], min_val=0, max_val=PAIRS - P * i)
                        one_pass(f, e, i, start)
                    with act.Else():
                        act.sem_inc(S(f"silu_done_{f}"), 4)
                        act.sem_inc(S(f"evac_a_{f}"), 1)
                        act.sem_inc(S(f"written_{f}"), 16)

            with act.Fori(0, NE) as e:
                expert(e)
            for t in range(NT):
                act.wait_ge(S("x2_done"), t + 1)
                a(A(picked[:, t, 0, :], X[:, t, :], ACT.Square, accum_out=st[:, t:t + 1]))
                a.settle()
                A(st[:, 3 + t:4 + t], st[:, t:t + 1], ACT.Sqrt, bias=epsc[:, 0:1],
                  scale=1.0 / D).then_inc(S("root3_done"), 1)

        @block.vector
        def _(dve):
            V_ = nc.vector
            d = Steps(dve, S("dve_own"))

            def v(ins):
                d(ins)
                d.settle()

            tt, ts, stt, cp = V_.tensor_tensor, V_.tensor_scalar, V_.scalar_tensor_tensor, V_.tensor_copy
            v(V_.memset(epsc[:, :], EPS))
            dve.wait_ge(S("dt_ready"), 1)
            dve.wait_ge(S("a_in"), 64)
            tt(adrow[0:64, :].rearrange("q (t n) -> q t n", t=2), arow[0:64, :].rearrange("q (t n) -> q t n", t=2),
               dtr[0:64, 0:2].unsqueeze(2).broadcast_to([64, 2, 64]), ALU.mult).then_inc(S("adt_done"), 1)
            dve.wait_ge(S("vec_ready"), 1)
            cp(vecT[:, 0:96], bank[7][:, 0:96]).then_inc(S("small_copied"), 1)
            dve.wait_ge(S("acol_ready"), 1)
            d(cp(acol.rearrange("p a b -> p (a b)"), bank[6][:, 0:P]))
            d(cp(s0c.rearrange("p a b -> p (a b)"), bank[6][:, 64:P]))
            v(cp(adcol.rearrange("p a b -> p (a b)"), bank[6][:, P:P + 64]))
            dve.sem_inc(S("small_copied"), 1)
            ar, ai, adi = acol[:, 0, :], acol[:, 1, :], adcol[:, 1, :]
            k, r, rq = tp[0][:, :], tp[1][:, :], tp[2][:, :]
            lim = 3.1415925
            v(ts(k, adi, 1.0 / (2 * PI), 12582912.0, ALU.mult, ALU.add))
            v(ts(k, k, -12582912.0, None, ALU.add))
            v(stt(r, k, -6.28125, adi, ALU.mult, ALU.add))
            v(stt(r, k, -(2 * PI - 6.28125), r, ALU.mult, ALU.add))
            v(ts(rq, r, PI / 2, None, ALU.add))
            v(ts(k, rq, PI, -2 * PI, ALU.is_gt, ALU.mult))
            v(tt(rq, rq, k, ALU.add))
            ts(sincos_in, sincos_in, lim, -lim, ALU.min, ALU.max).then_inc(S("phase_done"), 1)

            dve.wait_ge(S("root_done"), 1)
            V_.reciprocal(st[:, 6:9], st[:, 3:6]).then_inc(S("rstd_done"), 1)
            dve.wait_ge(S("trig_done"), 2)
            d(V_.memset(pw[:, 0, 0, :], 1.0))
            d(V_.memset(pw[:, 0, 1, :], 0.0))
            d(tt(pw[:, 1, 0, :], tp[5][:, :], tp[4][:, :], ALU.mult))
            v(tt(pw[:, 1, 1, :], tp[5][:, :], tp[3][:, :], ALU.mult))

            def cmul(o, x, y):
                d(tt(tp[0][:, :], x[:, 0, :], y[:, 0, :], ALU.mult))
                d(tt(tp[1][:, :], x[:, 1, :], y[:, 1, :], ALU.mult))
                d(tt(tp[2][:, :], x[:, 0, :], y[:, 1, :], ALU.mult))
                v(tt(tp[3][:, :], x[:, 1, :], y[:, 0, :], ALU.mult))
                d(tt(o[:, 0, :], tp[0][:, :], tp[1][:, :], ALU.subtract))
                v(tt(o[:, 1, :], tp[2][:, :], tp[3][:, :], ALU.add))

            cmul(pw[:, 2], pw[:, 1], pw[:, 1])
            cmul(pw[:, 3], pw[:, 2], pw[:, 1])
            cmul(pw[:, 4], pw[:, 2], pw[:, 2])
            er1, den, fr, fi, m0, m1 = (x[:, :] for x in tp[:6])
            ei = pw[:, 1, 1, :]
            d(ts(er1, pw[:, 1, 0, :], -1.0, None, ALU.add))
            d(tt(m0, ar, ar, ALU.mult))
            v(tt(m1, ai, ai, ALU.mult))
            v(tt(m0, m0, m1, ALU.add))
            v(V_.reciprocal(den, m0))
            d(tt(m0, er1, ar, ALU.mult))
            v(tt(m1, ei, ai, ALU.mult))
            v(tt(m0, m0, m1, ALU.add))
            v(tt(fr, m0, den, ALU.mult))
            d(tt(m0, ei, ar, ALU.mult))
            v(tt(m1, er1, ai, ALU.mult))
            v(tt(m0, m0, m1, ALU.subtract))
            v(tt(fi, m0, den, ALU.mult))
            for t in range(CH):
                for x, kf, kb in ((pwB, 3 - t, t), (pwC, t + 1, 4 - t)):
                    d(cp(x[:, :, t, 0:GP], pw[:, kf, :, 0:GP]))
                    d(cp(x[:, :, t, GP:Q], pw[:, kb, :, GP:Q]))
            for ri in range(2):
                d(cp(Tre[:, :, ri, :], pw[:, 4, 0, :].rearrange("p (d g) -> p d g", d=2)))
            d(cp(Tim[:, :, 0, :], pw[:, 4, 1, :].rearrange("p (d g) -> p d g", d=2)))
            v(ts(Tim[:, :, 1, :], pw[:, 4, 1, :].rearrange("p (d g) -> p d g", d=2), -1.0, None, ALU.mult))

            def over_h(x, n=16):
                return x.unsqueeze(2).broadcast_to([P, Q, n])

            def halves(o, in0, in1, op):
                for g in range(2):
                    part = slice(64 * g, 64 * g + 64)
                    d(tt(o[part, :, 16 * g:16 * g + 16], in0[part], in1[part], op))

            dve.wait_ge(S("bt_raw_ready"), 1)
            for i in range(2):
                d(cp(BT.rearrange("p r q h -> p h (r q)")[:, 8 * i:8 * i + 8, :],
                     bank[i][:, :].rearrange("p (h q) -> p h q", h=8)))
            d.settle()
            for o, x, y, op in ((0, 0, 1, ALU.subtract), (1, 1, 0, ALU.add)):
                d(tt(prod1, BT[:, x], over_h(fr), ALU.mult))
                v(tt(prod2, BT[:, y], over_h(fi), ALU.mult))
                v(tt(Bb[:, o], prod1, prod2, op))
            dve.wait_ge(S("zeros_done"), 1)
            for t in range(CH):
                if t == 1:
                    dve.wait_ge(S("ct_raw_ready"), 1)
                    for i in range(2):
                        cp(CT.rearrange("p r q h -> p h (r q)")[:, 8 * i:8 * i + 8, :],
                             bank[2 + i][:, :].rearrange("p (h q) -> p h q", h=8)).then_inc(S("raw_copied"), 1)
                    dve.wait_ge(S("raw_copied"), 2)
                if t == 2:
                    dve.wait_ge(S("mod_a_ready"), 1)
                    v(tt(modT, bank[5][:, 0:32].rearrange("p (m k s) -> p m s k", m=2, s=2),
                         vecT[:, 32:48].rearrange("p (m k) -> p m k", m=2).unsqueeze(2).broadcast_to([P, 2, 2, KD]),
                         ALU.add))
                    dve.sem_inc(S("mod_a_copied"), 1)
                    stt(aff1, modT[:, 1], 1.0, vecT[:, 16:24].unsqueeze(1).broadcast_to([P, 2, KD]),
                        ALU.add, ALU.mult).then_inc(S("aff1_done"), 1)
                for o, x, y, op in ((0, 0, 1, ALU.subtract), (1, 1, 0, ALU.add)):
                    d(tt(prod1, Bb[:, x], over_h(pwB[:, 0, t, :]), ALU.mult))
                    v(tt(prod2, Bb[:, y], over_h(pwB[:, 1, t, :]), ALU.mult))
                    halves(BB[o][:, :, 32 * t:32 * t + 32], prod1, prod2, op)
                    d.settle()
            for g in range(2):
                part = slice(64 * g, 64 * g + 64)
                d(cp(Cbd[part, 0, :, 16 * g:16 * g + 16], CT[part, 0]))
                v(ts(Cbd[part, 1, :, 16 * g:16 * g + 16], CT[part, 1], -1.0, None, ALU.mult))
            dve.sem_inc(S("bb_done"), 1)

            for t in range(CH):
                d(tt(prod1, CT[:, 0], over_h(pwC[:, 0, t, :]), ALU.mult))
                v(tt(prod2, CT[:, 1], over_h(pwC[:, 1, t, :]), ALU.mult))
                halves(CA[:, 0, :, 32 * t:32 * t + 32], prod1, prod2, ALU.subtract)
                d.settle()
                d(tt(prod1, CT[:, 0], over_h(pwC[:, 1, t, :]), ALU.mult))
                v(tt(prod2, CT[:, 1], over_h(pwC[:, 0, t, :]), ALU.mult))
                for g in range(2):
                    part = slice(64 * g, 64 * g + 64)
                    d(stt(CA[part, 1, :, 32 * t + 16 * g:32 * t + 16 * g + 16], prod1[part], -1.0, prod2[part],
                          ALU.mult, ALU.subtract))
                d.settle()
            dve.sem_inc(S("params_done"), 1)

            dve.wait_ge(S("unit_used"), 5)
            for b in range(2, 4):
                for t in range(CH):
                    last = cp(chunk_dst(t, b), chunk_src(t, b))
            last.then_inc(S("u_done_v"), 1)
            for n in range(16):
                dve.wait_ge(S("bt_ready"), n + 1)
                ri, q = divmod(4 * n, Q)
                cp(Bt[:, ri, q:q + 4, :], bank[n % 4][:, :].rearrange("p (a b) -> p a b", a=4)
                   ).then_inc(S("bt_copied"), 1)
            dve.wait_ge(S("l_gathered"), 1)
            for t in range(CH):
                o = L[32 * t:32 * t + 32, :, 32 * t:32 * t + 32]
                d(tt(o, o, bank[7][0:32, :].rearrange("p (a b) -> p a b", a=GP), ALU.add))
            d.settle()
            dve.sem_inc(S("lk_copied"), 1)
            for gp in range(GP):
                d(stt(L[:, gp, :], ident[:, :], vecT[:, 80 + gp:81 + gp], L[:, gp, :], ALU.mult, ALU.add))
            dve.wait_ge(S("v_copied"), 16)
            d.settle()
            d(V_.memset(V[:, 0, :], 0.0))
            d(cp(V[:, LAT, :].rearrange("p (i g) -> p i g", i=2), s0c[:, :, 0:GP]))
            v(cp(V[:, 2 * ROWS - 1, :].rearrange("p (i g) -> p i g", i=2), s0c[:, :, GP:Q]))
            dve.sem_inc(S("v_init"), 1)

            def row_pair(f, b):
                return V[:, f:b + 1:b - f, :].rearrange("p d (i g) -> p d i g", i=2)

            for s in range(64):
                prev = row_pair(LAT + s, 2 * ROWS - 1 - s)
                nxt = row_pair(LAT + 1 + s, 2 * ROWS - 2 - s)
                d(tt(dt1, prev, Tre, ALU.mult))
                d(tt(dt2[:, :, ::-1, :], prev, Tim, ALU.mult))
                d.settle(d.n - 1)
                d(tt(nxt, nxt, dt1, ALU.add))
                d.settle()
                last = tt(nxt, nxt, dt2, ALU.add)
                if s < 63:
                    v(last)
            last.then_inc(S("lat_states"), 1)

            dve.wait_ge(S("ln_in"), 48)
            for t in range(NT):
                dve.wait_ge(S("vg_done"), t + 1)
                v(V_.bn_stats(bnst[:, :], vn[:, t, :]))
                v(V_.bn_aggr(bnag[:, 2 * t:2 * t + 2], bnst[:, :]))
            bv = bnag[:, 0:6].rearrange("p (t m) -> p m t", m=2)
            cp(st[:, 12:15], bv[:, 1, :]).then_inc(S("ln_var"), 1)
            dve.wait_ge(S("ln_root"), 1)
            v(V_.reciprocal(st[:, 20:23], st[:, 16:19]))
            for t in range(NT):
                v(ts(vn[:, t, :], vn[:, t, :], bnag[:, 2 * t:2 * t + 1], st[:, 20 + t:21 + t],
                     ALU.subtract, ALU.mult))
                v(tt(vn[:, t, :], vn[:, t, :], lnw[:, :], ALU.mult))
                tt(vn[:, t, :], vn[:, t, :], lnb[:, :], ALU.add).then_inc(S("vn_done"), 1)
            dve.wait_ge(S("ws_ready"), 1)
            cp(wsT.rearrange("p a b -> p (a b)"), bank[4][:, :]).then_inc(S("ws_copied"), 1)
            for t in range(NT):
                dve.wait_ge(S("spatial_ready"), t + 1)
                o = yT[:, 4:8, T0[t]:T0[t] + P]
                v(tt(o, bank[(7, 5, 6)[t]][:, :].rearrange("p (a b) -> p a b", a=4), bsr, ALU.add))
                tt(o, o, ugT[:, :, T0[t]:T0[t] + P], ALU.mult).then_inc(S("yg_done"), 1)
            dve.wait_ge(S("ctx_states"), 1)
            d(cp(fin[:, :, 0:GP], V[:, LAT - 1, :].rearrange("p (i g) -> p i g", i=2)))
            cp(fin[:, :, GP:Q], V[:, ROWS, :].rearrange("p (i g) -> p i g", i=2)).then_inc(S("fin_done"), 1)
            dve.wait_ge(S("states_ready"), 1)
            cp(statesT[0:64, :], bank[4][0:64, 0:P]).then_inc(S("states_copied"), 1)
            for c in range(4):
                dve.wait_ge(S("sgm_done"), c + 1)
                tt(yT[:, c, :], gT[:, c, :], sgm[:, c, :], ALU.mult).then_inc(S("yt_done"), 1)
            dve.wait_ge(S("g1_in"), 16)
            for n in range(6):
                t, h = divmod(n, 2)
                c = slice(h * 512, h * 512 + 512)
                dve.wait_ge(S("wo_ready"), n + 1)
                v(tt(xtmp[:, :], bank[4 + n % 4][:, :], g1rows[:, min(t, 1), c], ALU.mult))
                tt(X[:, t, c], X[:, t, c], xtmp[:, :], ALU.add).then_inc(S("x1_done"), 1)
                if n < 5:
                    dve.wait_ge(S("x1_done"), n + 1)
            dve.wait_ge(S("ab_in"), 32)
            dve.wait_ge(S("a2_done"), 1)
            for t in range(NT):
                dve.wait_ge(S("root2_done"), t + 1)
                v(V_.reciprocal(st[:, 6 + t:7 + t], st[:, 3 + t:4 + t]))
                v(stt(h2[:, t, :], X[:, t, :], st[:, 6 + t:7 + t], abrows[:, 0, min(t, 1), :], ALU.mult, ALU.mult))
                tt(h2[:, t, :], h2[:, t, :], abrows[:, 1, min(t, 1), :], ALU.add).then_inc(S("h2_done"), 1)

            flat = "p a b -> p (a b)"
            row16 = desc[:, :].unsqueeze(1).broadcast_to([P, NT, NE])
            row4 = desc[:, 12:16].unsqueeze(1).broadcast_to([P, NT, 4])
            dve.wait_ge(S("exp_done"), 1)
            dve.wait_ge(S("tri_done"), 1)
            v(ts(r1.rearrange(flat), r1.rearrange(flat), 1.0, None, ALU.add))
            v(V_.reciprocal(sig.rearrange(flat), r1.rearrange(flat)))
            v(tt(sel, sig, rbrow[:, :].unsqueeze(1).broadcast_to([P, NT, NE]), ALU.add))
            quad = sel.rearrange("p t (g e) -> p e t g", e=4)
            d(tt(g1, quad[:, 0], quad[:, 1], ALU.max))
            d(tt(g2, quad[:, 0], quad[:, 1], ALU.min))
            d(tt(g3, quad[:, 2], quad[:, 3], ALU.max))
            v(tt(g4, quad[:, 2], quad[:, 3], ALU.min))
            v(tt(g4, g2, g4, ALU.max))
            d(tt(g2, g1, g3, ALU.min))
            v(tt(g1, g1, g3, ALU.max))
            v(tt(g2, g2, g4, ALU.max))
            v(tt(g1, g1, g2, ALU.add))

            def first_max(o, x, n, prio, scratch):
                v(V_.tensor_reduce(q1[:, 0:NT], x, AX.X, ALU.max))
                v(tt(scratch, x, q1[:, 0:NT].unsqueeze(2).broadcast_to([P, NT, n]), ALU.is_equal))
                v(tt(scratch, scratch, prio, ALU.mult))
                v(V_.tensor_reduce(q1[:, 0:NT], scratch, AX.X, ALU.max))
                v(tt(o, scratch, q1[:, 0:NT].unsqueeze(2).broadcast_to([P, NT, n]), ALU.is_equal))

            first_max(g3, g1, 4, row4, g2)
            v(ts(g3, g3, BIG, -BIG, ALU.mult, ALU.add))
            v(tt(r1.rearrange("p t (g e) -> p (t g) e", e=4), sel.rearrange("p t (g e) -> p (t g) e", e=4),
                 g3.rearrange(flat).unsqueeze(2).broadcast_to([P, 12, 4]), ALU.add))
            first_max(oh1, r1, NE, row16, r2)
            v(stt(r1, oh1, -BIG, r1, ALU.mult, ALU.add))
            first_max(oh2, r1, NE, row16, r2)
            tt(mk, oh1, oh2, ALU.add).then_inc(S("mk_done"), 1)
            v(tt(r1, sig, oh1, ALU.mult))
            v(V_.tensor_reduce(q1[:, 0:NT], r1, AX.X, ALU.add))
            v(tt(r1, sig, oh2, ALU.mult))
            v(V_.tensor_reduce(q2[:, 0:NT], r1, AX.X, ALU.add))
            v(tt(q3[:, 0:NT], q1[:, 0:NT], q2[:, 0:NT], ALU.add))
            v(V_.reciprocal(st[:, 24:27], q3[:, 0:NT]))
            d(tt(wts[:, 0:3], q1[:, 0:NT], st[:, 24:27], ALU.mult))
            d(tt(wts[:, 3:6], q2[:, 0:NT], st[:, 24:27], ALU.mult))
            dve.wait_ge(S("ranks_ready"), 1)
            cnt, inc = r2[:, 0, :], r2[:, 1, :]
            v(cp(cnt, bank[5][:, 48:64]))
            v(V_.tensor_tensor_scan(inc, ones[:, 0:NE], cnt, 0.0, ALU.mult, ALU.add))
            v(tt(inc, inc, cnt, ALU.subtract))
            d(cp(n_i[:, :], cnt))
            v(cp(off_i[:, :], inc))
            dve.sem_inc(S("int_done"), 1)
            v(tt(r1, bank[5][:, 0:NT * NE].rearrange("p (t e) -> p t e", t=NT),
                 inc.unsqueeze(1).broadcast_to([P, NT, NE]), ALU.add))
            for o, c in ((oh1, 0), (oh2, 3)):
                v(tt(o, o, r1, ALU.mult))
                v(V_.tensor_reduce(q1[:, 0:NT], o, AX.X, ALU.add))
                v(cp(pos_u[:, c:c + 3], q1[:, 0:NT]))
            dve.sem_inc(S("routed"), 1)
            for n in range(1, 12, 2):
                dve.wait_ge(S("hs_ready"), n + 1)
                t, h = divmod(n, 2)
                cp(hTs[:, 4 * h:4 * h + 4, t * P:(t + 1) * P],
                   bank[n % 4][:, :].rearrange("p (a b) -> p a b", a=4)).then_inc(S("hs_copied_v"), 1)

            for f in FAM:
                dve.sem_inc(S(f"evac_v_{f}"), 1)

            def one_pass(f, e):
                for j in range(4):
                    dve.wait_ge(S(f"silu_done_{f}"), e * 4 + j + 1)
                    tt(actT[:, j, :], sg[:, j % 2, :], bank[j][:, P:2 * P], ALU.mult).then_inc(S(f"act_done_{f}"), 1)
                dve.wait_ge(S(f"down_ready_{f}"), e * 2 + 2)
                if f == "a":
                    for x in FAM:
                        dve.wait_ge(S(f"written_{x}"), (e + 1) * 16)
                else:
                    dve.wait_ge(S("written_a" if f == "b" else "written_b"), (e + 2) * 16)
                cp(ystage[:, 512:D], bank[5][:, :]).then_inc(S(f"evac_v_{f}"), 1)

            def expert(e):
                one_pass("a", e)
                for i, f in enumerate("bc"):
                    n = dve.value_load(n_i[0:1, bass.ds(e, 1)], min_val=0, max_val=NT * P)
                    with dve.If(n > P * (i + 1)):
                        one_pass(f, e)
                    with dve.Else():
                        dve.sem_inc(S(f"act_done_{f}"), 4)
                        dve.sem_inc(S(f"evac_v_{f}"), 1)

            with dve.Fori(0, NE) as e:
                expert(e)

            dve.wait_ge(S("g2_in"), 16)
            for t in range(NT):
                dve.wait_ge(S(f"picked_in{t}"), 32)
                y0, y1 = picked[:, t, 0, :], picked[:, t, 1, :]
                v(ts(y0, y0, wts[:, t:t + 1], None, ALU.mult))
                v(stt(y0, y1, wts[:, 3 + t:4 + t], y0, ALU.mult, ALU.add))
                v(tt(y0, y0, g2rows[:, min(t, 1), :], ALU.mult))
                tt(X[:, t, :], X[:, t, :], y0, ALU.add).then_inc(S("x2_done"), 1)
            dve.wait_ge(S("fnw_in"), 16)
            for t in range(NT):
                dve.wait_ge(S("root3_done"), t + 1)
                v(V_.reciprocal(st[:, 6 + t:7 + t], st[:, 3 + t:4 + t]))
                stt(X[:, t, :], X[:, t, :], st[:, 6 + t:7 + t], fnw[:, :], ALU.mult,
                    ALU.mult).then_inc(S("final_done"), 1)

        @block.gpsimd
        def _(pool):
            G = nc.gpsimd
            p = Steps(pool, S("pool_own"))

            def w(ins):
                p(ins)
                p.settle()

            for i in range(2):
                pool.dma_start(dtr[32 * i:32 * i + 32, 0:2],
                               io["ssm_log_dt"][0].rearrange("d (g t) -> (d g) t", t=2)).then_inc(S("dt_in"), 16)
            for i, name in enumerate(("ssm_a_re", "ssm_a_im", "state_ssm_re", "state_ssm_im")):
                src = io[name][0] if i < 2 else io[name][0, 0]
                pool.dma_start(arow[32 * i:32 * i + 32, :],
                               src.rearrange("d (g t) n -> (d g) (t n)", t=2)).then_inc(S("a_in"), 16)
            w(G.memset(ident[:, :], 0.0))
            G.affine_select(out=ident[:, :], in_=ident[:, :], compare_op=ALU.not_equal, fill=1.0, base=0,
                            pattern=[[-1, P]], channel_multiplier=1).then_inc(S("ident_ready"), 1)
            for t in range(CH):
                pool.dma_start(vrows[80:96, 32 * t:32 * t + 32],
                               io["ssm_d"][0].rearrange("(g h) -> g h", h=32)).then_inc(S("d_in"), 16)
            p(G.memset(BB[0], 0.0))
            p(G.memset(BB[1], 0.0))
            p(G.memset(Cbd, 0.0))
            w(G.memset(CA, 0.0))
            pool.sem_inc(S("zeros_done"), 1)
            G.memset(h1T[:, :, P:T0[1]], 0.0).then_inc(S("gap_done"), 1)
            pool.wait_ge(S("x_in"), 48)
            pool.wait_ge(S("v_init"), 1)
            for s in range(32):
                f, b = s, ROWS + LAT - 1 - s
                prev = V[:, f:b + 1:b - f, :].rearrange("p d (i g) -> p d i g", i=2)
                f, b = s + 1, ROWS + LAT - 2 - s
                nxt = V[:, f:b + 1:b - f, :].rearrange("p d (i g) -> p d i g", i=2)
                p(G.tensor_tensor(pt1, prev, Tre, ALU.mult))
                w(G.tensor_tensor(pt2[:, :, ::-1, :], prev, Tim, ALU.mult))
                w(G.tensor_tensor(nxt, nxt, pt1, ALU.add))
                last = G.tensor_tensor(nxt, nxt, pt2, ALU.add)
                if s < 31:
                    w(last)
            last.then_inc(S("ctx_states"), 1)
            pool.wait_ge(S("yg_done"), 3)
            pool.dma_start(router_w, io["router_w"].rearrange("(k p) n -> p k n", p=P)).then_inc(S("rw_in"), 16)
            pool.dma_start(rbrow, io["router_b"].partition_broadcast(P)).then_inc(S("rw_in"), 16)
            p(G.memset(ones[:, :], 1.0))
            w(G.memset(tri[:, :], 1.0))
            p(G.affine_select(out=tri[:, :], in_=tri[:, :], compare_op=ALU.is_gt, fill=0.0, base=0,
                              pattern=[[1, P]], channel_multiplier=-1))
            w(G.iota(desc_i, [[-1, NE]], base=NE, channel_multiplier=0))
            G.tensor_copy(desc[:, :], desc_i).then_inc(S("tri_done"), 1)
            pool.wait_ge(S("rw_in"), 32)
            pool.wait_ge(S("n2_in"), 16)
            pool.wait_ge(S("ab_in"), 32)
            w(G.tensor_scalar(abrows[:, 0], abrows[:, 0], 1.0, None, ALU.add))
            G.tensor_tensor(abrows[:, 0], abrows[:, 0], n2rows[:, :].unsqueeze(1).broadcast_to([P, 2, D]),
                            ALU.mult).then_inc(S("a2_done"), 1)
            pool.wait_ge(S("routed"), 1)
            for k in range(2):
                for t in range(NT):
                    pool.indirect_dma_start(
                        out=hsd, out_offset=bass.IndirectOffsetOnAxis(ap=pos_u[:, 3 * k + t:3 * k + t + 1], axis=0),
                        in_=h2[:, t, :], in_offset=None).then_inc(S("tok_sent"), 16)
            pool.dma_start(ysd[PAIRS:SORTED, :], h2[:, 0, :]).then_inc(S("tok_sent"), 16)
            G.memset(hTs[:, :, PAIRS:SORTED], 0.0).then_inc(S("pad_done"), 1)
            for f in FAM:
                pool.wait_ge(S(f"written_{f}"), 16 * (NE + 1))
            for t in range(NT):
                for k in range(2):
                    pool.indirect_dma_start(
                        out=picked[:, t, k, :], out_offset=None, in_=ysd,
                        in_offset=bass.IndirectOffsetOnAxis(ap=pos_u[:, 3 * k + t:3 * k + t + 1], axis=0)
                    ).then_inc(S(f"picked_in{t}"), 16)


IN_NAMES = ["x_prompt", "x_sample", "c", "state_ssm_re", "state_ssm_im", "c_ctx", "norm1_w", "norm2_w", "w_mod",
            "b_mod", "w_in", "ssm_a_re", "ssm_a_im", "ssm_log_dt", "ssm_b_re", "ssm_b_im", "ssm_c_re", "ssm_c_im",
            "ssm_d", "w_glu", "gmlp_ln_w", "gmlp_ln_b", "gmlp_w_s", "gmlp_b_s", "w_out", "router_w", "router_b",
            "w_gate", "w_up", "w_down", "final_norm_w"]
OUTS = [("out_p", (1, 128, 1024)), ("out_s", (1, 256, 1024)), ("out_re", (1, 1, 2, 32, 64)),
        ("out_im", (1, 1, 2, 32, 64))]


def kernel(**inputs):
    import concourse.bacc as bacc
    import numpy as np
    from concourse.bass_utils import run_bass_kernel_spmd

    nc = bacc.Bacc("TRN2", target_bir_lowering=False, num_devices=1)
    arrays, io = {}, {}
    for name in IN_NAMES:
        a = np.ascontiguousarray(inputs[name])
        arrays[f"in_{name}"] = a
        io[name] = nc.dram_tensor(f"in_{name}", a.shape, mybir.dt.from_np(a.dtype), kind="ExternalInput").ap()
    for name, shape in OUTS:
        io[name] = nc.dram_tensor(name, shape, F32, kind="ExternalOutput").ap()
    build(nc, io)
    r = run_bass_kernel_spmd(nc, [arrays], core_ids=[0])
    return tuple(r.results[0][name] for name, _ in OUTS)
```

```python
from contextlib import ExitStack

import concourse.bass as bass
from concourse import mybir

F32 = mybir.dt.float32
F32R = mybir.dt.float32r
I32 = mybir.dt.int32
U32 = mybir.dt.uint32
ALU = mybir.AluOpType
ACT = mybir.ActivationFunctionType
AX = mybir.AxisListType

P = 128
D = 1024
KD = D // P
DS = 512
NT = 3
CH = 4
NC = 97
TOK = NC * CH
T0 = [0, 132, 260]
GP = 16
Q = 2 * GP
ROWS = 98
LAT = 33
HEADS = 4
NE = 16
DE = 512
PAIRS = 2 * NT * P
SORTED = PAIRS + P
UNIT = 4096
EPS = 1e-6
PI = 3.141592653589793
BIG = 1.0e30


class Steps:

    def __init__(self, eng, sem):
        self.eng, self.sem, self.n = eng, sem, 0

    def __call__(self, ins):
        ins.then_inc(self.sem, 1)
        self.n += 1
        return self.n

    def settle(self, n=None):
        self.eng.wait_ge(self.sem, self.n if n is None else n)


def build(nc, io):
    ctx = ExitStack()
    with ctx:
        sems = {}

        def S(name):
            if name not in sems:
                sems[name] = ctx.enter_context(nc.semaphore(name))
            return sems[name]

        arena = ctx.enter_context(nc.sbuf_tensor("arena", [P, 9 * UNIT + 16128], F32))
        arena_base = nc.sbuf_base - (9 * UNIT + 16128) * 4
        n_i = ctx.enter_context(nc.sbuf_tensor("n_i", [P, NE], I32))
        off_i = ctx.enter_context(nc.sbuf_tensor("off_i", [P, NE], I32))
        pos_u = ctx.enter_context(nc.sbuf_tensor("pos_u", [P, 8], U32))
        wts = ctx.enter_context(nc.sbuf_tensor("wts", [P, 8], F32))
        psum = ctx.enter_context(nc.psum_tensor("psum", [P, 8, 512], F32))
        bank = [psum[:, i, :] for i in range(8)]

        def view(off, *dims):
            n = 1
            for x in dims:
                n *= x
            v = arena[:, off:off + n]
            if len(dims) == 2:
                v = v.rearrange("p (a b) -> p a b", a=dims[0])
            if len(dims) == 3:
                v = v.rearrange("p (a b c) -> p a b c", a=dims[0], b=dims[1])
            if len(dims) == 4:
                v = v.rearrange("p (a b c d) -> p a b c d", a=dims[0], b=dims[1], c=dims[2])
            return v

        def slot(s):
            return s * UNIT

        F = 9 * UNIT
        X = view(F, NT, D)
        h1T = view(F + 3072, KD, TOK)
        yT = h1T
        U = view(F + 6176, GP, NC)
        L = view(F + 7728, GP, P)
        wglu = view(F + 9776, 4, DS)
        ugT = view(F + 11824, HEADS, TOK)
        vn = view(F + 13376, NT, DS)
        gT = view(F + 13376, 4, TOK)
        xn = view(F + 11824, NT, D)
        BT = view(slot(7), 2, Q, 16)
        Bb = view(slot(7) + 1024, 2, Q, 16)
        Cbd = view(slot(8) + 2048, 2, Q, 32)
        CA = view(slot(3), 2, Q, P)
        BB = [view(slot(5), Q, P), view(slot(2), Q, P)]
        rawB = arena[0:64, slot(6):slot(6) + 2048]
        rawC = arena[0:64, F + 7728:F + 7728 + 2048]
        CT = view(F + 9776, 2, Q, 16)
        prod1 = view(F + 10800, Q, 16)
        prod2 = view(F + 11312, Q, 16)
        Bt = view(slot(7), 2, Q, P)
        V = view(slot(5), 2 * ROWS, 32)
        prm = slot(6) + 2176
        lnw = view(prm, DS)
        lnb = view(prm + 512, DS)
        bsr = view(prm + 1024, HEADS, P)
        wsraw = view(slot(2), HEADS, P)
        wsT = view(slot(2) + 512, HEADS, P)
        wout = [view(slot(7), KD, 512), view(slot(8), KD, 512)]
        g1rows = view(F + 6176, 2, D)
        abrows = view(F + 9776, 2, 2, D)
        mrow1 = arena[0:2, slot(8):slot(8) + 2048]
        n2rows = view(F + 13872, D)
        mrow = arena[0:2, slot(2) + 1024:slot(2) + 4096]
        g2rows = view(slot(0), 2, D)
        h2 = view(slot(6), NT, D)
        h2T = view(F + 3072, KD, NT * P)
        hsr = view(slot(7), 6, D)
        sg = view(F + 13312, DE)
        hidden = view(F + 13824, DE)
        ystage = view(F + 13824, D)
        picked = view(slot(3), NT, 2, D)
        fnw = view(slot(1), D)

        def split_pair(name, off, *dims):
            n = 1
            for x in dims:
                n *= x
            return [nc.alloc_sbuf_tensor_at(f"{name}_{part}", [P, *dims], F32R, offset=arena_base + 4 * (off + i * n))
                    for i, part in enumerate(("hi", "lo"))]

        def overlay(name, off, *dims):
            return nc.alloc_sbuf_tensor_at(name, [P, *dims], F32, offset=arena_base + 4 * off)

        raw = {"gate": overlay("gate_raw", slot(0), KD, DE), "up": overlay("up_raw", slot(1), KD, DE),
               "down": overlay("down_raw", slot(2), 4, D)}
        hTs = overlay("sorted_rows", F + 3072, KD, SORTED)
        wsplit = {"gate": split_pair("gate", slot(3), KD, DE), "up": split_pair("up", slot(5), KD, DE),
                  "down": split_pair("down", slot(7), 4, D)}
        xs = split_pair("x", F + 10240, KD, P)
        hs = split_pair("hidden", F + 12288, 4, P)

        cur = [F + 14928]

        def small(*dims):
            n = 1
            for x in dims:
                n *= x
            v = view(cur[0], *dims)
            cur[0] += n
            assert cur[0] <= F + 16128
            return v

        ident = small(P)
        vecT = small(P)
        sil = small(KD, 2)
        modT = small(2, 2, KD)
        aff1 = small(2, KD)
        Tre = small(2, 2, GP)
        Tim = small(2, 2, GP)
        dt1, dt2 = small(2, 2, GP), small(2, 2, GP)
        pt1, pt2 = small(2, 2, GP), small(2, 2, GP)
        st = small(32)
        fin = small(2, Q)

        epsc = small(1)
        warm = small(3)
        bnst, bnag = small(6), small(6)

        pc = [prm]

        def temp(*dims):
            n = 1
            for x in dims:
                n *= x
            v = view(pc[0], *dims)
            pc[0] += n
            assert pc[0] <= slot(7)
            return v

        arow = temp(P)
        adrow = temp(P)
        dtr = temp(4)
        acol = temp(4, Q)
        adcol = temp(2, Q)
        tp = [temp(Q) for _ in range(8)]
        sincos_in = view(pc[0] - 7 * Q, 2 * Q)
        sincos_out = view(pc[0] - 5 * Q, 2 * Q)
        pw = temp(5, 2, Q)
        pwB = temp(2, 4, Q)
        pwC = temp(2, 4, Q)
        s0c = small(2, Q)
        statesT = small(P)
        vrows = view(slot(6) + 2048, P)

        hsd = nc.dram_tensor("sorted_tokens", (SORTED, D), F32, kind="Internal").ap()
        modd = nc.dram_tensor("modulation_rows", (6, 2, D), F32, kind="Internal").ap()
        ysd = nc.dram_tensor("sorted_outputs", (SORTED, D), F32, kind="Internal").ap()
        w_mod = io["w_mod"][0].rearrange("(k p) n -> p k n", p=P)
        w_in = io["w_in"][0].rearrange("(k p) n -> p k n", p=P)
        w_out = io["w_out"][0].rearrange("(k p) n -> p k n", p=P)
        wg = io["w_gate"][0].rearrange("e (k p) n -> p e k n", p=P)
        wu = io["w_up"][0].rearrange("e (k p) n -> p e k n", p=P)
        wd = io["w_down"][0].rearrange("e (k p) n -> p e k n", p=P)

        def mod_half(m, h):
            return ("mod", 2 * m + h, w_mod[:, :, m * D + h * 512:m * D + h * 512 + 512])

        def in_part(n):
            return ("in", n, w_in[:, :, n * 512:n * 512 + 512])

        units = [mod_half(0, 0), mod_half(0, 1), mod_half(1, 0), mod_half(1, 1), in_part(0), in_part(1), in_part(2)] \
            + [mod_half(m, h) for m in (2, 4, 3, 5) for h in range(2)]
        RING = 2
        NPRE = 13
        def chunk_dst(t, b):
            return U[32 * t:32 * t + 32, b:GP:4, :]

        def chunk_src(t, b):
            return psum[32 * b:32 * b + 32, 0:4, 0:TOK].rearrange("p c (j t) -> p t c j", t=CH)[:, t, :, :]

        router_w = view(slot(6) + 3840, KD, NE)
        rbrow = view(slot(6) + 3968, NE)
        rc = [slot(6) + 3072]

        def rtemp(*dims):
            n = 1
            for x in dims:
                n *= x
            v = view(rc[0], *dims)
            rc[0] += n
            assert rc[0] <= slot(6) + 3840
            return v

        tri = rtemp(P)
        ones = rtemp(P)
        desc = rtemp(NE)
        sig, sel, r1, r2, mk, oh1, oh2 = (rtemp(NT, NE) for _ in range(7))
        g1, g2, g3, g4 = (rtemp(NT, 4) for _ in range(4))
        q1, q2, q3 = rtemp(4), rtemp(4), rtemp(4)
        desc_i = rtemp(NE).bitcast(I32)
        sgm = view(slot(6), 4, TOK)
        xtmp = view(F + 6176 + 2048, 512)
        def fam(p):
            return "first" if p == 0 else "more"

        def nth(p, e):
            return e if p == 0 else e * 2 + p - 1

        def before(p, e):
            return ([("first", e + 1), ("more", e * 2 + 1)], [("first", e + 2)], [("more", e * 2 + 2)])[p]


        block = ctx.enter_context(nc.Block())


        @block.sync
        def _(sp):
            def prologue_unit(i):
                if i >= RING:
                    sp.wait_ge(S("unit_used"), i - RING + 1)
                sp.dma_start(view(slot(i % RING), KD, 512), units[i][2]).then_inc(S(f"unit_in{i % RING}"), 16)

            sp.wait_ge(S("vec_in"), 5 * 16)
            prologue_unit(0)
            for i, name in enumerate(("ssm_b_re", "ssm_b_im")):
                sp.dma_start(rawB[32 * i:32 * i + 32, :],
                             io[name][0].rearrange("d (g t) n h -> (d g) (t n h)", t=2)).then_inc(S("b_in"), 16)
            prologue_unit(1)
            for i, name in enumerate(("ssm_c_re", "ssm_c_im")):
                for g in range(2):
                    sp.dma_start(rawC[32 * i:32 * i + 32, :].rearrange("q (h t n) -> q t h n", h=16, t=2)[:, g],
                                 io[name][0].rearrange("d (g t) h n -> (d g) t h n", t=2)[:, g]
                                 ).then_inc(S("c_in"), 16)
            for i in range(2, 7):
                prologue_unit(i)
            sp.wait_ge(S("params_done"), 1)
            sp.dma_start(wglu, io["w_glu"][0].rearrange("(k p) n -> p k n", p=P)).then_inc(S("wglu_in"), 16)
            sp.dma_start(lnw, io["gmlp_ln_w"][0].partition_broadcast(P)).then_inc(S("ln_in"), 16)
            sp.dma_start(lnb, io["gmlp_ln_b"][0].partition_broadcast(P)).then_inc(S("ln_in"), 16)
            sp.dma_start(bsr, io["gmlp_b_s"][0].partition_broadcast(P)).then_inc(S("ln_in"), 16)
            sp.wait_ge(S("bt_ready"), 16)
            sp.dma_start(wsraw, io["gmlp_w_s"][0].rearrange("h p q -> p h q")).then_inc(S("ws_in"), 16)
            prologue_unit(7)
            prologue_unit(8)
            sp.wait_ge(S("v_ready"), 16)
            for h in range(2):
                sp.dma_start(wout[h], w_out[:, :, h * 512:h * 512 + 512]).then_inc(S("wout_in"), 16)
            for i in range(9, 15):
                prologue_unit(i)

            def load(name, e):
                w = {"gate": wg, "up": wu, "down": wd}[name]
                c = raw[name].shape[1] // 2
                for half in range(2):
                    if not isinstance(e, int) or e > 0:
                        sp.wait_ge(S(f"{name}_lo"), (e - 1) * 2 + half + 1)
                    k = slice(half * c, (half + 1) * c)
                    src = w[:, e, k, :] if isinstance(e, int) else \
                        w[:, bass.ds(e, 1), k, :].rearrange("p o k n -> p (o k) n")
                    sp.dma_start(raw[name][:, k, :], src).then_inc(S(f"{name}_in{half}"), 16)

            sp.wait_ge(S("y_ready"), 4)
            sp.wait_ge(S("modd_in2"), 16)
            sp.dma_start(g1rows.rearrange("p a b -> p (a b)"),
                         modd[2].rearrange("s d -> (s d)").partition_broadcast(P)).then_inc(S("g1_in"), 16)
            sp.wait_ge(S("yt_done"), 4)
            sp.dma_start(n2rows, io["norm2_w"][0].partition_broadcast(P)).then_inc(S("n2_in"), 16)
            for i, m in enumerate((4, 3)):
                sp.wait_ge(S(f"modd_in{m}"), 16)
                sp.dma_start(abrows[:, i].rearrange("p a b -> p (a b)"),
                             modd[m].rearrange("s d -> (s d)").partition_broadcast(P)).then_inc(S("ab_in"), 16)
            sp.wait_ge(S("unit_used"), 15)
            load("up", 0)
            load("gate", 0)
            for t in range(6):
                if t == 0:
                    sp.wait_ge(S("tok_sent"), 16 * 6)
                sp.dma_start(hsr[:, t, :], hsd[t * P:(t + 1) * P, :]).then_inc(S(f"hs_in{t}"), 16)
            sp.wait_ge(S("modd_in5"), 16)
            load("down", 0)
            load("gate", 1)
            with sp.Fori(1, NE - 1) as e:
                load("up", e)
                load("down", e)
                load("gate", e + 1)
            load("up", NE - 1)
            load("down", NE - 1)
            sp.wait_ge(S("gate_lo"), 2 * NE)
            sp.dma_start(g2rows.rearrange("p a b -> p (a b)"),
                         modd[5].rearrange("s d -> (s d)").partition_broadcast(P)).then_inc(S("g2_in"), 16)
            sp.wait_ge(S("up_lo"), 2 * NE)
            sp.dma_start(fnw, io["final_norm_w"].partition_broadcast(P)).then_inc(S("fnw_in"), 16)
            sp.wait_ge(S("states_copied"), 1)
            for ri, name in enumerate(("out_re", "out_im")):
                dst = io[name].rearrange("a b d (g t) n -> (a b d g) (t n)", t=2)
                sp.dma_start(dst, statesT[32 * ri:32 * ri + 32, :]).then_inc(S("out_done"), 16)
            for t in range(NT):
                sp.wait_ge(S("final_done"), t + 1)
                dst = io["out_p"][0] if t == 0 else io["out_s"][0, (t - 1) * P:t * P, :]
                sp.dma_start(dst, X[:, t, :]).then_inc(S("out_done"), 16)
            sp.wait_ge(S("out_done"), 16 * 5)

        @block.tensor
        def _(pe):
            mm, tr = nc.tensor.matmul, nc.tensor.transpose
            pe.wait_ge(S("ident_ready"), 1)
            pe.wait_ge(S("vec_in"), 5 * 16)
            pe.wait_ge(S("d_in"), 4 * 16)
            tr(bank[7][:, 0:96], vrows[0:96, :], ident[0:96, 0:96]).then_inc(S("vec_ready"), 1)
            pe.wait_ge(S("a_in"), 4 * 16)
            tr(bank[6][:, 0:P], arow[:, :], ident[:, :])
            pe.wait_ge(S("adt_done"), 1)
            tr(bank[6][:, P:P + 64], adrow[0:64, :], ident[0:64, 0:64]).then_inc(S("acol_ready"), 1)

            def unit_wait(i):
                pe.wait_ge(S(f"unit_in{i % RING}"), 16 * (i // RING + 1))
                return view(slot(i % RING), KD, 512)

            def modulation(i, b, bias):
                w = unit_wait(i)
                out = bank[b][0:2, :]
                for k in range(KD):
                    last = mm(out, sil[:, k, :], w[:, k, :], start=(k == 0), stop=(k == KD - 1 and not bias))
                if bias:
                    last.then_inc(S("unit_used"), 1)
                    for kk in range(4):
                        c = 32 + 4 * units[i][1] + kk
                        last = mm(out[:, kk * P:(kk + 1) * P], vecT[:, c:c + 1].broadcast_to([P, 2]), ident[:, :],
                                  start=False, stop=(kk == 3))
                return last

            pe.wait_ge(S("sil_ready"), 1)
            pe.wait_ge(S("small_copied"), 1)
            modulation(0, 4, False).then_inc(S("unit_used"), 1)
            modulation(1, 7, False).then_inc(S("unit_used"), 1)
            pe.wait_ge(S("b_in"), 32)
            for h in range(16):
                last = tr(bank[h // 8][:, (h % 8) * 64:(h % 8) * 64 + 64],
                          rawB.rearrange("q (n h) -> q h n", h=16)[:, h, :], ident[0:64, 0:64])
            last.then_inc(S("bt_raw_ready"), 1)
            pe.wait_ge(S("mrow_done"), 1)
            modulation(2, 4, False).then_inc(S("unit_used"), 1)
            pe.wait_ge(S("c_in"), 64)
            for h in range(16):
                last = tr(bank[2 + h // 8][:, (h % 8) * 64:(h % 8) * 64 + 64],
                          rawC[:, h * P:(h + 1) * P], ident[0:64, 0:64])
            last.then_inc(S("ct_raw_ready"), 1)
            pe.wait_ge(S("mrow_done"), 2)
            modulation(3, 7, False).then_inc(S("unit_used"), 1)
            pe.wait_ge(S("mrow_done"), 4)
            for i in range(16):
                last = tr(bank[5][:, 2 * i:2 * i + 2], mrow1[0:2, i * P:(i + 1) * P], ident[0:2, 0:2])
            last.then_inc(S("mod_a_ready"), 1)

            pe.wait_ge(S("xn_done"), 3)
            for k in range(KD):
                if k == 1:
                    pe.wait_ge(S("mod_a_copied"), 1)
                if k >= 2:
                    pe.wait_ge(S("h1_done"), k - 1)
                for t in range(NT):
                    last = tr(bank[4 + k % 2][:, T0[t]:T0[t] + P], xn[:, t, k * P:(k + 1) * P], ident[:, :])
                last.then_inc(S("xt_ready"), 1)

            def z_columns(w, c, out):
                for k in range(KD):
                    last = mm(out, w[:, k, c * P:(c + 1) * P], h1T[:, k, :], start=(k == 0), stop=(k == KD - 1))
                return last

            pe.wait_ge(S("h1_done"), KD)
            pe.wait_ge(S("gap_done"), 1)
            w = unit_wait(4)
            for c in range(4):
                pe.wait_ge(S("raw_copied"), 2)
                last = z_columns(w, c, bank[c][:, 0:TOK])
            last.then_inc(S("unit_used"), 1)
            pe.wait_ge(S("bb_done"), 1)
            pe.wait_ge(S("small_copied"), 2)
            for q in range(Q):
                out = bank[6 + q // 16][:, (q % 16) * 32:(q % 16) * 32 + 32]
                mm(out, BB[0][:, q, :], Cbd[:, 0, q, :], start=True, stop=False)
                last = mm(out, BB[1][:, q, :], Cbd[:, 1, q, :], start=False, stop=True)
            last.then_inc(S("lk_ready"), 1)
            pe.wait_ge(S("u_done_a"), 1)
            pe.wait_ge(S("u_done_v"), 1)
            for n in range(16):
                if n >= 4:
                    pe.wait_ge(S("bt_copied"), n - 3)
                for j in range(4):
                    ri, q = divmod(4 * n + j, Q)
                    last = tr(bank[n % 4][:, j * P:(j + 1) * P], BB[ri][:, q, :], ident[:, :])
                last.then_inc(S("bt_ready"), 1)
            pe.wait_ge(S("bt_copied"), 16)
            for n in range(16):
                if n >= 4:
                    pe.wait_ge(S("v_copied"), n - 3)
                for ri in range(2):
                    for j in range(2):
                        q = 2 * n + j
                        c = (2 * ri + j) * NC
                        last = mm(bank[n % 4][:, c:c + NC], Bt[:, ri, q, :], U[:, q % GP, :], start=True, stop=True)
                last.then_inc(S("v_ready"), 1)

            w = unit_wait(5)
            for c in range(4):
                if c >= 2:
                    pe.wait_ge(S("ug_done"), c - 1)
                last = z_columns(w, c, bank[4 + c % 2][:, 0:TOK])
                last.then_inc(S("zu_ready") if c < 3 else S("unit_used"), 1)
            w = unit_wait(6)
            pe.wait_ge(S("lk_copied"), 1)
            for t in range(NT):
                b = (7, 4, 5)[t]
                if t > 0:
                    pe.wait_ge(S("ug_done"), t + 2)
                for k in range(KD):
                    last = mm(bank[b][:, :], h1T[:, k, T0[t]:T0[t] + P], w[:, k, :],
                              start=(k == 0), stop=(k == KD - 1))
                last.then_inc(S("zv_ready") if t < 2 else S("unit_used"), 1)
            pe.wait_ge(S("v_copied"), 16)
            for i in range(7, NPRE):
                if i >= 9:
                    pe.wait_ge(S("mrow_done"), i - 4)
                modulation(i, (i + 1) % 2, True).then_inc(S("mrow_ready"), 1)
            pe.wait_ge(S("ws_in"), 16)
            pe.wait_ge(S("vg_done"), 2)
            for h in range(HEADS):
                last = tr(bank[4][:, h * P:(h + 1) * P], wsraw[:, h, :], ident[:, :])
            last.then_inc(S("ws_ready"), 1)
            pe.wait_ge(S("ws_copied"), 1)
            pe.wait_ge(S("vg_done"), 3)
            for t in range(NT):
                pe.wait_ge(S("vn_done"), t + 1)
                b = (7, 5, 6)[t]
                for h in range(HEADS):
                    last = mm(bank[b][:, h * P:(h + 1) * P], vn[:, t, h * P:(h + 1) * P], wsT[:, h, :],
                              start=True, stop=True)
                last.then_inc(S("spatial_ready"), 1)

            pe.wait_ge(S("mrow_done"), NPRE - 3)
            pe.wait_ge(S("lat_states"), 1)
            pe.wait_ge(S("ctx_states"), 1)
            for b in range(4):
                for c in range(4):
                    gp = 4 * c + b
                    out = bank[b][:, c * NC:(c + 1) * NC]
                    mm(out, L[:, gp, :], U[:, gp, :], start=True, stop=False)
                    for d in range(2):
                        for ri in range(2):
                            last = mm(out, CA[:, ri, d * GP + gp, :],
                                      V[:, d * ROWS + d:d * ROWS + d + NC, ri * GP + gp],
                                      start=False, stop=(d == 1 and ri == 1))
                last.then_inc(S("y_ready"), 1)
            pe.wait_ge(S("fin_done"), 1)
            tr(bank[4][0:64, 0:P], fin.rearrange("p a b -> p (a b)"), ident[:, :]).then_inc(S("states_ready"), 1)

            pe.wait_ge(S("wglu_in"), 16)
            pe.wait_ge(S("g_done"), 16)
            for c in range(4):
                for k in range(4):
                    last = mm(bank[c][:, 0:TOK], wglu[:, k, c * P:(c + 1) * P], gT[:, k, :],
                              start=(k == 0), stop=(k == 3))
                last.then_inc(S("glu_ready"), 1)
            pe.wait_ge(S("yt_done"), 4)
            pe.wait_ge(S("wout_in"), 32)
            for n in range(6):
                if n == 0:
                    pe.wait_ge(S("yg_done"), 3)
                    pe.wait_ge(S("states_copied"), 1)
                if n >= 4:
                    pe.wait_ge(S("x1_done"), n - 3)
                t, h = divmod(n, 2)
                for k in range(KD):
                    last = mm(bank[4 + n % 4][:, :], yT[:, k, T0[t]:T0[t] + P], wout[h][:, k, :],
                              start=(k == 0), stop=(k == KD - 1))
                last.then_inc(S("wo_ready"), 1)
            pe.wait_ge(S("x1_done"), 3)
            modulation(13, 6, True).then_inc(S("mrow_ready"), 1)
            for n in range(6):
                t, h = divmod(n, 2)
                pe.wait_ge(S("h2_done"), t + 1)
                if n >= 4:
                    pe.wait_ge(S("h2t_copied"), n - 3)
                for kk in range(4):
                    k = 4 * h + kk
                    last = tr(bank[n % 4][:, kk * P:(kk + 1) * P], h2[:, t, k * P:(k + 1) * P], ident[:, :])
                last.then_inc(S("h2t_ready"), 1)
            pe.wait_ge(S("h2t_copied"), 6)
            pe.wait_ge(S("x1_done"), 6)
            pe.wait_ge(S("rw_in"), 32)
            for t in range(NT):
                for k in range(KD):
                    last = mm(bank[4][:, t * NE:(t + 1) * NE], h2T[:, k, t * P:(t + 1) * P], router_w[:, k, :],
                              start=(k == 0), stop=(k == KD - 1))
            last.then_inc(S("logits_ready"), 1)
            modulation(14, 7, True).then_inc(S("mrow_ready"), 1)
            pe.wait_ge(S("mk_done"), 1)
            pe.wait_ge(S("tri_done"), 1)
            for t in range(NT):
                mm(bank[5][:, t * NE:(t + 1) * NE], tri[:, :], mk[:, t, :], start=True, stop=(t == 0))
                for s in range(t):
                    mm(bank[5][:, t * NE:(t + 1) * NE], ones[:, :], mk[:, s, :], start=False, stop=(s == t - 1))
            for s in range(NT):
                last = mm(bank[5][:, 48:64], ones[:, :], mk[:, s, :], start=(s == 0), stop=(s == NT - 1))
            last.then_inc(S("ranks_ready"), 1)

            for n in range(12):
                t, h = divmod(n, 2)
                pe.wait_ge(S(f"hs_in{t}"), 16)
                if n >= 4:
                    pe.wait_ge(S("hs_copied_a") if n % 2 == 0 else S("hs_copied_v"), (n - 4) // 2 + 1)
                for kk in range(4):
                    k = 4 * h + kk
                    last = tr(bank[n % 4][:, kk * P:(kk + 1) * P], hsr[:, t, k * P:(k + 1) * P], ident[:, :])
                last.then_inc(S("hs_ready"), 1)
            pe.wait_ge(S("hs_copied_a"), 6)
            pe.wait_ge(S("hs_copied_v"), 6)
            pe.wait_ge(S("int_done"), 1)
            for f in ("first", "more"):
                pe.sem_inc(S(f"down_done_{f}"), 1)

            def split_product(out, x, w, k, c, first, last):
                mm(out, x[0][:, k, :], w[0][:, k, c], start=first, stop=False)
                mm(out, x[0][:, k, :], w[1][:, k, c], start=False, stop=False)
                return mm(out, x[1][:, k, :], w[0][:, k, c], start=False, stop=last)

            def one_pass(p, e):
                f, i = fam(p), nth(p, e)
                pe.wait_ge(S(f"x_lo_{f}"), i + 1)
                for k in range(KD):
                    if p == 0 and k % 4 == 0:
                        pe.wait_ge(S("gate_lo"), e * 2 + k // 4 + 1)
                    last = split_product(bank[0][:, :], xs, wsplit["gate"], k, slice(0, DE), k == 0, k == KD - 1)
                last.then_inc(S(f"gate_done_{f}"), 1)
                for k in range(KD):
                    if p == 0 and k % 4 == 0:
                        pe.wait_ge(S("up_lo"), e * 2 + k // 4 + 1)
                    last = split_product(bank[1][:, :], xs, wsplit["up"], k, slice(0, DE), k == 0, k == KD - 1)
                last.then_inc(S(f"up_done_{f}"), 1)
                for half in range(2):
                    pe.wait_ge(S(f"mul_done_{f}"), i * 2 + half + 1)
                    for j in range(2):
                        c = (2 * half + j) * P
                        last = tr(bank[2 + half][:, j * P:(j + 1) * P], hidden[:, c:c + P], ident[:, :])
                    last.then_inc(S(f"tr_done_{f}"), 1)
                for x, count in before(p, e):
                    pe.wait_ge(S(f"evac_{x}"), count)
                for j in range(4):
                    if j % 2 == 0:
                        pe.wait_ge(S(f"h_lo_{f}"), i * 2 + j // 2 + 1)
                    if p == 0 and j % 2 == 0:
                        pe.wait_ge(S("down_lo"), e * 2 + j // 2 + 1)
                    for h in range(2):
                        last = split_product(bank[4 + h][:, :], hs, wsplit["down"], j,
                                             slice(h * 512, h * 512 + 512), j == 0, j == 3)
                last.then_inc(S(f"down_done_{f}"), 1)

            def skipped(f):
                pe.sem_inc(S(f"gate_done_{f}"), 1)
                pe.sem_inc(S(f"up_done_{f}"), 1)
                pe.sem_inc(S(f"tr_done_{f}"), 2)
                pe.sem_inc(S(f"down_done_{f}"), 1)

            with pe.Fori(0, NE) as e:
                n = pe.value_load(n_i[0:1, bass.ds(e, 1)], min_val=0, max_val=NT * P)
                one_pass(0, e)
                for p in (1, 2):
                    with pe.If(n > P * p):
                        one_pass(p, e)
                    with pe.Else():
                        if p == 2:
                            pe.wait_ge(S("down_done_more"), e * 2 + 2)
                        skipped("more")

        @block.scalar
        def _(act):
            A = nc.scalar.activation
            a = Steps(act, S("act_own"))
            for r0, src in ((0, io["c_ctx"].rearrange("(k p) -> k p", p=P)),
                            (8, io["c"][0].rearrange("(k p) -> k p", p=P)),
                            (16, io["norm1_w"][0].rearrange("(k p) -> k p", p=P)),
                            (24, io["norm2_w"][0].rearrange("(k p) -> k p", p=P)),
                            (32, io["b_mod"][0].rearrange("(k p) -> k p", p=P))):
                act.dma_start(vrows[r0:r0 + src.shape[0], :], src).then_inc(S("vec_in"), 16)
            for t in range(NT):
                src = io["x_prompt"][0] if t == 0 else io["x_sample"][0, (t - 1) * P:t * P, :]
                act.dma_start(X[:, t, :], src).then_inc(S("x_in"), 16)
            act.wait_ge(S("dt_in"), 32)
            A(dtr[0:64, 0:2], dtr[0:64, 0:2], ACT.Exp).then_inc(S("dt_ready"), 1)
            act.wait_ge(S("small_copied"), 1)
            A(sil.rearrange("p k s -> p s k"), vecT[:, 0:16].rearrange("p (s k) -> p s k", s=2),
              ACT.Silu).then_inc(S("sil_ready"), 1)
            act.wait_ge(S("phase_done"), 1)
            A(tp[5][:, :], adcol[:, 0, :], ACT.Exp).then_inc(S("trig_done"), 1)
            A(sincos_out, sincos_in, ACT.Sin).then_inc(S("trig_done"), 1)

            def first_rows(i):
                act.wait_ge(S("unit_used"), i + 1)
                A(mrow1[:, i * 512:(i + 1) * 512], bank[(4, 7)[i % 2]][0:2, :], ACT.Copy).then_inc(S("mrow_done"), 1)

            act.wait_ge(S("x_in"), 48)
            for t in range(NT):
                n = a(A(xn[:, t, :], X[:, t, :], ACT.Square, accum_out=st[:, t:t + 1]))
            a.settle()
            A(st[:, 3:6], st[:, 0:3], ACT.Sqrt, bias=epsc[:, 0:1], scale=1.0 / D).then_inc(S("root_done"), 1)
            act.wait_ge(S("rstd_done"), 1)
            for t in range(NT):
                A(xn[:, t, :], X[:, t, :], ACT.Copy, scale=st[:, 6 + t:7 + t]).then_inc(S("xn_done"), 1)
            for i in range(4):
                first_rows(i)
            act.wait_ge(S("aff1_done"), 1)
            for k in range(KD):
                act.wait_ge(S("xt_ready"), k + 1)
                b = bank[4 + k % 2]
                A(h1T[:, k, 0:P], b[:, 0:P], ACT.Identity, bias=modT[:, 0, 0, k:k + 1], scale=aff1[:, 0, k:k + 1])
                A(h1T[:, k, T0[1]:TOK], b[:, T0[1]:TOK], ACT.Identity, bias=modT[:, 0, 1, k:k + 1],
                  scale=aff1[:, 1, k:k + 1]).then_inc(S("h1_done"), 1)
            act.wait_ge(S("unit_used"), 5)
            for b in range(2):
                for t in range(CH):
                    last = A(chunk_dst(t, b), chunk_src(t, b), ACT.Copy)
            last.then_inc(S("u_done_a"), 1)
            act.wait_ge(S("lk_ready"), 1)
            for to in range(CH):
                for ti in range(CH):
                    o = L[32 * ti:32 * ti + 32, :, 32 * to:32 * to + 32]
                    b, s = (6, ti + 3 - to) if ti <= to else (7, ti - to)
                    last = A(o, bank[b][32 * s:32 * s + 32, :].rearrange("p (a b) -> p a b", a=GP), ACT.Copy)
            last.then_inc(S("l_gathered"), 1)
            Vr = V.rearrange("p (d r) (i g) -> p d i g r", d=2, i=2)
            for n in range(16):
                act.wait_ge(S("v_ready"), n + 1)
                dr, g0 = (2 * n) // GP, (2 * n) % GP
                for ri in range(2):
                    last = A(Vr[:, dr, ri, g0:g0 + 2, 1 - dr:1 - dr + NC],
                             bank[n % 4][:, 2 * ri * NC:2 * ri * NC + 2 * NC].rearrange("p (g j) -> p g j", g=2),
                             ACT.Copy)
                last.then_inc(S("v_copied"), 1)
            for c in range(4):
                act.wait_ge(S("zu_ready") if c < 3 else S("unit_used"), c + 1 if c < 3 else 6)
                A(ugT[:, c, :], bank[4 + c % 2][:, 0:TOK], ACT.Gelu_apprx_tanh).then_inc(S("ug_done"), 1)
            for t in range(NT):
                act.wait_ge(S("zv_ready") if t < 2 else S("unit_used"), t + 1 if t < 2 else 7)
                A(vn[:, t, :], bank[(7, 4, 5)[t]][:, :], ACT.Gelu_apprx_tanh).then_inc(S("vg_done"), 1)

            def ln_root():
                act.wait_ge(S("ln_var"), 1)
                A(st[:, 16:19], st[:, 12:15], ACT.Sqrt, bias=epsc[:, 0:1]).then_inc(S("ln_root"), 1)

            def row_half(i):
                m = (2, 4, 3, 5)[i // 2]
                c = (i // 2) % 3 * D + (i % 2) * 512
                if i == 6:
                    act.wait_ge(S("modd_in2"), 16)
                act.wait_ge(S("mrow_ready"), i + 1)
                b = i % 2 if i < NPRE - 7 else i
                A(mrow[:, c:c + 512], bank[b][0:2, :], ACT.Copy).then_inc(S("mrow_done"), 1)
                if i % 2 == 1:
                    act.wait_ge(S("mrow_done"), i + 5)
                    act.dma_start(modd[m], mrow[:, c - 512:c + 512]).then_inc(S(f"modd_in{m}"), 16)

            for i in range(NPRE - 7):
                if i == 2:
                    ln_root()
                row_half(i)
            act.wait_ge(S("spatial_ready"), 3)
            for b in range(4):
                act.wait_ge(S("y_ready"), b + 1)
                for t in range(CH):
                    A(gT[32 * b:32 * b + 32, :, :].rearrange("p c (j t) -> p t c j", t=CH)[:, t, :, :],
                      bank[b][32 * t:32 * t + 32, 0:4 * NC].rearrange("p (c j) -> p c j", c=4),
                      ACT.Gelu_apprx_tanh).then_inc(S("g_done"), 1)
            for c in range(4):
                act.wait_ge(S("glu_ready"), c + 1)
                A(sgm[:, c, :], bank[c][:, 0:TOK], ACT.Sigmoid).then_inc(S("sgm_done"), 1)
            for t in range(NT):
                act.wait_ge(S("x1_done"), 2 * t + 2)
                a(A(h2[:, t, :], X[:, t, :], ACT.Square, accum_out=st[:, t:t + 1]))
                a.settle()
                A(st[:, 3 + t:4 + t], st[:, t:t + 1], ACT.Sqrt, bias=epsc[:, 0:1],
                  scale=1.0 / D).then_inc(S("root2_done"), 1)
            for n in range(6):
                act.wait_ge(S("h2t_ready"), n + 1)
                t, h = divmod(n, 2)
                A(h2T[:, 4 * h:4 * h + 4, t * P:(t + 1) * P], bank[n % 4][:, :].rearrange("p (a b) -> p a b", a=4),
                  ACT.Copy).then_inc(S("h2t_copied"), 1)
            act.wait_ge(S("logits_ready"), 1)
            A(r1.rearrange("p a b -> p (a b)"), bank[4][:, 0:NT * NE], ACT.Exp, scale=-1.0).then_inc(S("exp_done"), 1)
            def split_hi(name, e, halves=(0, 1)):
                c = raw[name].shape[1] // 2
                for half in halves:
                    act.wait_ge(S(f"{name}_in{half}"), (e + 1) * 16)
                    A(wsplit[name][0][:, half * c:(half + 1) * c, :], raw[name][:, half * c:(half + 1) * c, :],
                      ACT.Copy).then_inc(S(f"{name}_hi"), 1)

            row_half(6)
            row_half(7)
            act.wait_ge(S("y_ready"), 4)
            split_hi("gate", 0)
            split_hi("up", 0)
            for n in range(0, 12, 2):
                act.wait_ge(S("hs_ready"), n + 1)
                t, h = divmod(n, 2)
                A(hTs[:, 4 * h:4 * h + 4, t * P:(t + 1) * P], bank[n % 4][:, :].rearrange("p (a b) -> p a b", a=4),
                  ACT.Copy).then_inc(S("hs_copied_a"), 1)

            act.wait_ge(S("int_done"), 1)
            for f in ("first", "more"):
                act.sem_inc(S(f"evac_{f}"), 1)
                act.sem_inc(S(f"written_{f}"), 16)
            act.wait_ge(S("pad_done"), 1)
            act.wait_ge(S("pad_sent"), 16)
            act.wait_ge(S("hs_copied_v"), 6)

            def stage_x(p, e, start):
                A(xs[0][:, :, :], hTs[:, :, bass.ds(start + P * p, P)], ACT.Copy).then_inc(S(f"x_hi_{fam(p)}"), 1)

            def silu(p, e):
                f = fam(p)
                act.wait_ge(S(f"gate_done_{f}"), nth(p, e) + 1)
                A(sg[:, :], bank[0][:, :], ACT.Silu).then_inc(S(f"silu_done_{f}"), 1)

            def hidden_hi(p, e):
                f, i = fam(p), nth(p, e)
                for half in range(2):
                    act.wait_ge(S(f"tr_done_{f}"), i * 2 + half + 1)
                    A(hs[0][:, 2 * half:2 * half + 2, :],
                      bank[2 + half][:, 0:2 * P].rearrange("p (a b) -> p a b", a=2),
                      ACT.Copy).then_inc(S(f"h_hi_{f}"), 1)

            def evacuate(p, e, start, n):
                f, i = fam(p), nth(p, e)
                act.wait_ge(S(f"down_done_{f}"), i + 2)
                A(ystage[:, :], psum[:, 4:6, :].rearrange("p a b -> p (a b)"), ACT.Copy).then_inc(S(f"evac_{f}"), 1)
                act.wait_ge(S(f"evac_{f}"), i + 2)
                if p > 0:
                    act.dma_start(ysd[bass.ds(start + P * p, P), :], ystage[:, :]).then_inc(S(f"written_{f}"), 16)
                    return
                A(warm[:, 1:2], epsc[:, :], ACT.Copy)
                with act.If(n > 64):
                    act.dma_start(ysd[bass.ds(start, P), :], ystage[:, :]).then_inc(S("written_first"), 16)
                with act.Else():
                    act.dma_start(ysd[bass.ds(start, 64), :], ystage[0:64, :]).then_inc(S("written_first"), 16)

            def skipped(f):
                act.sem_inc(S(f"evac_{f}"), 1)
                act.sem_inc(S(f"written_{f}"), 16)
                act.sem_inc(S(f"x_hi_{f}"), 1)
                act.sem_inc(S(f"silu_done_{f}"), 1)
                act.sem_inc(S(f"h_hi_{f}"), 2)

            def expert(e, more):
                n = act.value_load(n_i[0:1, bass.ds(e, 1)], min_val=0, max_val=NT * P)
                start = act.value_load(off_i[0:1, bass.ds(e, 1)], min_val=0, max_val=PAIRS)
                A(warm[:, 0:1], epsc[:, :], ACT.Silu)
                silu(0, e)

                def next_x(p):
                    act.wait_ge(S(f"up_done_{fam(p)}"), nth(p, e) + 1)
                    nxt = act.value_load(off_i[0:1, bass.ds(e + 1, 1)], min_val=0, max_val=PAIRS)
                    stage_x(0, e + 1, nxt)

                def last_pass(p, start):
                    if more:
                        split_hi("gate", e + 1, (0,))
                    hidden_hi(p, e)
                    if more:
                        split_hi("gate", e + 1, (1,))
                        next_x(p)
                        split_hi("up", e + 1)
                    evacuate(p, e, start, n)

                with act.If(n > P):
                    hidden_hi(0, e)
                    s1 = act.value_load(off_i[0:1, bass.ds(e, 1)], min_val=0, max_val=PAIRS - P)
                    stage_x(1, e, s1)
                    evacuate(0, e, start, n)
                    silu(1, e)
                    with act.If(n > 2 * P):
                        hidden_hi(1, e)
                        s2 = act.value_load(off_i[0:1, bass.ds(e, 1)], min_val=0, max_val=PAIRS - 2 * P)
                        stage_x(2, e, s2)
                        evacuate(1, e, s1, n)
                        silu(2, e)
                        last_pass(2, s2)
                    with act.Else():
                        last_pass(1, s1)
                        act.wait_ge(S("written_more"), (e * 2 + 2) * 16)
                        skipped("more")
                with act.Else():
                    last_pass(0, start)
                    skipped("more")
                    skipped("more")

                if more:
                    split_hi("down", e + 1)

            first = act.value_load(off_i[0:1, 0:1], min_val=0, max_val=PAIRS)
            stage_x(0, 0, first)
            split_hi("down", 0)
            with act.Fori(0, NE - 1) as e:
                expert(e, True)
            expert(NE - 1, False)
            A(warm[:, 2:3], epsc[:, :], ACT.Sqrt)

            def first_choice(t):
                act.wait_ge(S(f"picked_in{t}"), 32)
                A(picked[:, t, 0, :], picked[:, t, 0, :], ACT.Copy, scale=wts[:, t:t + 1]).then_inc(S("y0_done"), 1)

            first_choice(0)
            for t in range(NT):
                if t + 1 < NT:
                    first_choice(t + 1)
                act.wait_ge(S("x2_done"), t + 1)
                a(A(picked[:, t, 0, :], X[:, t, :], ACT.Square, accum_out=st[:, t:t + 1]))
                a.settle()
                A(st[:, 3 + t:4 + t], st[:, t:t + 1], ACT.Sqrt, bias=epsc[:, 0:1],
                  scale=1.0 / D).then_inc(S("root3_done"), 1)

        @block.vector
        def _(dve):
            V_ = nc.vector
            d = Steps(dve, S("dve_own"))

            def v(ins):
                d(ins)
                d.settle()

            tt, ts, stt, cp = V_.tensor_tensor, V_.tensor_scalar, V_.scalar_tensor_tensor, V_.tensor_copy
            v(V_.memset(epsc[:, :], EPS))
            dve.wait_ge(S("dt_ready"), 1)
            dve.wait_ge(S("a_in"), 64)
            tt(adrow[0:64, :].rearrange("q (t n) -> q t n", t=2), arow[0:64, :].rearrange("q (t n) -> q t n", t=2),
               dtr[0:64, 0:2].unsqueeze(2).broadcast_to([64, 2, 64]), ALU.mult).then_inc(S("adt_done"), 1)
            dve.wait_ge(S("vec_ready"), 1)
            cp(vecT[:, 0:96], bank[7][:, 0:96]).then_inc(S("small_copied"), 1)
            dve.wait_ge(S("acol_ready"), 1)
            d(cp(acol.rearrange("p a b -> p (a b)"), bank[6][:, 0:P]))
            d(cp(s0c.rearrange("p a b -> p (a b)"), bank[6][:, 64:P]))
            v(cp(adcol.rearrange("p a b -> p (a b)"), bank[6][:, P:P + 64]))
            dve.sem_inc(S("small_copied"), 1)
            ar, ai, adi = acol[:, 0, :], acol[:, 1, :], adcol[:, 1, :]
            k, r, rq = tp[0][:, :], tp[1][:, :], tp[2][:, :]
            lim = 3.1415925
            v(ts(k, adi, 1.0 / (2 * PI), 12582912.0, ALU.mult, ALU.add))
            v(ts(k, k, -12582912.0, None, ALU.add))
            v(stt(r, k, -6.28125, adi, ALU.mult, ALU.add))
            v(stt(r, k, -(2 * PI - 6.28125), r, ALU.mult, ALU.add))
            v(ts(rq, r, PI / 2, None, ALU.add))
            v(ts(k, rq, PI, -2 * PI, ALU.is_gt, ALU.mult))
            v(tt(rq, rq, k, ALU.add))
            ts(sincos_in, sincos_in, lim, -lim, ALU.min, ALU.max).then_inc(S("phase_done"), 1)

            dve.wait_ge(S("root_done"), 1)
            V_.reciprocal(st[:, 6:9], st[:, 3:6]).then_inc(S("rstd_done"), 1)
            dve.wait_ge(S("trig_done"), 2)
            d(V_.memset(pw[:, 0, 0, :], 1.0))
            d(V_.memset(pw[:, 0, 1, :], 0.0))
            d(tt(pw[:, 1, 0, :], tp[5][:, :], tp[4][:, :], ALU.mult))
            v(tt(pw[:, 1, 1, :], tp[5][:, :], tp[3][:, :], ALU.mult))

            def cmul(o, x, y):
                d(tt(tp[0][:, :], x[:, 0, :], y[:, 0, :], ALU.mult))
                d(tt(tp[1][:, :], x[:, 1, :], y[:, 1, :], ALU.mult))
                d(tt(tp[2][:, :], x[:, 0, :], y[:, 1, :], ALU.mult))
                v(tt(tp[3][:, :], x[:, 1, :], y[:, 0, :], ALU.mult))
                d(tt(o[:, 0, :], tp[0][:, :], tp[1][:, :], ALU.subtract))
                v(tt(o[:, 1, :], tp[2][:, :], tp[3][:, :], ALU.add))

            cmul(pw[:, 2], pw[:, 1], pw[:, 1])
            cmul(pw[:, 3], pw[:, 2], pw[:, 1])
            cmul(pw[:, 4], pw[:, 2], pw[:, 2])
            er1, den, fr, fi, m0, m1 = (x[:, :] for x in tp[:6])
            ei = pw[:, 1, 1, :]
            d(ts(er1, pw[:, 1, 0, :], -1.0, None, ALU.add))
            d(tt(m0, ar, ar, ALU.mult))
            v(tt(m1, ai, ai, ALU.mult))
            v(tt(m0, m0, m1, ALU.add))
            v(V_.reciprocal(den, m0))
            d(tt(m0, er1, ar, ALU.mult))
            v(tt(m1, ei, ai, ALU.mult))
            v(tt(m0, m0, m1, ALU.add))
            v(tt(fr, m0, den, ALU.mult))
            d(tt(m0, ei, ar, ALU.mult))
            v(tt(m1, er1, ai, ALU.mult))
            v(tt(m0, m0, m1, ALU.subtract))
            v(tt(fi, m0, den, ALU.mult))
            for t in range(CH):
                for x, kf, kb in ((pwB, 3 - t, t), (pwC, t + 1, 4 - t)):
                    d(cp(x[:, :, t, 0:GP], pw[:, kf, :, 0:GP]))
                    d(cp(x[:, :, t, GP:Q], pw[:, kb, :, GP:Q]))
            for ri in range(2):
                d(cp(Tre[:, :, ri, :], pw[:, 4, 0, :].rearrange("p (d g) -> p d g", d=2)))
            d(cp(Tim[:, :, 0, :], pw[:, 4, 1, :].rearrange("p (d g) -> p d g", d=2)))
            v(ts(Tim[:, :, 1, :], pw[:, 4, 1, :].rearrange("p (d g) -> p d g", d=2), -1.0, None, ALU.mult))

            def over_h(x, n=16):
                return x.unsqueeze(2).broadcast_to([P, Q, n])

            def halves(o, in0, in1, op):
                for g in range(2):
                    part = slice(64 * g, 64 * g + 64)
                    d(tt(o[part, :, 16 * g:16 * g + 16], in0[part], in1[part], op))

            dve.wait_ge(S("bt_raw_ready"), 1)
            for i in range(2):
                d(cp(BT.rearrange("p r q h -> p h (r q)")[:, 8 * i:8 * i + 8, :],
                     bank[i][:, :].rearrange("p (h q) -> p h q", h=8)))
            d.settle()
            for o, x, y, op in ((0, 0, 1, ALU.subtract), (1, 1, 0, ALU.add)):
                d(tt(prod1, BT[:, x], over_h(fr), ALU.mult))
                v(tt(prod2, BT[:, y], over_h(fi), ALU.mult))
                v(tt(Bb[:, o], prod1, prod2, op))
            dve.wait_ge(S("zeros_done"), 1)
            for t in range(CH):
                if t == 1:
                    dve.wait_ge(S("ct_raw_ready"), 1)
                    for i in range(2):
                        cp(CT.rearrange("p r q h -> p h (r q)")[:, 8 * i:8 * i + 8, :],
                             bank[2 + i][:, :].rearrange("p (h q) -> p h q", h=8)).then_inc(S("raw_copied"), 1)
                    dve.wait_ge(S("raw_copied"), 2)
                if t == 2:
                    dve.wait_ge(S("mod_a_ready"), 1)
                    v(tt(modT, bank[5][:, 0:32].rearrange("p (m k s) -> p m s k", m=2, s=2),
                         vecT[:, 32:48].rearrange("p (m k) -> p m k", m=2).unsqueeze(2).broadcast_to([P, 2, 2, KD]),
                         ALU.add))
                    dve.sem_inc(S("mod_a_copied"), 1)
                    stt(aff1, modT[:, 1], 1.0, vecT[:, 16:24].unsqueeze(1).broadcast_to([P, 2, KD]),
                        ALU.add, ALU.mult).then_inc(S("aff1_done"), 1)
                for o, x, y, op in ((0, 0, 1, ALU.subtract), (1, 1, 0, ALU.add)):
                    d(tt(prod1, Bb[:, x], over_h(pwB[:, 0, t, :]), ALU.mult))
                    v(tt(prod2, Bb[:, y], over_h(pwB[:, 1, t, :]), ALU.mult))
                    halves(BB[o][:, :, 32 * t:32 * t + 32], prod1, prod2, op)
                    d.settle()
            for g in range(2):
                part = slice(64 * g, 64 * g + 64)
                d(cp(Cbd[part, 0, :, 16 * g:16 * g + 16], CT[part, 0]))
                v(ts(Cbd[part, 1, :, 16 * g:16 * g + 16], CT[part, 1], -1.0, None, ALU.mult))
            dve.sem_inc(S("bb_done"), 1)

            for t in range(CH):
                d(tt(prod1, CT[:, 0], over_h(pwC[:, 0, t, :]), ALU.mult))
                v(tt(prod2, CT[:, 1], over_h(pwC[:, 1, t, :]), ALU.mult))
                halves(CA[:, 0, :, 32 * t:32 * t + 32], prod1, prod2, ALU.subtract)
                d.settle()
                d(tt(prod1, CT[:, 0], over_h(pwC[:, 1, t, :]), ALU.mult))
                v(tt(prod2, CT[:, 1], over_h(pwC[:, 0, t, :]), ALU.mult))
                for g in range(2):
                    part = slice(64 * g, 64 * g + 64)
                    d(stt(CA[part, 1, :, 32 * t + 16 * g:32 * t + 16 * g + 16], prod1[part], -1.0, prod2[part],
                          ALU.mult, ALU.subtract))
                d.settle()
            dve.sem_inc(S("params_done"), 1)

            dve.wait_ge(S("unit_used"), 5)
            for b in range(2, 4):
                for t in range(CH):
                    last = cp(chunk_dst(t, b), chunk_src(t, b))
            last.then_inc(S("u_done_v"), 1)
            for n in range(16):
                dve.wait_ge(S("bt_ready"), n + 1)
                ri, q = divmod(4 * n, Q)
                cp(Bt[:, ri, q:q + 4, :], bank[n % 4][:, :].rearrange("p (a b) -> p a b", a=4)
                   ).then_inc(S("bt_copied"), 1)
            dve.wait_ge(S("l_gathered"), 1)
            for t in range(CH):
                o = L[32 * t:32 * t + 32, :, 32 * t:32 * t + 32]
                d(tt(o, o, bank[7][0:32, :].rearrange("p (a b) -> p a b", a=GP), ALU.add))
            d.settle()
            dve.sem_inc(S("lk_copied"), 1)
            for gp in range(GP):
                d(stt(L[:, gp, :], ident[:, :], vecT[:, 80 + gp:81 + gp], L[:, gp, :], ALU.mult, ALU.add))
            dve.wait_ge(S("v_copied"), 16)
            d.settle()
            d(V_.memset(V[:, 0, :], 0.0))
            d(cp(V[:, LAT, :].rearrange("p (i g) -> p i g", i=2), s0c[:, :, 0:GP]))
            v(cp(V[:, 2 * ROWS - 1, :].rearrange("p (i g) -> p i g", i=2), s0c[:, :, GP:Q]))
            dve.sem_inc(S("v_init"), 1)

            def row_pair(f, b):
                return V[:, f:b + 1:b - f, :].rearrange("p d (i g) -> p d i g", i=2)

            for s in range(64):
                prev = row_pair(LAT + s, 2 * ROWS - 1 - s)
                nxt = row_pair(LAT + 1 + s, 2 * ROWS - 2 - s)
                d(tt(dt1, prev, Tre, ALU.mult))
                d(tt(dt2[:, :, ::-1, :], prev, Tim, ALU.mult))
                d.settle(d.n - 1)
                d(tt(nxt, nxt, dt1, ALU.add))
                d.settle()
                last = tt(nxt, nxt, dt2, ALU.add)
                if s < 63:
                    v(last)
            last.then_inc(S("lat_states"), 1)

            dve.wait_ge(S("ln_in"), 48)
            for t in range(NT):
                dve.wait_ge(S("vg_done"), t + 1)
                v(V_.bn_stats(bnst[:, :], vn[:, t, :]))
                v(V_.bn_aggr(bnag[:, 2 * t:2 * t + 2], bnst[:, :]))
            bv = bnag[:, 0:6].rearrange("p (t m) -> p m t", m=2)
            cp(st[:, 12:15], bv[:, 1, :]).then_inc(S("ln_var"), 1)
            dve.wait_ge(S("ln_root"), 1)
            v(V_.reciprocal(st[:, 20:23], st[:, 16:19]))
            for t in range(NT):
                v(ts(vn[:, t, :], vn[:, t, :], bnag[:, 2 * t:2 * t + 1], st[:, 20 + t:21 + t],
                     ALU.subtract, ALU.mult))
                v(tt(vn[:, t, :], vn[:, t, :], lnw[:, :], ALU.mult))
                tt(vn[:, t, :], vn[:, t, :], lnb[:, :], ALU.add).then_inc(S("vn_done"), 1)
            dve.wait_ge(S("ws_ready"), 1)
            cp(wsT.rearrange("p a b -> p (a b)"), bank[4][:, :]).then_inc(S("ws_copied"), 1)
            for t in range(NT):
                dve.wait_ge(S("spatial_ready"), t + 1)
                o = yT[:, 4:8, T0[t]:T0[t] + P]
                v(tt(o, bank[(7, 5, 6)[t]][:, :].rearrange("p (a b) -> p a b", a=4), bsr, ALU.add))
                tt(o, o, ugT[:, :, T0[t]:T0[t] + P], ALU.mult).then_inc(S("yg_done"), 1)
            dve.wait_ge(S("ctx_states"), 1)
            d(cp(fin[:, :, 0:GP], V[:, LAT - 1, :].rearrange("p (i g) -> p i g", i=2)))
            cp(fin[:, :, GP:Q], V[:, ROWS, :].rearrange("p (i g) -> p i g", i=2)).then_inc(S("fin_done"), 1)
            dve.wait_ge(S("states_ready"), 1)
            cp(statesT[0:64, :], bank[4][0:64, 0:P]).then_inc(S("states_copied"), 1)
            for c in range(4):
                dve.wait_ge(S("sgm_done"), c + 1)
                tt(yT[:, c, :], gT[:, c, :], sgm[:, c, :], ALU.mult).then_inc(S("yt_done"), 1)
            dve.wait_ge(S("g1_in"), 16)
            for n in range(6):
                t, h = divmod(n, 2)
                c = slice(h * 512, h * 512 + 512)
                dve.wait_ge(S("wo_ready"), n + 1)
                v(tt(xtmp[:, :], bank[4 + n % 4][:, :], g1rows[:, min(t, 1), c], ALU.mult))
                tt(X[:, t, c], X[:, t, c], xtmp[:, :], ALU.add).then_inc(S("x1_done"), 1)
                if n < 5:
                    dve.wait_ge(S("x1_done"), n + 1)
            dve.wait_ge(S("ab_in"), 32)
            dve.wait_ge(S("a2_done"), 1)
            for t in range(NT):
                dve.wait_ge(S("root2_done"), t + 1)
                v(V_.reciprocal(st[:, 6 + t:7 + t], st[:, 3 + t:4 + t]))
                v(stt(h2[:, t, :], X[:, t, :], st[:, 6 + t:7 + t], abrows[:, 0, min(t, 1), :], ALU.mult, ALU.mult))
                tt(h2[:, t, :], h2[:, t, :], abrows[:, 1, min(t, 1), :], ALU.add).then_inc(S("h2_done"), 1)

            flat = "p a b -> p (a b)"
            row16 = desc[:, :].unsqueeze(1).broadcast_to([P, NT, NE])
            row4 = desc[:, 12:16].unsqueeze(1).broadcast_to([P, NT, 4])
            dve.wait_ge(S("exp_done"), 1)
            dve.wait_ge(S("tri_done"), 1)
            v(ts(r1.rearrange(flat), r1.rearrange(flat), 1.0, None, ALU.add))
            v(V_.reciprocal(sig.rearrange(flat), r1.rearrange(flat)))
            v(tt(sel, sig, rbrow[:, :].unsqueeze(1).broadcast_to([P, NT, NE]), ALU.add))
            quad = sel.rearrange("p t (g e) -> p e t g", e=4)
            d(tt(g1, quad[:, 0], quad[:, 1], ALU.max))
            d(tt(g2, quad[:, 0], quad[:, 1], ALU.min))
            d(tt(g3, quad[:, 2], quad[:, 3], ALU.max))
            v(tt(g4, quad[:, 2], quad[:, 3], ALU.min))
            v(tt(g4, g2, g4, ALU.max))
            d(tt(g2, g1, g3, ALU.min))
            v(tt(g1, g1, g3, ALU.max))
            v(tt(g2, g2, g4, ALU.max))
            v(tt(g1, g1, g2, ALU.add))

            def first_max(o, x, n, prio, scratch):
                v(V_.tensor_reduce(q1[:, 0:NT], x, AX.X, ALU.max))
                v(tt(scratch, x, q1[:, 0:NT].unsqueeze(2).broadcast_to([P, NT, n]), ALU.is_equal))
                v(tt(scratch, scratch, prio, ALU.mult))
                v(V_.tensor_reduce(q1[:, 0:NT], scratch, AX.X, ALU.max))
                v(tt(o, scratch, q1[:, 0:NT].unsqueeze(2).broadcast_to([P, NT, n]), ALU.is_equal))

            first_max(g3, g1, 4, row4, g2)
            v(ts(g3, g3, BIG, -BIG, ALU.mult, ALU.add))
            v(tt(r1.rearrange("p t (g e) -> p (t g) e", e=4), sel.rearrange("p t (g e) -> p (t g) e", e=4),
                 g3.rearrange(flat).unsqueeze(2).broadcast_to([P, 12, 4]), ALU.add))
            first_max(oh1, r1, NE, row16, r2)
            v(stt(r1, oh1, -BIG, r1, ALU.mult, ALU.add))
            first_max(oh2, r1, NE, row16, r2)
            tt(mk, oh1, oh2, ALU.add).then_inc(S("mk_done"), 1)
            v(tt(r1, sig, oh1, ALU.mult))
            v(V_.tensor_reduce(q1[:, 0:NT], r1, AX.X, ALU.add))
            v(tt(r1, sig, oh2, ALU.mult))
            v(V_.tensor_reduce(q2[:, 0:NT], r1, AX.X, ALU.add))
            v(tt(q3[:, 0:NT], q1[:, 0:NT], q2[:, 0:NT], ALU.add))
            v(V_.reciprocal(st[:, 24:27], q3[:, 0:NT]))
            d(tt(wts[:, 0:3], q1[:, 0:NT], st[:, 24:27], ALU.mult))
            d(tt(wts[:, 3:6], q2[:, 0:NT], st[:, 24:27], ALU.mult))
            dve.wait_ge(S("ranks_ready"), 1)
            cnt, inc = r2[:, 0, :], r2[:, 1, :]
            v(cp(cnt, bank[5][:, 48:64]))
            v(V_.tensor_tensor_scan(inc, ones[:, 0:NE], cnt, 0.0, ALU.mult, ALU.add))
            v(tt(inc, inc, cnt, ALU.subtract))
            d(cp(n_i[:, :], cnt))
            v(cp(off_i[:, :], inc))
            dve.sem_inc(S("int_done"), 1)
            v(tt(r1, bank[5][:, 0:NT * NE].rearrange("p (t e) -> p t e", t=NT),
                 inc.unsqueeze(1).broadcast_to([P, NT, NE]), ALU.add))
            for o, c in ((oh1, 0), (oh2, 3)):
                v(tt(o, o, r1, ALU.mult))
                v(V_.tensor_reduce(q1[:, 0:NT], o, AX.X, ALU.add))
                v(cp(pos_u[:, c:c + 3], q1[:, 0:NT]))
            dve.sem_inc(S("routed"), 1)
            def split_lo(name, e, halves=(0, 1)):
                c = raw[name].shape[1] // 2
                for half in halves:
                    dve.wait_ge(S(f"{name}_hi"), e * 2 + half + 1)
                    k = slice(half * c, (half + 1) * c)
                    tt(wsplit[name][1][:, k, :], raw[name][:, k, :], wsplit[name][0][:, k, :].bitcast(F32),
                       ALU.subtract).then_inc(S(f"{name}_lo"), 1)

            split_lo("gate", 0)
            for n in range(1, 12, 2):
                dve.wait_ge(S("hs_ready"), n + 1)
                t, h = divmod(n, 2)
                cp(hTs[:, 4 * h:4 * h + 4, t * P:(t + 1) * P],
                   bank[n % 4][:, :].rearrange("p (a b) -> p a b", a=4)).then_inc(S("hs_copied_v"), 1)

            def stage_x(p, e, start):
                dve.wait_ge(S(f"x_hi_{fam(p)}"), nth(p, e) + 1)
                tt(xs[1][:, :, :], hTs[:, :, bass.ds(start + P * p, P)], xs[0][:, :, :].bitcast(F32),
                   ALU.subtract).then_inc(S(f"x_lo_{fam(p)}"), 1)

            def hidden_values(p, e):
                f, i = fam(p), nth(p, e)
                dve.wait_ge(S(f"silu_done_{f}"), i + 1)
                for x, count in before(p, e):
                    dve.wait_ge(S(f"written_{x}"), count * 16)
                dve.wait_ge(S(f"up_done_{f}"), i + 1)
                for half in range(2):
                    c = slice(half * DE // 2, half * DE // 2 + DE // 2)
                    tt(hidden[:, c], sg[:, c], bank[1][:, c], ALU.mult).then_inc(S(f"mul_done_{f}"), 1)
                for half in range(2):
                    dve.wait_ge(S(f"h_hi_{f}"), i * 2 + half + 1)
                    tt(hs[1][:, 2 * half:2 * half + 2, :],
                       bank[2 + half][:, 0:2 * P].rearrange("p (a b) -> p a b", a=2),
                       hs[0][:, 2 * half:2 * half + 2, :].bitcast(F32), ALU.subtract).then_inc(S(f"h_lo_{f}"), 1)

            def skipped(f):
                dve.sem_inc(S(f"x_lo_{f}"), 1)
                dve.sem_inc(S(f"mul_done_{f}"), 2)
                dve.sem_inc(S(f"h_lo_{f}"), 2)

            def expert(e, more):
                n = dve.value_load(n_i[0:1, bass.ds(e, 1)], min_val=0, max_val=NT * P)

                def next_x():
                    nxt = dve.value_load(off_i[0:1, bass.ds(e + 1, 1)], min_val=0, max_val=PAIRS)
                    stage_x(0, e + 1, nxt)

                def last_pass(p):
                    hidden_values(p, e)
                    if more:
                        split_lo("gate", e + 1, (0,))
                        next_x()
                        split_lo("gate", e + 1, (1,))
                        split_lo("up", e + 1)

                with dve.If(n > P):
                    hidden_values(0, e)
                    s1 = dve.value_load(off_i[0:1, bass.ds(e, 1)], min_val=0, max_val=PAIRS - P)
                    stage_x(1, e, s1)
                    with dve.If(n > 2 * P):
                        hidden_values(1, e)
                        s2 = dve.value_load(off_i[0:1, bass.ds(e, 1)], min_val=0, max_val=PAIRS - 2 * P)
                        stage_x(2, e, s2)
                        last_pass(2)
                    with dve.Else():
                        last_pass(1)
                        dve.wait_ge(S("h_lo_more"), (e * 2 + 1) * 2)
                        skipped("more")
                with dve.Else():
                    last_pass(0)
                    skipped("more")
                    skipped("more")
                if more:
                    split_lo("down", e + 1)

            first = dve.value_load(off_i[0:1, 0:1], min_val=0, max_val=PAIRS)
            stage_x(0, 0, first)
            dve.wait_ge(S("tok_sent"), 16 * 6)
            dve.wait_ge(S("pad_sent"), 16)
            split_lo("up", 0)
            split_lo("down", 0)
            with dve.Fori(0, NE - 1) as e:
                expert(e, True)
            expert(NE - 1, False)

            dve.wait_ge(S("g2_in"), 16)
            def final_norm(t):
                dve.wait_ge(S("root3_done"), t + 1)
                v(V_.reciprocal(st[:, 6 + t:7 + t], st[:, 3 + t:4 + t]))
                stt(X[:, t, :], X[:, t, :], st[:, 6 + t:7 + t], fnw[:, :], ALU.mult,
                    ALU.mult).then_inc(S("final_done"), 1)

            dve.wait_ge(S("fnw_in"), 16)
            for t in range(NT):
                dve.wait_ge(S("y0_done"), t + 1)
                y0, y1 = picked[:, t, 0, :], picked[:, t, 1, :]
                v(stt(y0, y1, wts[:, 3 + t:4 + t], y0, ALU.mult, ALU.add))
                v(tt(y0, y0, g2rows[:, min(t, 1), :], ALU.mult))
                tt(X[:, t, :], X[:, t, :], y0, ALU.add).then_inc(S("x2_done"), 1)
                if t > 0:
                    final_norm(t - 1)
            final_norm(NT - 1)

        @block.gpsimd
        def _(pool):
            G = nc.gpsimd
            p = Steps(pool, S("pool_own"))

            def w(ins):
                p(ins)
                p.settle()

            for i in range(2):
                pool.dma_start(dtr[32 * i:32 * i + 32, 0:2],
                               io["ssm_log_dt"][0].rearrange("d (g t) -> (d g) t", t=2)).then_inc(S("dt_in"), 16)
            for i, name in enumerate(("ssm_a_re", "ssm_a_im", "state_ssm_re", "state_ssm_im")):
                src = io[name][0] if i < 2 else io[name][0, 0]
                pool.dma_start(arow[32 * i:32 * i + 32, :],
                               src.rearrange("d (g t) n -> (d g) (t n)", t=2)).then_inc(S("a_in"), 16)
            w(G.memset(ident[:, :], 0.0))
            G.affine_select(out=ident[:, :], in_=ident[:, :], compare_op=ALU.not_equal, fill=1.0, base=0,
                            pattern=[[-1, P]], channel_multiplier=1).then_inc(S("ident_ready"), 1)
            for t in range(CH):
                pool.dma_start(vrows[80:96, 32 * t:32 * t + 32],
                               io["ssm_d"][0].rearrange("(g h) -> g h", h=32)).then_inc(S("d_in"), 16)
            p(G.memset(BB[0], 0.0))
            p(G.memset(BB[1], 0.0))
            p(G.memset(Cbd, 0.0))
            w(G.memset(CA, 0.0))
            pool.sem_inc(S("zeros_done"), 1)
            G.memset(h1T[:, :, P:T0[1]], 0.0).then_inc(S("gap_done"), 1)
            pool.wait_ge(S("x_in"), 48)
            pool.wait_ge(S("v_init"), 1)
            for s in range(32):
                f, b = s, ROWS + LAT - 1 - s
                prev = V[:, f:b + 1:b - f, :].rearrange("p d (i g) -> p d i g", i=2)
                f, b = s + 1, ROWS + LAT - 2 - s
                nxt = V[:, f:b + 1:b - f, :].rearrange("p d (i g) -> p d i g", i=2)
                p(G.tensor_tensor(pt1, prev, Tre, ALU.mult))
                w(G.tensor_tensor(pt2[:, :, ::-1, :], prev, Tim, ALU.mult))
                w(G.tensor_tensor(nxt, nxt, pt1, ALU.add))
                last = G.tensor_tensor(nxt, nxt, pt2, ALU.add)
                if s < 31:
                    w(last)
            last.then_inc(S("ctx_states"), 1)
            pool.wait_ge(S("yg_done"), 3)
            pool.dma_start(router_w, io["router_w"].rearrange("(k p) n -> p k n", p=P)).then_inc(S("rw_in"), 16)
            pool.dma_start(rbrow, io["router_b"].partition_broadcast(P)).then_inc(S("rw_in"), 16)
            p(G.memset(ones[:, :], 1.0))
            w(G.memset(tri[:, :], 1.0))
            p(G.affine_select(out=tri[:, :], in_=tri[:, :], compare_op=ALU.is_gt, fill=0.0, base=0,
                              pattern=[[1, P]], channel_multiplier=-1))
            w(G.iota(desc_i, [[-1, NE]], base=NE, channel_multiplier=0))
            G.tensor_copy(desc[:, :], desc_i).then_inc(S("tri_done"), 1)
            pool.wait_ge(S("rw_in"), 32)
            pool.wait_ge(S("n2_in"), 16)
            pool.wait_ge(S("ab_in"), 32)
            w(G.tensor_scalar(abrows[:, 0], abrows[:, 0], 1.0, None, ALU.add))
            G.tensor_tensor(abrows[:, 0], abrows[:, 0], n2rows[:, :].unsqueeze(1).broadcast_to([P, 2, D]),
                            ALU.mult).then_inc(S("a2_done"), 1)
            pool.wait_ge(S("h2_done"), 1)
            pool.dma_start(ysd[PAIRS:SORTED, :], h2[:, 0, :]).then_inc(S("pad_sent"), 16)
            pool.wait_ge(S("routed"), 1)
            for k in range(2):
                for t in range(NT):
                    pool.indirect_dma_start(
                        out=hsd, out_offset=bass.IndirectOffsetOnAxis(ap=pos_u[:, 3 * k + t:3 * k + t + 1], axis=0),
                        in_=h2[:, t, :], in_offset=None).then_inc(S("tok_sent"), 16)
            G.memset(hTs[:, :, PAIRS:SORTED], 0.0).then_inc(S("pad_done"), 1)
            for x, count in before(0, NE):
                pool.wait_ge(S(f"written_{x}"), 16 * count)
            for t in range(NT):
                for k in range(2):
                    pool.indirect_dma_start(
                        out=picked[:, t, k, :], out_offset=None, in_=ysd,
                        in_offset=bass.IndirectOffsetOnAxis(ap=pos_u[:, 3 * k + t:3 * k + t + 1], axis=0)
                    ).then_inc(S(f"picked_in{t}"), 16)


IN_NAMES = ["x_prompt", "x_sample", "c", "state_ssm_re", "state_ssm_im", "c_ctx", "norm1_w", "norm2_w", "w_mod",
            "b_mod", "w_in", "ssm_a_re", "ssm_a_im", "ssm_log_dt", "ssm_b_re", "ssm_b_im", "ssm_c_re", "ssm_c_im",
            "ssm_d", "w_glu", "gmlp_ln_w", "gmlp_ln_b", "gmlp_w_s", "gmlp_b_s", "w_out", "router_w", "router_b",
            "w_gate", "w_up", "w_down", "final_norm_w"]
OUTS = [("out_p", (1, 128, 1024)), ("out_s", (1, 256, 1024)), ("out_re", (1, 1, 2, 32, 64)),
        ("out_im", (1, 1, 2, 32, 64))]


def kernel(**inputs):
    import concourse.bacc as bacc
    import numpy as np
    from concourse.bass_utils import run_bass_kernel_spmd

    nc = bacc.Bacc("TRN2", target_bir_lowering=False, num_devices=1)
    arrays, io = {}, {}
    for name in IN_NAMES:
        a = np.ascontiguousarray(inputs[name])
        arrays[f"in_{name}"] = a
        io[name] = nc.dram_tensor(f"in_{name}", a.shape, mybir.dt.from_np(a.dtype), kind="ExternalInput").ap()
    for name, shape in OUTS:
        io[name] = nc.dram_tensor(name, shape, F32, kind="ExternalOutput").ap()
    build(nc, io)
    r = run_bass_kernel_spmd(nc, [arrays], core_ids=[0])
    return tuple(r.results[0][name] for name, _ in OUTS)
```
